# Optimizing a Trainium2 kernel written in Bass

```python
import jax, jax.numpy as jnp
from jax import lax
import numpy as np

D_MODEL = 1024
BATCH = 1
SEQ = 256
DEPTH = 1

CTX_LEN = 256
GRID_W = 64
EPS = 1e-6

ATT_HEADS = 8
ATT_KV_HEADS = 2
ATT_GROUP = ATT_HEADS // ATT_KV_HEADS
ATT_HEAD_DIM = 64
WINDOW = 128
ATT_BLOCK = 128
ROPE_BASE = 10000.0
ROPE_AXIS_DIM = ATT_HEAD_DIM // 2

ML_HEADS = 4
ML_V_DIM = 128
ML_QK_DIM = 64
ML_CHUNK = 64
ML_CONV = 3

ATT_WIDTH = ATT_HEADS * ATT_HEAD_DIM
ATT_KV_WIDTH = ATT_KV_HEADS * ATT_HEAD_DIM
ML_WIDTH = ML_HEADS * ML_V_DIM
ML_QK_WIDTH = ML_HEADS * ML_QK_DIM
ML_GATES = 4 * ML_HEADS
MIX_WIDTH = ATT_WIDTH + ML_WIDTH
FFN_HIDDEN = -(-8 * D_MODEL // (3 * 256)) * 256

COLS = (ATT_WIDTH, ATT_KV_WIDTH, ATT_KV_WIDTH, ML_QK_WIDTH, ML_QK_WIDTH, ML_WIDTH, ML_WIDTH, ML_GATES)
IN_WIDTH = sum(COLS)
SPLIT_AT = tuple(sum(COLS[:i + 1]) for i in range(len(COLS) - 1))


def rms_norm(x, g):
    xf = x.astype(jnp.float32)
    y = xf * lax.rsqrt(jnp.mean(xf * xf, axis=-1, keepdims=True) + EPS)
    return (y * g.astype(jnp.float32)).astype(x.dtype)

def modulate(h, shift, scale):
    return h * (1.0 + scale) + shift

def axial_rope_tables(n_tokens, dtype):
    n_rows = n_tokens // GRID_W
    row = jnp.repeat(jnp.arange(n_rows, dtype=jnp.float32), GRID_W)
    col = jnp.tile(jnp.arange(GRID_W, dtype=jnp.float32), n_rows)
    half = ROPE_AXIS_DIM // 2
    inv_freq = jnp.power(ROPE_BASE, -jnp.arange(half, dtype=jnp.float32) / half)
    ang_r = row[:, None] * inv_freq
    ang_c = col[:, None] * inv_freq
    return tuple(t[:, None, :].astype(dtype) for t in (jnp.cos(ang_r), jnp.sin(ang_r), jnp.cos(ang_c), jnp.sin(ang_c)))

def axial_rope(x, cos_r, sin_r, cos_c, sin_c):
    def rot(u, cos, sin):
        u1, u2 = jnp.split(u, 2, axis=-1)
        return jnp.concatenate([u1 * cos - u2 * sin, u2 * cos + u1 * sin], axis=-1)
    xr, xc = jnp.split(x, 2, axis=-1)
    return jnp.concatenate([rot(xr, cos_r, sin_r), rot(xc, cos_c, sin_c)], axis=-1)

def window_attention(q, k, v, kc, vc, sink):
    B, S = q.shape[:2]
    nb = S // ATT_BLOCK
    scale = ATT_HEAD_DIM ** -0.5
    qb = q.reshape(B, nb, ATT_BLOCK, ATT_KV_HEADS, ATT_GROUP, ATT_HEAD_DIM)
    pad = ((0, 0), (ATT_BLOCK, ATT_BLOCK), (0, 0), (0, 0))

    def band(t):
        tp = jnp.pad(t, pad).reshape(B, nb + 2, ATT_BLOCK, ATT_KV_HEADS, ATT_HEAD_DIM)
        return jnp.concatenate([tp[:, :-2], tp[:, 1:-1], tp[:, 2:]], axis=2)

    kw, vw = band(k), band(v)
    qpos = jnp.arange(S).reshape(nb, ATT_BLOCK)
    kpos = (jnp.arange(nb)[:, None] - 1) * ATT_BLOCK + jnp.arange(3 * ATT_BLOCK)[None, :]
    valid = ((jnp.abs(qpos[:, :, None] - kpos[:, None, :]) <= WINDOW)
             & (kpos[:, None, :] >= 0) & (kpos[:, None, :] < S))
    s_loc = jnp.einsum('bnqhgd,bnkhd->bnhgqk', qb, kw).astype(jnp.float32) * scale
    s_loc = jnp.where(valid[None, :, None, None], s_loc, -jnp.inf)
    s_ctx = jnp.einsum('bnqhgd,bchd->bnhgqc', qb, kc).astype(jnp.float32) * scale
    sk = sink.astype(jnp.float32).reshape(1, 1, ATT_KV_HEADS, ATT_GROUP, 1, 1)
    m = jnp.maximum(jnp.maximum(s_loc.max(-1, keepdims=True), s_ctx.max(-1, keepdims=True)), sk)
    p_loc = jnp.exp(s_loc - m)
    p_ctx = jnp.exp(s_ctx - m)
    inv = 1.0 / (p_loc.sum(-1, keepdims=True) + p_ctx.sum(-1, keepdims=True) + jnp.exp(sk - m))
    o = (jnp.einsum('bnhgqk,bnkhd->bnqhgd', (p_loc * inv).astype(v.dtype), vw)
         + jnp.einsum('bnhgqc,bchd->bnqhgd', (p_ctx * inv).astype(v.dtype), vc))
    return o.reshape(B, S, ATT_WIDTH)

def context_self_attention(qc, kc, vc, sink):
    B, L = qc.shape[:2]
    scale = ATT_HEAD_DIM ** -0.5
    qg = qc.reshape(B, L, ATT_KV_HEADS, ATT_GROUP, ATT_HEAD_DIM)
    s = jnp.einsum('bqhgd,bkhd->bhgqk', qg, kc).astype(jnp.float32) * scale
    sk = sink.astype(jnp.float32).reshape(1, ATT_KV_HEADS, ATT_GROUP, 1, 1)
    m = jnp.maximum(s.max(-1, keepdims=True), sk)
    p = jnp.exp(s - m)
    p = p / (p.sum(-1, keepdims=True) + jnp.exp(sk - m))
    o = jnp.einsum('bhgqk,bkhd->bqhgd', p.astype(vc.dtype), vc)
    return o.reshape(B, L, ATT_WIDTH)

def centred_dwconv(t, w):
    pad = w.shape[0] // 2
    return lax.conv_general_dilated(t, w[:, None, :].astype(t.dtype), window_strides=(1,),
                                    padding=[(pad, pad)], dimension_numbers=('NWC', 'WIO', 'NWC'),
                                    feature_group_count=t.shape[-1])

def mlstm_heads(t, d):
    B, T = t.shape[:2]
    return t.reshape(B, T, ML_HEADS, d).transpose(0, 2, 1, 3).astype(jnp.float32)

def mlstm_prepare(mq, mk, mv, mg, w_conv, gate_bias):
    qk = jax.nn.silu(centred_dwconv(jnp.concatenate([mq, mk], axis=-1), w_conv))
    mq, mk = jnp.split(qk, 2, axis=-1)
    B, T = mq.shape[:2]
    g = (mg.astype(jnp.float32) + gate_bias.astype(jnp.float32)).reshape(B, T, 4, ML_HEADS).transpose(0, 3, 1, 2)
    return mlstm_heads(mq, ML_QK_DIM), mlstm_heads(mk, ML_QK_DIM), mlstm_heads(mv, ML_V_DIM), g

def mlstm_zero_state(B):
    return (jnp.zeros((B, ML_HEADS, ML_V_DIM, ML_QK_DIM), jnp.float32),
            jnp.zeros((B, ML_HEADS, ML_QK_DIM), jnp.float32),
            jnp.zeros((B, ML_HEADS), jnp.float32))

def mlstm_chunkwise(q, k, v, ig, lf, state):
    B, H, T, _ = q.shape
    nc = T // ML_CHUNK
    q = q * (ML_QK_DIM ** -0.5)

    def to_chunks(a):
        return jnp.moveaxis(a.reshape(B, H, nc, ML_CHUNK, *a.shape[3:]), 2, 0)

    xs = tuple(to_chunks(a) for a in (q, k, v, ig, lf))
    lower = jnp.tril(jnp.ones((ML_CHUNK, ML_CHUNK), dtype=bool))

    def step(carry, inp):
        C, n, m = carry
        qc, kc, vc, ic, fc = inp
        b = jnp.cumsum(fc, axis=-1)
        a_inter = b + m[..., None]
        d = jnp.where(lower, b[..., :, None] - b[..., None, :] + ic[..., None, :], -jnp.inf)
        m_t = jnp.maximum(a_inter, d.max(-1))
        w_intra = jnp.exp(d - m_t[..., None])
        w_inter = jnp.exp(a_inter - m_t)
        s = jnp.einsum('bhtd,bhsd->bhts', qc, kc) * w_intra
        num = jnp.einsum('bhts,bhsv->bhtv', s, vc) + w_inter[..., None] * jnp.einsum('bhvd,bhtd->bhtv', C, qc)
        den = s.sum(-1) + w_inter * jnp.einsum('bhd,bhtd->bht', n, qc)
        h = num / jnp.maximum(jnp.abs(den), jnp.exp(-m_t))[..., None]
        b_last = b[..., -1]
        g = b_last[..., None] - b + ic
        m_new = jnp.maximum(b_last + m, g.max(-1))
        decay = jnp.exp(b_last + m - m_new)
        wk = jnp.exp(g - m_new[..., None])
        C = decay[..., None, None] * C + jnp.einsum('bhs,bhsv,bhsd->bhvd', wk, vc, kc)
        n = decay[..., None] * n + jnp.einsum('bhs,bhsd->bhd', wk, kc)
        return (C, n, m_new), h

    state, hs = lax.scan(step, state, xs)
    return jnp.moveaxis(hs, 0, 2).reshape(B, H, T, ML_V_DIM), state

def mlstm_bidir(q, k, v, g, state_f, state_b):
    h_f, st_f = mlstm_chunkwise(q, k, v, g[..., 0], jax.nn.log_sigmoid(g[..., 1]), state_f)
    flip = lambda t: jnp.flip(t, axis=2)
    h_b, st_b = mlstm_chunkwise(flip(q), flip(k), flip(v), flip(g[..., 2]),
                                flip(jax.nn.log_sigmoid(g[..., 3])), state_b)
    return h_f + flip(h_b), st_f, st_b

def mlstm_output(h, o_pre, gain):
    B, H, T, DV = h.shape
    hf = h.transpose(0, 2, 1, 3)
    hf = hf * lax.rsqrt(jnp.mean(hf * hf, axis=-1, keepdims=True) + EPS) * gain.astype(jnp.float32).reshape(ML_HEADS, ML_V_DIM)
    return hf.reshape(B, T, ML_WIDTH).astype(o_pre.dtype) * jax.nn.sigmoid(o_pre)

def swiglu(h, w_in, w_out):
    gate, up = jnp.split(h @ w_in, 2, axis=-1)
    return (jax.nn.silu(gate) * up) @ w_out

def first_inputs(seed: int = 0) -> dict:
    key = jax.random.key(seed)
    ks = jax.random.split(key, 20)
    nrm = lambda k, shape, s: jax.random.normal(k, shape, jnp.float32) * s
    fgt = jnp.linspace(3.0, 6.0, ML_HEADS, dtype=jnp.float32)
    zh = jnp.zeros((ML_HEADS,), jnp.float32)
    gate_base = jnp.concatenate([zh, fgt, zh, fgt])
    return {
        'x': nrm(ks[0], (BATCH, SEQ, D_MODEL), 1.0),
        'c': nrm(ks[1], (BATCH, D_MODEL), 1.0),
        'ctx': nrm(ks[2], (BATCH, CTX_LEN, D_MODEL), 1.0),
        'c_ctx': nrm(ks[3], (D_MODEL,), 1.0),
        'w_ada': nrm(ks[4], (DEPTH, D_MODEL, 6 * D_MODEL), 0.5 * D_MODEL ** -0.5),
        'b_ada': nrm(ks[5], (DEPTH, 6 * D_MODEL), 0.02),
        'g_pre_mix': 1.0 + nrm(ks[6], (DEPTH, D_MODEL), 0.05),
        'w_in': nrm(ks[7], (DEPTH, D_MODEL, IN_WIDTH), D_MODEL ** -0.5),
        'w_conv_qk': nrm(ks[8], (DEPTH, ML_CONV, 2 * ML_QK_WIDTH), ML_CONV ** -0.5),
        'b_gates': gate_base[None, :] + nrm(ks[9], (DEPTH, ML_GATES), 0.1),
        'attn_sink': nrm(ks[10], (DEPTH, ATT_HEADS), 0.5),
        'g_mlstm_out': 1.0 + nrm(ks[11], (DEPTH, ML_WIDTH), 0.05),
        'w_out': nrm(ks[12], (DEPTH, MIX_WIDTH, D_MODEL), MIX_WIDTH ** -0.5),
        'g_post_mix': 1.0 + nrm(ks[13], (DEPTH, D_MODEL), 0.05),
        'g_pre_ffn': 1.0 + nrm(ks[14], (DEPTH, D_MODEL), 0.05),
        'w_ffn_in': nrm(ks[15], (DEPTH, D_MODEL, 2 * FFN_HIDDEN), D_MODEL ** -0.5),
        'w_ffn_out': nrm(ks[16], (DEPTH, FFN_HIDDEN, D_MODEL), FFN_HIDDEN ** -0.5),
        'g_post_ffn': 1.0 + nrm(ks[17], (DEPTH, D_MODEL), 0.05),
    }

def first_block(x, c, ctx, c_ctx, w_ada, b_ada, g_pre_mix, w_in, w_conv_qk, b_gates, attn_sink,
              g_mlstm_out, w_out, g_post_mix, g_pre_ffn, w_ffn_in, w_ffn_out, g_post_ffn):
    B, S, _ = x.shape
    L = ctx.shape[1]
    rope = axial_rope_tables(S, x.dtype)
    silu_c = jax.nn.silu(c)
    silu_cc = jax.nn.silu(c_ctx)
    for layer in range(DEPTH):
        advance_ctx = layer + 1 < DEPTH
        mod_x = (silu_c @ w_ada[layer] + b_ada[layer])[:, None, :]
        mod_c = silu_cc @ w_ada[layer] + b_ada[layer]
        sh_m, sc_m, gt_m, sh_f, sc_f, gt_f = jnp.split(mod_x, 6, axis=-1)
        csh_m, csc_m, cgt_m, csh_f, csc_f, cgt_f = jnp.split(mod_c, 6, axis=-1)

        px = modulate(rms_norm(x, g_pre_mix[layer]), sh_m, sc_m) @ w_in[layer]
        pc = modulate(rms_norm(ctx, g_pre_mix[layer]), csh_m, csc_m) @ w_in[layer]
        aqx, akx, avx, mqx, mkx, mvx, mox, mgx = jnp.split(px, SPLIT_AT, axis=-1)
        aqc, akc, avc, mqc, mkc, mvc, moc, mgc = jnp.split(pc, SPLIT_AT, axis=-1)

        kc_att = akc.reshape(B, L, ATT_KV_HEADS, ATT_HEAD_DIM)
        vc_att = avc.reshape(B, L, ATT_KV_HEADS, ATT_HEAD_DIM)
        qx_att = axial_rope(aqx.reshape(B, S, ATT_HEADS, ATT_HEAD_DIM), *rope)
        kx_att = axial_rope(akx.reshape(B, S, ATT_KV_HEADS, ATT_HEAD_DIM), *rope)
        att_x = window_attention(qx_att, kx_att, avx.reshape(B, S, ATT_KV_HEADS, ATT_HEAD_DIM),
                                 kc_att, vc_att, attn_sink[layer])

        cq, ck, cv, cg = mlstm_prepare(mqc, mkc, mvc, mgc, w_conv_qk[layer], b_gates[layer])
        h_ml_c, st_f, st_b = mlstm_bidir(cq, ck, cv, cg, mlstm_zero_state(B), mlstm_zero_state(B))
        xq, xk, xv, xg = mlstm_prepare(mqx, mkx, mvx, mgx, w_conv_qk[layer], b_gates[layer])
        h_ml_x, _, _ = mlstm_bidir(xq, xk, xv, xg, st_f, st_b)
        ml_x = mlstm_output(h_ml_x, mox, g_mlstm_out[layer])

        mix_x = jnp.concatenate([att_x, ml_x], axis=-1) @ w_out[layer]
        x = x + gt_m * rms_norm(mix_x, g_post_mix[layer])
        if advance_ctx:
            att_c = context_self_attention(aqc.reshape(B, L, ATT_HEADS, ATT_HEAD_DIM), kc_att, vc_att, attn_sink[layer])
            ml_c = mlstm_output(h_ml_c, moc, g_mlstm_out[layer])
            mix_c = jnp.concatenate([att_c, ml_c], axis=-1) @ w_out[layer]
            ctx = ctx + cgt_m * rms_norm(mix_c, g_post_mix[layer])

        fx = swiglu(modulate(rms_norm(x, g_pre_ffn[layer]), sh_f, sc_f), w_ffn_in[layer], w_ffn_out[layer])
        x = x + gt_f * rms_norm(fx, g_post_ffn[layer])
        if advance_ctx:
            fc = swiglu(modulate(rms_norm(ctx, g_pre_ffn[layer]), csh_f, csc_f), w_ffn_in[layer], w_ffn_out[layer])
            ctx = ctx + cgt_f * rms_norm(fc, g_post_ffn[layer])
    return x


CHUNK = 64
N_META = 16
WINDOW_CHUNKS = WINDOW // CHUNK
GLA_HEADS = 4
GLA_DK = 64
GLA_DV = 128
GLA_GATE_RANK = 16
GLA_GATE_TEMP = 16.0
D_FF = 2816

ATT_Q = ATT_HEADS * ATT_HEAD_DIM
ATT_KV = ATT_KV_HEADS * ATT_HEAD_DIM
GLA_QK = GLA_HEADS * GLA_DK
GLA_V = GLA_HEADS * GLA_DV
SPLITS = (ATT_Q, ATT_KV, ATT_KV, GLA_QK, GLA_QK, GLA_V, GLA_V, GLA_GATE_RANK, D_MODEL, D_MODEL)
D_IN = ATT_Q + 2 * ATT_KV + 2 * GLA_QK + 2 * GLA_V + GLA_GATE_RANK + 2 * D_MODEL


def rmsnorm(x, g):
    xf = x.astype(jnp.float32)
    y = xf * lax.rsqrt(jnp.mean(xf * xf, axis=-1, keepdims=True) + EPS)
    return (y * g.astype(jnp.float32)).astype(x.dtype)

def swiglu_2(x, w_gate, w_up, w_down):
    return (jax.nn.silu(x @ w_gate) * (x @ w_up)) @ w_down

def window_sink_attention(q, k, v, sinks):
    B, L = q.shape[0], q.shape[1]
    n_frames = L - N_META
    nc = n_frames // CHUNK
    G = ATT_HEADS // ATT_KV_HEADS
    NB = (WINDOW_CHUNKS + 1) * CHUNK
    pad = WINDOW_CHUNKS * CHUNK
    scale = ATT_HEAD_DIM ** -0.5
    slopes = jnp.exp2(-8.0 * jnp.arange(1, ATT_HEADS + 1, dtype=jnp.float32) / ATT_HEADS).reshape(ATT_KV_HEADS, G)
    sink = sinks.astype(jnp.float32).reshape(ATT_KV_HEADS, G)

    qm = q[:, :N_META].reshape(B, N_META, ATT_KV_HEADS, G, ATT_HEAD_DIM)
    qf = q[:, N_META:].reshape(B, nc, CHUNK, ATT_KV_HEADS, G, ATT_HEAD_DIM)
    km, kf = k[:, :N_META], k[:, N_META:]
    vm, vf = v[:, :N_META], v[:, N_META:]

    def band(t):
        tp = jnp.pad(t, ((0, 0), (pad, 0), (0, 0), (0, 0)))
        tp = tp.reshape(B, nc + WINDOW_CHUNKS, CHUNK, ATT_KV_HEADS, ATT_HEAD_DIM)
        return jnp.concatenate([tp[:, j:j + nc] for j in range(WINDOW_CHUNKS + 1)], axis=2)

    kb, vb = band(kf), band(vf)
    qi = jnp.arange(nc)[:, None] * CHUNK + jnp.arange(CHUNK)[None, :]
    ki = jnp.arange(nc)[:, None] * CHUNK - pad + jnp.arange(NB)[None, :]
    dist = jnp.abs(qi[:, :, None] - ki[:, None, :]).astype(jnp.float32)
    valid = (ki >= 0)[:, None, :]

    s_band = jnp.einsum('bcqkgd,bcskd->bkgcqs', qf, kb).astype(jnp.float32) * scale
    s_band = s_band - slopes[None, :, :, None, None, None] * dist[None, None, None]
    s_band = jnp.where(valid, s_band, -jnp.inf)
    s_meta = jnp.einsum('bcqkgd,bmkd->bkgcqm', qf, km).astype(jnp.float32) * scale
    s_sink = jnp.broadcast_to(sink[None, :, :, None, None, None], (B, ATT_KV_HEADS, G, nc, CHUNK, 1))
    p = jax.nn.softmax(jnp.concatenate([s_meta, s_band, s_sink], axis=-1), axis=-1).astype(v.dtype)
    of = (jnp.einsum('bkgcqm,bmkd->bcqkgd', p[..., :N_META], vm)
          + jnp.einsum('bkgcqs,bcskd->bcqkgd', p[..., N_META:N_META + NB], vb))
    of = of.reshape(B, n_frames, ATT_Q)

    sm = jnp.einsum('bqkgd,bmkd->bkgqm', qm, km).astype(jnp.float32) * scale
    sm_sink = jnp.broadcast_to(sink[None, :, :, None, None], (B, ATT_KV_HEADS, G, N_META, 1))
    pm = jax.nn.softmax(jnp.concatenate([sm, sm_sink], axis=-1), axis=-1).astype(v.dtype)
    om = jnp.einsum('bkgqm,bmkd->bqkgd', pm[..., :N_META], vm).reshape(B, N_META, ATT_Q)
    return jnp.concatenate([om, of], axis=1)

def gated_linear_attention(q, k, v, log_a):
    B, L = q.shape[0], q.shape[1]
    lead = (-L) % CHUNK
    nc = (L + lead) // CHUNK

    def chunked(t):
        t = jnp.pad(t.astype(jnp.float32), ((0, 0), (lead, 0), (0, 0), (0, 0)))
        return t.reshape(B, nc, CHUNK, t.shape[2], t.shape[3]).transpose(0, 3, 1, 2, 4)

    qc = chunked(q) * (GLA_DK ** -0.5)
    kc, vc, gc = chunked(k), chunked(v), chunked(log_a)
    b = jnp.cumsum(gc, axis=3)
    qe = qc * jnp.exp(b)
    ke = kc * jnp.exp(-b)
    causal = jnp.tril(jnp.ones((CHUNK, CHUNK), dtype=bool))
    att = jnp.where(causal, jnp.einsum('bhcid,bhcjd->bhcij', qe, ke), 0.0)
    o_intra = jnp.einsum('bhcij,bhcjv->bhciv', att, vc)

    b_last = b[:, :, :, -1:]
    chunk_kv = jnp.einsum('bhcjd,bhcjv->bhcdv', kc * jnp.exp(b_last - b), vc)
    decay = jnp.exp(b_last[:, :, :, 0])

    def step(S, inp):
        dec, kv = inp
        return dec[..., None] * S + kv, S

    S0 = jnp.zeros((B, q.shape[2], GLA_DK, GLA_DV), jnp.float32)
    _, S_start = lax.scan(step, S0, (jnp.moveaxis(decay, 2, 0), jnp.moveaxis(chunk_kv, 2, 0)))
    S_start = jnp.moveaxis(S_start, 0, 2)
    o_inter = jnp.einsum('bhcid,bhcdv->bhciv', qe, S_start)
    o = (o_intra + o_inter).transpose(0, 2, 3, 1, 4).reshape(B, nc * CHUNK, q.shape[2], GLA_DV)
    return o[:, lead:]

def second_inputs(seed: int = 0) -> dict:
    key = jax.random.key(seed)
    ks = jax.random.split(key, 24)
    f32 = jnp.float32

    def nrm(k, shape, scale):
        return jax.random.normal(k, shape, f32) * scale

    def gain(k, shape):
        return 1.0 + 0.02 * jax.random.normal(k, shape, f32)

    return {
        "x": nrm(ks[0], (BATCH, SEQ, D_MODEL), 1.0),
        "meta_tokens": nrm(ks[1], (N_META, D_MODEL), 1.0),
        "ffn1_norm": gain(ks[2], (DEPTH, D_MODEL)),
        "ffn1_w_gate": nrm(ks[3], (DEPTH, D_MODEL, D_FF), D_MODEL ** -0.5),
        "ffn1_w_up": nrm(ks[4], (DEPTH, D_MODEL, D_FF), D_MODEL ** -0.5),
        "ffn1_w_down": nrm(ks[5], (DEPTH, D_FF, D_MODEL), D_FF ** -0.5),
        "mix_norm": gain(ks[6], (DEPTH, D_MODEL)),
        "w_in": nrm(ks[7], (DEPTH, D_MODEL, D_IN), D_MODEL ** -0.5),
        "gla_gate_w": nrm(ks[8], (DEPTH, GLA_GATE_RANK, GLA_QK), GLA_GATE_RANK ** -0.5),
        "gla_gate_b": nrm(ks[9], (DEPTH, GLA_QK), 0.1),
        "gla_out_norm": gain(ks[10], (DEPTH, GLA_DV)),
        "att_sinks": nrm(ks[11], (DEPTH, ATT_HEADS), 1.0),
        "w_branch_att": nrm(ks[12], (DEPTH, ATT_Q, D_MODEL), ATT_Q ** -0.5),
        "w_branch_gla": nrm(ks[13], (DEPTH, GLA_V, D_MODEL), GLA_V ** -0.5),
        "w_out": nrm(ks[14], (DEPTH, D_MODEL, D_MODEL), D_MODEL ** -0.5),
        "ffn2_norm": gain(ks[15], (DEPTH, D_MODEL)),
        "ffn2_w_gate": nrm(ks[16], (DEPTH, D_MODEL, D_FF), D_MODEL ** -0.5),
        "ffn2_w_up": nrm(ks[17], (DEPTH, D_MODEL, D_FF), D_MODEL ** -0.5),
        "ffn2_w_down": nrm(ks[18], (DEPTH, D_FF, D_MODEL), D_FF ** -0.5),
        "final_norm": gain(ks[19], (D_MODEL,)),
    }

def second_block(x, meta_tokens, ffn1_norm, ffn1_w_gate, ffn1_w_up, ffn1_w_down, mix_norm, w_in,
              gla_gate_w, gla_gate_b, gla_out_norm, att_sinks, w_branch_att, w_branch_gla, w_out,
              ffn2_norm, ffn2_w_gate, ffn2_w_up, ffn2_w_down, final_norm):
    B = x.shape[0]
    meta = jnp.broadcast_to(meta_tokens[None].astype(x.dtype), (B, N_META, D_MODEL))
    h = jnp.concatenate([meta, x], axis=1)
    L = h.shape[1]
    offsets = np.cumsum(SPLITS)[:-1]
    for l in range(DEPTH):
        h = h + 0.5 * swiglu_2(rmsnorm(h, ffn1_norm[l]), ffn1_w_gate[l], ffn1_w_up[l], ffn1_w_down[l])

        u = rmsnorm(h, mix_norm[l])
        (aq, ak, av, gq, gk, gv, gr, g_low, gate_a, gate_b) = jnp.split(u @ w_in[l], offsets, axis=-1)

        ya = window_sink_attention(aq.reshape(B, L, ATT_HEADS, ATT_HEAD_DIM),
                                   ak.reshape(B, L, ATT_KV_HEADS, ATT_HEAD_DIM),
                                   av.reshape(B, L, ATT_KV_HEADS, ATT_HEAD_DIM),
                                   att_sinks[l])

        z = (g_low @ gla_gate_w[l] + gla_gate_b[l]).astype(jnp.float32)
        log_a = jax.nn.log_sigmoid(z) / GLA_GATE_TEMP
        og = gated_linear_attention(gq.reshape(B, L, GLA_HEADS, GLA_DK),
                                    gk.reshape(B, L, GLA_HEADS, GLA_DK),
                                    gv.reshape(B, L, GLA_HEADS, GLA_DV),
                                    log_a.reshape(B, L, GLA_HEADS, GLA_DK)).astype(x.dtype)
        og = rmsnorm(og, gla_out_norm[l]) * jax.nn.silu(gr.reshape(B, L, GLA_HEADS, GLA_DV))
        yb = og.reshape(B, L, GLA_V)

        mixed = (jax.nn.sigmoid(gate_a) * (ya @ w_branch_att[l])
                 + jax.nn.sigmoid(gate_b) * (yb @ w_branch_gla[l]))
        h = h + mixed @ w_out[l]

        h = h + 0.5 * swiglu_2(rmsnorm(h, ffn2_norm[l]), ffn2_w_gate[l], ffn2_w_up[l], ffn2_w_down[l])
    return rmsnorm(h, final_norm)[:, N_META:]


def setup_inputs(seed=0):
    out = dict(first_inputs(seed))
    for name, value in second_inputs(seed + 1).items():
        if name != "x":
            out[name + "_2"] = value
    return out


def reference(
    x, c, ctx, c_ctx, w_ada, b_ada, g_pre_mix, w_in, w_conv_qk, b_gates, attn_sink, g_mlstm_out,
    w_out, g_post_mix, g_pre_ffn, w_ffn_in, w_ffn_out, g_post_ffn, meta_tokens_2, ffn1_norm_2,
    ffn1_w_gate_2, ffn1_w_up_2, ffn1_w_down_2, mix_norm_2, w_in_2, gla_gate_w_2, gla_gate_b_2,
    gla_out_norm_2, att_sinks_2, w_branch_att_2, w_branch_gla_2, w_out_2, ffn2_norm_2,
    ffn2_w_gate_2, ffn2_w_up_2, ffn2_w_down_2, final_norm_2,
):
    x = first_block(
        x, c, ctx, c_ctx, w_ada, b_ada, g_pre_mix, w_in, w_conv_qk, b_gates, attn_sink,
        g_mlstm_out, w_out, g_post_mix, g_pre_ffn, w_ffn_in, w_ffn_out, g_post_ffn,
    )
    return second_block(
        x, meta_tokens_2, ffn1_norm_2, ffn1_w_gate_2, ffn1_w_up_2, ffn1_w_down_2, mix_norm_2,
        w_in_2, gla_gate_w_2, gla_gate_b_2, gla_out_norm_2, att_sinks_2, w_branch_att_2,
        w_branch_gla_2, w_out_2, ffn2_norm_2, ffn2_w_gate_2, ffn2_w_up_2, ffn2_w_down_2,
        final_norm_2,
    )


_drawn_inputs = setup_inputs


def setup_inputs(seed=0):
    import zlib

    import numpy as np

    out = dict(_drawn_inputs(seed))
    spreads = {}
    factors = {'attn_sink': 8.0,
     'g_mlstm_out': 3.269,
     'g_post_mix': 2.784,
     'g_post_ffn': 3.209,
     'ffn1_norm_2': 6.63,
     'mix_norm_2': 4.7,
     'gla_gate_b_2': 4.784,
     'gla_out_norm_2': 24.653,
     'att_sinks_2': 64.0,
     'ffn2_norm_2': 23.16}
    for name, (base, spread) in spreads.items():
        noise = np.random.default_rng([zlib.crc32(name.encode()), seed]).standard_normal(out[name].shape)
        drawn = base * np.exp(spread * noise) if base else spread * noise
        out[name] = __import__('jax').numpy.asarray(drawn.astype(out[name].dtype))
    for name, factor in factors.items():
        out[name] = (out[name] * factor).astype(out[name].dtype)
    return out
```

```python
from contextlib import ExitStack

import numpy as np
import concourse.bass as bass
from concourse import mybir

F32 = mybir.dt.float32
F32R = mybir.dt.float32r
U32 = mybir.dt.uint32
ACT = mybir.ActivationFunctionType
ALU = mybir.AluOpType
ds = bass.ds

P = 128
D = 1024
KD = D // P
T = 256
L = 256
META = 16
TM = META + T
HID = 2816
KH = HID // P
EPS = 1e-6
BIG = 1e30
HD = 64
NHEAD = 8
HALF = KH // 2
SLOT = HALF * P
RING = 4
QS = -(HD ** -0.5)

V_C, V_BADA, V_NORM, V_CONV, V_GML, V_GB, V_GO = 0, 16, 64, 128, 140, 144, 146
V_SINK1, V_SINK2, V_BG, NV = 147, 155, 163, 179
N_PRE, N_POST, N_PREF, N_POSTF, N_F1, N_MIX, N_F2, N_FIN = range(8)

PHASES = [("ada1", 4), ("win0", 1), ("ada2a", 2), ("win1", 1), ("ada2b", 2), ("win2", 1), ("ada2c", 2),
          ("win3", 1), ("ada2d", 2), ("win4", 1), ("wout", 2), ("gu0", 11), ("dn0", 4), ("gu1", 11), ("dn1", 4),
          ("in2k", 5), ("in2g", 4), ("bra", 1), ("brb", 1), ("wout2", 2), ("gu2", 11), ("dn2", 4)]
BASE, USE = {}, {}
_it = _use = 0
for _name, _n in PHASES:
    BASE[_name], USE[_name] = _it, _use
    _it += _n
    _use += _n * (2 if _name in ("bra", "brb") else 1)
COUNT = dict(PHASES)
LASTG = _it


def shape_constants():
    f = np.float32
    p = np.arange(P)
    ident = np.eye(P, dtype=f)
    ones = np.ones((P, P), f)
    perm = np.zeros((P, P), f)
    for d in range(P):
        if d % 32 < 16:
            perm[d + 16, d] = -1.0
        else:
            perm[d - 16, d] = 1.0
    swap = np.zeros((P, P), f)
    swap[p, (p + HD) % P] = 1.0
    tok = np.arange(T)
    inv_freq = np.power(f(10000.0), -np.arange(16, dtype=f) / f(16)).astype(f)
    pos = np.where((p % HD < 32)[:, None], (tok // 64)[None, :], (tok % 64)[None, :]).astype(f)
    ang = (pos * inv_freq[p % 16][:, None]).astype(f)
    win = np.zeros((P, 2, 512), f)
    for b in range(2):
        q = b * P + p
        win[:, b, 0:T] = np.where(np.abs(q[:, None] - tok[None, :]) <= 128, 0.0, BIG)
    up = np.where(p[:, None] <= p[None, :], 0.0, BIG).astype(f)
    low = np.where(p[:, None] >= p[None, :], 0.0, BIG).astype(f)
    zero = np.zeros((P, P), f)
    ordf = np.concatenate([up, zero], 1)
    ordb = np.concatenate([zero, low], 1)
    sel = np.zeros((P, 4, P), f)
    for h in range(4):
        sel[h, h, :] = 1.0
    one_row = np.ones((P, 256), f)
    first = [a.reshape(P, -1) for a in (perm, np.cos(ang), np.sin(ang), win, ordf, ordb, low, sel, one_row)]
    dist = np.full((P, 2, TM), BIG, f)
    for b in range(2):
        q = b * P + p
        dist[:, b, 0:META] = 0.0
        gap = (q // 64)[:, None] - (tok // 64)[None, :]
        dist[:, b, META:] = np.where((gap >= 0) & (gap <= 2), np.abs(q[:, None] - tok[None, :]), BIG)
    reset = np.ones((P, TM), f)
    reset[:, [0] + [META + 64 * c for c in range(4)]] = 0.0
    second = [a.reshape(P, -1) for a in (dist, reset)]
    causal = np.zeros((P, 8, 64), np.uint32)
    causal[0:64] = (np.arange(64)[:, None] <= np.arange(64)[None, :])[:, None, :]
    cat = lambda xs: np.ascontiguousarray(np.concatenate(xs, 1).astype(f))
    return cat([ident, ones, swap]), cat(first), cat(second), causal


def program(nc, dr, out):
    with ExitStack() as root:
        def sbuf(stack, name, shape, dt=F32):
            return stack.enter_context(nc.sbuf_tensor(name, shape, dt))

        def sem(name):
            return root.enter_context(nc.semaphore(name))

        cst = sbuf(root, "cst", [P, 3 * P])
        ident, ones, swap = cst[:, 0:P], cst[:, P:2 * P], cst[:, 2 * P:3 * P]
        vec = sbuf(root, "vec", [P, NV])
        mods = sbuf(root, "mods", [P, 48, 2])
        gmod = sbuf(root, "gmod", [P, KD, 5])
        silu_c = sbuf(root, "silu_c", [P, 16])
        cH = sbuf(root, "cH", [P, 16], F32R)
        cL = sbuf(root, "cL", [P, 16], F32R)
        R = sbuf(root, "R", [P, KD, TM])
        raw = sbuf(root, "raw", [P, RING, SLOT])
        hi = sbuf(root, "hi", [P, RING, SLOT], F32R)
        lo = sbuf(root, "lo", [P, RING, SLOT], F32R)
        mixH = sbuf(root, "mixH", [P, KD, T], F32R)
        mixL = sbuf(root, "mixL", [P, KD, T], F32R)
        inv = sbuf(root, "inv", [P, 512])
        rms = sbuf(root, "rms", [P, 512])
        sinkn = sbuf(root, "sinkn", [P, 16])
        negm = sbuf(root, "negm", [P, 32])
        rsum = sbuf(root, "rsum", [P, 32])
        esink = sbuf(root, "esink", [P, 32])
        rinv = sbuf(root, "rinv", [P, 32])

        blk1 = ExitStack()
        c1 = sbuf(blk1, "c1", [P, 3072])
        o = 0
        def c1_take(n):
            nonlocal o
            o += n
            return c1[:, o - n:o]
        perm, cosT, sinT = c1_take(P), c1_take(T), c1_take(T)
        winmask = c1_take(1024).rearrange("p (b k) -> p b k", b=2)
        ordf, ordb, ordlow = c1_take(256), c1_take(256), c1_take(P)
        sel4 = c1_take(512).rearrange("p (h m) -> p h m", h=4)
        onerow = c1_take(256)
        kvraw = sbuf(blk1, "kvraw", [P, 2, 512])
        cinq = sbuf(blk1, "cinq", [P, 2, T + 2])
        cink = sbuf(blk1, "cink", [P, 2, 2, T + 2])
        mvT = sbuf(blk1, "mvT", [P, 4, 512])
        qT = sbuf(blk1, "qT", [P, 4, T])
        sgo = sbuf(blk1, "sgo", [P, 4, T])
        gt = sbuf(blk1, "gt", [P, 4, 16])
        glog = sbuf(blk1, "glog", [P, 4, 2, 4])
        nrm1 = ExitStack()
        n5H = sbuf(nrm1, "n5H", [P, KD, 512], F32R)
        n5L = sbuf(nrm1, "n5L", [P, KD, 512], F32R)
        sq5 = sbuf(nrm1, "sq5", [P, KD, 512])
        ctxT = sbuf(nrm1, "ctxT", [P, KD, L])
        nrm1.close()
        mx1 = ExitStack()
        mq = sbuf(mx1, "mq", [P, 2, T])
        mk = sbuf(mx1, "mk", [P, 2, 512])
        kT = sbuf(mx1, "kT", [P, 512])
        kTs = sbuf(mx1, "kTs", [P, 512])
        avz = sbuf(mx1, "avz", [P, 4, 2, 192])
        vtok = sbuf(mx1, "vtok", [P, 4, 512])
        ktok = sbuf(mx1, "ktok", [P, 2, T])
        kw = sbuf(mx1, "kw", [P, 2, 2, T])
        Cst = sbuf(mx1, "Cst", [P, 4, 256])
        bR = sbuf(mx1, "bR", [4, 2, 512])
        rR = sbuf(mx1, "rR", [4, 2, 512])
        MR = sbuf(mx1, "MR", [4, 2, 512])
        m0 = sbuf(mx1, "m0", [4, 2])
        D16 = sbuf(mx1, "D16", [4, 16])
        rcol = sbuf(mx1, "rcol", [P, 4, 8])
        bc16 = sbuf(mx1, "bc16", [P, 16])
        wkx = sbuf(mx1, "wkx", [P, 2, 8])
        Sm = sbuf(mx1, "Sm", [P, 2, 512])
        pT = sbuf(mx1, "pT", [P, 2, 512])
        t1 = sbuf(mx1, "t1", [P, 2, T])
        hT = sbuf(mx1, "hT", [P, 4, T])
        den1 = sbuf(mx1, "den1", [P, T])
        emt = sbuf(mx1, "emt", [P, 2, T])
        zE = mvT[:, 0, 0:384]
        Aw = mvT[:, 1, 0:384]
        wint = mvT[:, 2, 0:T]
        qw = mvT[:, 2, 256:512]
        hsq = mvT[:, 3, :]
        mx1.close()
        blk1.close()

        ffn = ExitStack()
        nH = sbuf(ffn, "nH", [P, KD, TM], F32R)
        nL = sbuf(ffn, "nL", [P, KD, TM], F32R)
        ffn2 = ExitStack()
        sq = sbuf(ffn2, "sq", [P, KD, TM])
        Y = sbuf(ffn2, "Y", [P, KD, T])
        gH = sbuf(ffn2, "gH", [P, KH, TM], F32R)
        gL = sbuf(ffn2, "gL", [P, KH, TM], F32R)
        sg = sbuf(ffn2, "sg", [P, 2, TM])
        hbuf = sbuf(ffn2, "hbuf", [P, 2, TM])
        ffn2.close()
        blk2 = ExitStack()
        c2 = sbuf(blk2, "c2", [P, 3 * TM])
        dist = c2[:, 0:2 * TM].rearrange("p (b k) -> p b k", b=2)
        reset = c2[:, 2 * TM:3 * TM]
        causal = sbuf(blk2, "causal", [P, 8, 64], U32)
        gatew = sbuf(blk2, "gatew", [16, 256])
        glT = sbuf(blk2, "glT", [16, TM])
        kvraw2 = sbuf(blk2, "kvraw2", [P, 2, TM])
        gkT = sbuf(blk2, "gkT", [P, 2, TM])
        gqT = sbuf(blk2, "gqT", [P, 2, T])
        gvT = sbuf(blk2, "gvT", [P, 4, TM])
        qT2 = sbuf(blk2, "qT2", [P, 4, T])
        grT = sbuf(blk2, "grT", [P, 4, T])
        gab = sbuf(blk2, "gab", [P, 2 * KD, T])
        tA = sbuf(blk2, "tA", [P, 2, TM])
        tB = sbuf(blk2, "tB", [P, 2, TM])
        tC = sbuf(blk2, "tC", [P, 2, TM])
        blast = sbuf(blk2, "blast", [P, 2, 4])
        kdT = sbuf(blk2, "kdT", [P, 2, TM])
        kS2 = sbuf(blk2, "kS2", [P, TM])
        avz2 = sbuf(blk2, "avz2", [P, 3, 2, 192])
        gvtok = sbuf(blk2, "gvtok", [64, 5, 512])
        kdtok = sbuf(blk2, "kdtok", [64, 4, 256])
        St = sbuf(blk2, "St", [P, 4, 2, P])
        attm = sbuf(blk2, "attm", [64, 4, 4, 64])
        bias2 = sbuf(blk2, "bias2", [P, 2, 2, TM])
        Sm2 = sbuf(blk2, "Sm2", [P, 2, TM])
        pT2 = sbuf(blk2, "pT2", [P, 2, 384])
        og = gvT
        blk2.close()
        ffn.close()

        acc = root.enter_context(nc.psum_tensor("acc", [P, 4, 512], F32))
        wk = root.enter_context(nc.psum_tensor("wk", [P, 4, 512], F32))

        vec_in, tok_in, cst_in, c1_in, c2_in = (sem(n) for n in ("vec_in", "tok_in", "cst_in", "c1_in", "c2_in"))
        raw_ready = [sem(f"raw_ready{j}") for j in range(RING)]
        hi_ready, lo_ready = sem("hi_ready"), sem("lo_ready")
        mm_done = sem("mm_done")
        acc_free = [sem("acc_free0"), sem("acc_free1")]
        act_chain, dve_chain = sem("act_chain"), sem("dve_chain")
        c_hi, c_lo = sem("c_hi"), sem("c_lo")
        sq_ready, ssq_ps, rms_ready = sem("sq_ready"), sem("ssq_ps"), sem("rms_ready")
        xn_ready, nh_ready, nl_ready = sem("xn_ready"), sem("nh_ready"), sem("nl_ready")
        r_ready = sem("r_ready")
        gh_ready, gl_ready = sem("gh_ready"), sem("gl_ready")
        mx_sum, mxh_ready, mxl_ready = sem("mx_sum"), sem("mxh_ready"), sem("mxl_ready")
        out_ready, out_sent = sem("out_ready"), sem("out_sent")
        pads, zero2, bias_ready = sem("pads"), sem("zero2"), sem("bias_ready")
        s_ps, s_max, p_exp, p_norm = sem("s_ps"), sem("s_max"), sem("p_exp"), sem("p_norm")
        pt_ps, pt_ready, o_ps, oh_ready, ol_ready = (sem(n) for n in ("pt_ps", "pt_ready", "o_ps", "oh_ready", "ol_ready"))
        gt_log, lf_ready, rows_ps, rows_ready = sem("gt_log"), sem("lf_ready"), sem("rows_ps"), sem("rows_ready")
        cols_ps, wk_arg, wk_ready = sem("cols_ps"), sem("wk_arg"), sem("wk_ready")
        rope_ps, rope_ready, avt_ps, avz_ready = sem("rope_ps"), sem("rope_ready"), sem("avt_ps"), sem("avz_ready")
        mvt_ps, vtok_ready, conv_ready, mqk_ready = sem("mvt_ps"), sem("vtok_ready"), sem("conv_ready"), sem("mqk_ready")
        kt_ps, ktok_ready, ks_ps, ks_ready = sem("kt_ps"), sem("ktok_ready"), sem("ks_ps"), sem("ks_ready")
        kw_ready, cst_ps, cst_ready = sem("kw_ready"), sem("cst_ps"), sem("cst_ready")
        ms_ps, mb_ps, mw_ready, z_ready, e_ready = (sem(n) for n in ("ms_ps", "mb_ps", "mw_ready", "z_ready", "e_ready"))
        a_ready, qw_ready, nd_ps, nd_used = sem("a_ready"), sem("qw_ready"), sem("nd_ps"), sem("nd_used")
        hsum_ready, hsq_ready, hss_ps, hrms = sem("hsum_ready"), sem("hsq_ready"), sem("hss_ps"), sem("hrms")
        mlo_ready, mlh_ready, mll_ready = sem("mlo_ready"), sem("mlh_ready"), sem("mll_ready")
        z_ps, z_abs, z_ln, b_ready, eb_ready = (sem(n) for n in ("z_ps", "z_abs", "z_ln", "b_ready", "eb_ready"))
        bl_ready, ed_ready, kd_ready, qk_ready = sem("bl_ready"), sem("ed_ready"), sem("kd_ready"), sem("qk_ready")
        gvt_ps, gvt_ready, kdt_ps, kdt_ready = sem("gvt_ps"), sem("gvt_ready"), sem("kdt_ps"), sem("kdt_ready")
        kv_ps, st_ready, at_ps, at_ready = sem("kv_ps"), sem("st_ready"), sem("at_ps"), sem("at_ready")
        rows_done, go_ps, go_ready, gss_ps, grms = sem("rows_done"), sem("go_ps"), sem("go_ready"), sem("gss_ps"), sem("grms")
        yb_ready, ybh_ready, ybl_ready = sem("yb_ready"), sem("ybh_ready"), sem("ybl_ready")
        ks2_ps, ks2_ready, av2_ps, av2_ready = sem("ks2_ps"), sem("ks2_ready"), sem("av2_ps"), sem("av2_ready")

        epsc = EPS
        GV_BANKS = [wk[:, 2, :], wk[:, 3, :], acc[:, 2, :], acc[:, 3, :], wk[:, 2, :]]
        MV_BANKS = {2: wk[:, 1, :], 3: wk[:, 2, :], 0: wk[:, 3, :], 1: acc[:, 1, :]}
        CST_BANKS = [wk[:, 1, :], wk[:, 2, :], wk[:, 3, :], acc[:, 3, :]]
        HEADS = (0, 2, 1, 3)
        UNITS = [(hp, b, par) for hp in range(4) for b in range(2) for par in range(2)]

        def chunk(c):
            return (0, META) if c == 0 else (META + 64 * (c - 1), META + 64 * c)

        def lanes(h):
            return slice(HD * (h % 2), HD * (h % 2) + HD)

        def order(v):
            h, d = divmod(v, 2)
            return h, d, (0, 1, P) if d == 0 else (1, 0, 0)

        block = root.enter_context(nc.Block())

        @block.sync
        def _(sp):
            def load(g, j, src, first=False):
                if not first:
                    sp.wait_ge(lo_ready, 4 * g + j - 3)
                w = 1
                for n in src.shape[1:]:
                    w *= n
                dst = raw[:, j, 0:w].rearrange("p (k m) -> p k m", m=src.shape[2])
                sp.dma_start(dst, src).then_inc(raw_ready[j], 16)

            def panel(w, col, q, width=256):
                return w[512 * q:512 * q + 512, ds(col, width)].rearrange("(k p) m -> p k m", p=P)

            def columns(g, w, cols, first=False):
                for j in range(4):
                    load(g, j, panel(w, cols[j // 2], j % 2), first)

            def ada2(part):
                name = "ada2" + "abcd"[part]
                with sp.Fori(0, 2) as i:
                    c = 2048 + 1024 * part
                    columns(BASE[name] + i, dr["w_ada"], (512 * i + c, 512 * i + c + 256))

            def down(name, w):
                with sp.Fori(0, COUNT[name]) as i:
                    for j in range(4):
                        rows = w[SLOT * (j % 2):SLOT * (j % 2) + SLOT, ds(256 * i + P * (j // 2), P)]
                        load(BASE[name] + i, j, rows.rearrange("(k p) m -> p k m", p=P))

            def gate_up(name, wg, wu, up0):
                with sp.Fori(0, COUNT[name]) as i:
                    for j in range(4):
                        load(BASE[name] + i, j, panel(wg, 256 * i, j) if j < 2 else panel(wu, 256 * i + up0, j - 2))

            columns(0, dr["w_ada"], (0, 256), first=True)
            with sp.Fori(1, COUNT["ada1"]) as i:
                columns(i, dr["w_ada"], (512 * i, 512 * i + 256))
            w = dr["w_in"]
            g = BASE["win0"]
            load(g, 0, panel(w, 2304, 0, 16))
            load(g, 1, panel(w, 2304, 1, 16))
            load(g, 2, panel(w, 512, 0))
            load(g, 3, panel(w, 512, 1))
            ada2(0)
            for n, cols in enumerate(((768, 1024), (1280, 1536), (0, 256), (1792, 2048))):
                columns(BASE[f"win{n + 1}"], w, cols)
                if n < 3:
                    ada2(n + 1)
            with sp.Fori(0, COUNT["wout"]) as i:
                columns(BASE["wout"] + i, dr["w_out"], (512 * i, 512 * i + 256))
            gate_up("gu0", dr["w_ffn_in"], dr["w_ffn_in"], HID)
            down("dn0", dr["w_ffn_out"])
            gate_up("gu1", dr["ffn1_w_gate_2"], dr["ffn1_w_up_2"], 0)
            down("dn1", dr["ffn1_w_down_2"])
            w = dr["w_in_2"]
            g = BASE["in2k"]
            load(g, 0, panel(w, 2304, 0, 16))
            load(g, 1, panel(w, 2304, 1, 16))
            load(g, 2, panel(w, 512, 0))
            load(g, 3, panel(w, 512, 1))
            for n, cols in enumerate(((1024, 768), (1280, 1536), (0, 256), (1792, 2048))):
                columns(g + 1 + n, w, cols)
            with sp.Fori(0, COUNT["in2g"]) as i:
                columns(BASE["in2g"] + i, w, (512 * i + 2320, 512 * i + 2576))
            for name, wb in (("bra", dr["w_branch_att_2"]), ("brb", dr["w_branch_gla_2"])):
                for j in range(4):
                    load(BASE[name], j, panel(wb, 256 * j, 0))
            with sp.Fori(0, COUNT["wout2"]) as i:
                columns(BASE["wout2"] + i, dr["w_out_2"], (512 * i, 512 * i + 256))
            gate_up("gu2", dr["ffn2_w_gate_2"], dr["ffn2_w_up_2"], 0)
            down("dn2", dr["ffn2_w_down_2"])
            for k in range(KD):
                sp.wait_ge(out_ready, k + 1)
                sp.dma_start(out[:, k, :], Y[:, k, :]).then_inc(out_sent, 16)
            sp.wait_ge(out_sent, 16 * KD)

        @block.gpsimd
        def _(pool):
            pool.memset(cinq[:], 0.0)
            pool.memset(cink[:], 0.0).then_inc(pads, 1)
            pool.wait_ge(mm_done, 4 * BASE["win4"] + 4)
            pool.memset(avz[:], 0.0).then_inc(pads, 1)
            pool.wait_ge(mm_done, 4 * BASE["in2k"] + 2)
            pool.dma_start(c2[:], dr["c2"]).then_inc(c2_in, 16)
            pool.dma_start(causal[:], dr["causal"]).then_inc(c2_in, 16)
            pool.dma_start(gatew[:], dr["gla_gate_w_2"]).then_inc(c2_in, 16)
            pool.memset(avz2[:], 0.0)
            pool.memset(attm[:], 0.0).then_inc(zero2, 1)
            pool.wait_ge(c2_in, 48)
            for h in range(NHEAD):
                if h >= 2:
                    pool.wait_ge(s_max, 16 + 4 * (h // 2 - 1) + 2 + h % 2 + 1)
                pool.tensor_scalar(bias2[:, h % 2], dist, 2.0 ** -(h + 1), None, ALU.mult).then_inc(bias_ready, 1)

        @block.scalar
        def _(act):
            chain = 0

            def link(ins):
                nonlocal chain
                chain += 1
                ins.then_inc(act_chain, 1)
                act.wait_ge(act_chain, chain)

            def split(g, j, width):
                act.wait_ge(raw_ready[j], 16 * g + 16)
                if not (isinstance(g, int) and g == 0):
                    act.wait_ge(mm_done, 4 * g + j - 3)
                act.activation(hi[:, j, 0:width], raw[:, j, 0:width], ACT.Copy).then_inc(hi_ready, 1)

            def pipeline(name, width, evac, ahead):
                first, n = BASE[name], COUNT[name]
                if n > 1:
                    with act.Fori(1, n) as i:
                        for j in range(4):
                            split(first + i, j, width)
                            evac(i - 1, j)
                for j in range(4):
                    if ahead:
                        split(first + n, j, ahead[j])
                    evac(n - 1, j)

            K4 = [1024] * 4
            DN = [SLOT] * 4
            MG = [64, 64, 1024, 1024]

            def nothing(i, j):
                pass

            def multiplied(name, i, j):
                act.wait_ge(mm_done, 4 * (BASE[name] + i) + j + 1)

            act.dma_start(vec[:], dr["vecs"]).then_inc(vec_in, 16)
            act.dma_start(R[:], dr["hT"]).then_inc(tok_in, 16)
            act.dma_start(ctxT[:], dr["ctxT"]).then_inc(tok_in, 16)
            act.dma_start(cst[:], dr["cst"]).then_inc(cst_in, 16)
            act.dma_start(c1[:], dr["c1"]).then_inc(c1_in, 16)

            act.wait_ge(vec_in, 16)
            link(act.activation(silu_c[:], vec[:, V_C:V_C + 16], ACT.Silu))
            act.activation(cH[:], silu_c[:], ACT.Copy).then_inc(c_hi, 1)
            for j in range(4):
                split(0, j, 1024)
            act.wait_ge(tok_in, 32)
            for k in range(0, KD, 2):
                act.activation(sq5[:, k:k + 2, 0:T], R[:, k:k + 2, META:TM], ACT.Square).then_inc(sq_ready, 1)
                act.activation(sq5[:, k:k + 2, T:512], ctxT[:, k:k + 2, :], ACT.Square).then_inc(sq_ready, 1)
            pipeline("ada1", 1024, nothing, MG)

            def norm_rms(n, width):
                act.wait_ge(ssq_ps, n + 1)
                act.activation(rms[:, 0:width], wk[:, 0, 0:width], ACT.Sqrt, bias=epsc,
                               scale=1.0 / D).then_inc(rms_ready, 1)

            norm_rms(0, 512)
            for n in range(2 * KD):
                k, c = divmod(n, 2)
                act.wait_ge(xn_ready, n + 1)
                act.activation(n5H[:, k, T * c:T * c + T], sq5[:, k, T * c:T * c + T], ACT.Identity,
                               bias=mods[:, k, c:c + 1]).then_inc(nh_ready, 1)

            def evac_win0(i, j):
                if j == 3:
                    multiplied("win0", i, j)
                    act.activation(kvraw[:], acc[:, 2:4, :], ACT.Copy).then_inc(acc_free[1], 1)

            def evac_win1(i, j):
                if j == 1:
                    multiplied("win1", i, j)
                    act.wait_ge(pads, 1)
                    act.activation(cinq[:, :, 1:T + 1], acc[:, 0:2, 0:T], ACT.Copy).then_inc(acc_free[0], 1)

            def evac_win2(i, j):
                if j == 1:
                    multiplied("win2", i, j)
                    act.activation(mvT[:, 0:2, :], acc[:, 0:2, :], ACT.Copy).then_inc(acc_free[0], 1)

            def evac_win3(i, j):
                if j == 1:
                    multiplied("win3", i, j)
                    act.activation(qT[:, 0:2, :], acc[:, 0:2, 0:T], ACT.Copy, scale=QS).then_inc(acc_free[0], 1)

            def evac_win4(i, j):
                if j in (1, 3):
                    multiplied("win4", i, j)
                    act.activation(sgo[:, j - 1:j + 1, :], acc[:, j - 1:j + 1, 0:T],
                                   ACT.Sigmoid).then_inc(acc_free[j // 2], 1)

            pipeline("win0", 1024, evac_win0, K4)
            gf = gt[:].rearrange("p t (a q h) -> p t a q h", a=2, q=2)[:, :, :, 1, :]
            act.wait_ge(acc_free[0], USE["win0"] + 1)
            link(act.activation(glog[:], gf, ACT.Abs))
            link(act.activation(glog[:], glog[:], ACT.Exp, scale=-1.0))
            act.activation(glog[:], glog[:], ACT.Ln, bias=1.0).then_inc(gt_log, 1)
            pipeline("ada2a", 1024, nothing, K4)
            pipeline("win1", 1024, evac_win1, K4)
            pipeline("ada2b", 1024, nothing, K4)
            pipeline("win2", 1024, evac_win2, K4)
            pipeline("ada2c", 1024, nothing, K4)
            pipeline("win3", 1024, evac_win3, K4)
            pipeline("ada2d", 1024, nothing, K4)
            pipeline("win4", 1024, evac_win4, K4)

            for n, a in enumerate((mk[:, 0, :], mk[:, 1, :], mq[:, 0, :], mq[:, 1, :])):
                act.wait_ge(conv_ready, n + 1)
                act.activation(a, a, ACT.Silu).then_inc(mqk_ready, 1)
            act.wait_ge(pads, 2)
            act.wait_ge(avt_ps, 1)
            act.activation(avz[:, :, :, 64:128], acc[:, 3, :].rearrange("p (t g d) -> p t g d", t=4, g=2),
                           ACT.Copy).then_inc(avz_ready, 1)
            for n, t in enumerate((2, 3, 0, 1)):
                act.wait_ge(mvt_ps, n + 1)
                act.activation(vtok[:, t, :], MV_BANKS[t], ACT.Copy).then_inc(vtok_ready, 1)
            act.wait_ge(kt_ps, 1)
            act.activation(ktok[:], acc[:, 0, :].rearrange("p (t d) -> p t d", t=2), ACT.Copy).then_inc(ktok_ready, 1)
            act.wait_ge(wk_arg, 1)
            act.activation(wkx[:], wkx[:], ACT.Exp).then_inc(wk_ready, 1)
            act.wait_ge(ks_ps, 1)
            act.activation(kTs[:], acc[:, 2, :], ACT.Copy).then_inc(ks_ready, 1)

            def exp_scores(n, sm, sink):
                act.wait_ge(s_max, n + 1)
                act.activation(sm, sm, ACT.Exp, bias=negm[:, n:n + 1], scale=-1.0, accum_out=rsum[:, n:n + 1])
                act.activation(esink[:, n:n + 1], sink, ACT.Exp, bias=negm[:, n:n + 1], scale=-1.0).then_inc(p_exp, 1)

            def heads_out(n, hp):
                act.wait_ge(o_ps, n + 1)
                act.activation(mixH[:, hp, :], wk[:, 3, 0:T], ACT.Copy).then_inc(oh_ready, 1)

            for u in range(17):
                if u % 2 == 0 and u >= 2:
                    act.wait_ge(z_ready, u // 2)
                    act.activation(zE, zE, ACT.Exp, scale=-1.0).then_inc(e_ready, 1)
                if u < 16:
                    hp, b, par = UNITS[u]
                    exp_scores(u, Sm[:, u % 2, :], sinkn[:, 2 * hp + par:2 * hp + par + 1])
                if u % 2 == 1:
                    v = u // 2
                    h, d, _ = order(v)
                    act.wait_ge(mb_ps, v + 1)
                    if v >= 1:
                        act.wait_ge(qw_ready, v)
                    if v >= 2:
                        act.wait_ge(nd_used, v - 1)
                    act.activation(wint[lanes(h), :], acc[lanes(h), 1, 0:T], ACT.Exp, scale=-1.0,
                                   bias=bc16[lanes(h), 8 + 4 * d + h:9 + 4 * d + h])
                    act.activation(emt[:, v % 2, :], acc[:, 1, T:512], ACT.Exp, scale=-1.0).then_inc(mw_ready, 1)
                if u >= 1:
                    act.wait_ge(pt_ps, u)
                    act.activation(pT[:, (u - 1) % 2, :], wk[:, 2, :], ACT.Copy).then_inc(pt_ready, 1)
                    if (u - 1) % 4 == 3:
                        heads_out((u - 1) // 4, (u - 1) // 4)

            for hp in range(2):
                act.wait_ge(hsum_ready, 2 * hp + 2)
                act.activation(Sm[:, hp, :], hT[:, 2 * hp:2 * hp + 2, :].rearrange("p h t -> p (h t)"),
                               ACT.Square).then_inc(hsq_ready, 1)
            for hp in range(2):
                act.wait_ge(hss_ps, hp + 1)
                act.activation(pT[:, hp, :], acc[:, 1 + 2 * hp, :], ACT.Sqrt, bias=epsc, scale=1.0 / P).then_inc(hrms, 1)
            for h in range(4):
                act.wait_ge(mlo_ready, h + 1)
                act.activation(mixH[:, 4 + h, :], hT[:, h, :], ACT.Copy).then_inc(mlh_ready, 1)

            def copy_square(name, i, s, n, width):
                act.activation(Y[:, n, :], acc[:, 2 * s:2 * s + width, 0:T], ACT.Copy)
                act.activation(sq[:, n, 0:T], acc[:, 2 * s:2 * s + width, 0:T], ACT.Square).then_inc(acc_free[s], 1)

            def evac_wout(i, j):
                if j in (1, 3):
                    multiplied("wout", i, j)
                    copy_square("wout", i, j // 2, ds(4 * i + j - 1, 2), 2)

            def evac_dn0(i, j):
                if j in (1, 3):
                    multiplied("dn0", i, j)
                    copy_square("dn0", i, j // 2, ds(2 * i + j // 2, 1), 1)

            def square_r(k, width, t0, wait):
                act.wait_ge(*wait)
                act.activation(sq[:, k, 0:width], R[:, k, t0:t0 + width], ACT.Square).then_inc(sq_ready, 1)

            def gate_up(name, f, width, ahead):
                def evac(i, j):
                    if j == 1:
                        multiplied(name, i, j)
                        act.wait_ge(acc_free[1], USE[name] + i)
                        act.activation(sg[:, :, 0:width], acc[:, 0:2, 0:width], ACT.Silu).then_inc(acc_free[0], 1)
                    if j == 3:
                        act.wait_ge(acc_free[1], USE[name] + i + 1)
                        act.activation(gH[:, ds(2 * i, 2), 0:width], hbuf[:, :, 0:width], ACT.Copy).then_inc(gh_ready, 1)
                pipeline(name, 1024, evac, ahead)

            def normed(first, width, shift):
                for k in range(KD):
                    act.wait_ge(xn_ready, first + k + 1)
                    if shift is None:
                        act.activation(nH[:, k, 0:width], sq[:, k, 0:width], ACT.Copy).then_inc(nh_ready, 1)
                    else:
                        act.activation(nH[:, k, 0:width], sq[:, k, 0:width], ACT.Identity,
                                       bias=mods[:, shift + k, 0:1]).then_inc(nh_ready, 1)

            pipeline("wout", 1024, evac_wout, K4)
            norm_rms(1, T)
            for k in range(KD):
                square_r(k, T, META, (r_ready, k + 1))
            norm_rms(2, T)
            normed(16, T, 24)
            gate_up("gu0", 0, T, DN)
            pipeline("dn0", SLOT, evac_dn0, K4)
            norm_rms(3, T)
            for k in range(KD):
                square_r(k, TM, 0, (r_ready, 8 + k + 1))
            norm_rms(4, TM)
            normed(24, TM, None)
            gate_up("gu1", 1, TM, DN)

            def evac_dn(name, width, t0):
                def evac(i, j):
                    if j in (1, 3):
                        square_r(ds(2 * i + j // 2, 1), width, t0, (acc_free[j // 2], USE[name] + i + 1))
                return evac

            pipeline("dn1", SLOT, evac_dn("dn1", TM, 0), MG)
            norm_rms(5, TM)
            normed(32, TM, None)

            def evac_in2k(i, j):
                if j not in (1, 3):
                    return
                s = j // 2
                multiplied("in2k", i, j)
                src = acc[:, 2 * s:2 * s + 2, 0:TM]
                if i == 0 and s == 0:
                    ins = act.activation(glT[:], acc[0:16, 0, 0:TM], ACT.Copy)
                elif i == 0:
                    ins = act.activation(kvraw2[:], src, ACT.Copy)
                elif i == 1:
                    ins = act.activation(gkT[:] if s == 0 else gqT[:], src if s == 0 else src[:, :, 0:T], ACT.Copy)
                elif i == 2:
                    ins = act.activation(gvT[:, 2 * s:2 * s + 2, :], src, ACT.Copy)
                elif i == 3:
                    ins = act.activation(qT2[:, 2 * s:2 * s + 2, :], src[:, :, 0:T], ACT.Copy, scale=QS)
                else:
                    ins = act.activation(grT[:, 2 * s:2 * s + 2, :], src[:, :, 0:T], ACT.Silu)
                ins.then_inc(acc_free[s], 1)

            first = BASE["in2k"]
            for i in range(COUNT["in2k"]):
                for j in range(4):
                    split(first + i + 1, j, 1024)
                    evac_in2k(i, j)

            def evac_in2g(i, j):
                if j in (1, 3):
                    multiplied("in2g", i, j)
                    act.activation(gab[:, ds(4 * i + j - 1, 2), :], acc[:, j - 1:j + 1, 0:T],
                                   ACT.Sigmoid).then_inc(acc_free[j // 2], 1)

            pipeline("in2g", 1024, evac_in2g, K4)

            act.wait_ge(z_ps, 1)
            for t in range(2):
                ins = act.activation(tA[:, t, :], wk[:, t, 0:TM], ACT.Abs, bias=vec[:, V_GB + t:V_GB + t + 1])
            ins.then_inc(z_abs, 1)
            act.wait_ge(z_abs, 1)
            link(act.activation(tA[:], tA[:], ACT.Exp, scale=-1.0))
            act.activation(tA[:], tA[:], ACT.Ln, bias=1.0).then_inc(z_ln, 1)
            act.wait_ge(zero2, 1)
            act.wait_ge(av2_ps, 1)
            act.activation(avz2[0:META, 0, :, 64:128], acc[0:META, 0, 0:P].rearrange("p (g d) -> p g d", g=2), ACT.Copy)
            act.activation(avz2[:, 1:3, :, 64:128], acc[:, 0, P:3 * P].rearrange("p (t g d) -> p t g d", t=2, g=2),
                           ACT.Copy).then_inc(av2_ready, 1)
            act.wait_ge(ks2_ps, 1)
            act.activation(kS2[:], acc[:, 1, 0:TM], ACT.Copy).then_inc(ks2_ready, 1)
            for c in range(5):
                act.wait_ge(gvt_ps, c + 1)
                n = chunk(c)[1] - chunk(c)[0]
                act.activation(gvtok[0:n, c, :], GV_BANKS[c][0:n, :], ACT.Copy).then_inc(gvt_ready, 1)
            act.wait_ge(b_ready, 1)
            act.activation(tA[:], tC[:], ACT.Exp, scale=1.0 / 16)
            act.activation(tB[:], tC[:], ACT.Exp, scale=-1.0 / 16).then_inc(eb_ready, 1)
            act.wait_ge(bl_ready, 1)
            act.activation(tC[:, :, 0:208], tC[:, :, 0:208], ACT.Exp, scale=-1.0 / 16).then_inc(ed_ready, 1)

            for u in range(17):
                if u < 16:
                    hp, b, par = UNITS[u]
                    nk = META + P * (b + 1)
                    exp_scores(16 + u, Sm2[:, u % 2, 0:nk], sinkn[:, 8 + 2 * hp + par:9 + 2 * hp + par])
                if u >= 1:
                    b = UNITS[u - 1][1]
                    act.wait_ge(pt_ps, 16 + u)
                    act.activation(pT2[0:META, (u - 1) % 2, 0:P], wk[0:META, 2, 0:P], ACT.Copy)
                    act.activation(pT2[:, (u - 1) % 2, P:P * (b + 2)], wk[:, 2, P:P * (b + 2)],
                                   ACT.Copy).then_inc(pt_ready, 1)
                    if (u - 1) % 4 == 3:
                        heads_out(4 + (u - 1) // 4, (u - 1) // 4)

            act.wait_ge(kdt_ps, 1)
            act.activation(kdtok[0:META, 0, :], wk[0:META, 0, 0:T], ACT.Copy)
            act.activation(kdtok[:, 1, :], wk[0:64, 0, T:512], ACT.Copy).then_inc(kdt_ready, 1)
            act.wait_ge(kdt_ps, 2)
            act.activation(kdtok[:, 2:4, :], wk[0:64, 1, :].rearrange("p (c d) -> p c d", c=2),
                           ACT.Copy).then_inc(kdt_ready, 1)
            gsq = (tA, tB)
            grt = (tC, kdT)
            for n in range(2):
                act.wait_ge(go_ps, n + 1)
                act.activation(og[:, 2 * n:2 * n + 2, 0:T], acc[:, n, :].rearrange("p (h t) -> p h t", h=2), ACT.Copy)
                act.activation(gsq[n][:, :, 0:T], acc[:, n, :].rearrange("p (h t) -> p h t", h=2),
                               ACT.Square).then_inc(go_ready, 1)
            for n in range(2):
                act.wait_ge(gss_ps, n + 1)
                act.activation(grt[n][:, :, 0:T], acc[:, 2 + n, :].rearrange("p (h t) -> p h t", h=2), ACT.Sqrt, bias=epsc,
                               scale=1.0 / P).then_inc(grms, 1)
            for n, h in enumerate(HEADS):
                act.wait_ge(yb_ready, n + 1)
                act.activation(mixH[:, 4 + h, :], og[:, n, 0:T], ACT.Copy).then_inc(ybh_ready, 1)

            pipeline("bra", 1024, nothing, K4)

            def evac_brb(i, j):
                act.wait_ge(mx_sum, j + 1)
                act.activation(nH[:, 2 * j:2 * j + 2, 0:T], gab[:, 2 * j:2 * j + 2, :], ACT.Copy).then_inc(mxh_ready, 1)

            pipeline("brb", 1024, evac_brb, K4)

            def evac_wout2(i, j):
                if j in (1, 3):
                    square_r(ds(4 * i + j - 1, 2), T, META, (acc_free[j // 2], USE["wout2"] + i + 1))

            pipeline("wout2", 1024, evac_wout2, K4)
            norm_rms(6, T)
            normed(40, T, None)
            gate_up("gu2", 2, T, DN)
            pipeline("dn2", SLOT, evac_dn("dn2", T, META), None)
            norm_rms(7, T)

        @block.vector
        def _(dve):
            chain = 0

            def link(ins):
                nonlocal chain
                chain += 1
                ins.then_inc(dve_chain, 1)
                dve.wait_ge(dve_chain, chain)

            def split(g, j, width):
                dve.wait_ge(hi_ready, 4 * g + j + 1)
                dve.tensor_tensor(lo[:, j, 0:width], raw[:, j, 0:width], hi[:, j, 0:width].bitcast(F32),
                                  ALU.subtract).then_inc(lo_ready, 1)

            def pipeline(name, width, evac, ahead):
                first, n = BASE[name], COUNT[name]
                if n > 1:
                    with dve.Fori(1, n) as i:
                        for j in range(4):
                            split(first + i, j, width)
                            evac(i - 1, j)
                for j in range(4):
                    if ahead:
                        split(first + n, j, ahead[j])
                    evac(n - 1, j)

            K4 = [1024] * 4
            DN = [SLOT] * 4
            MG = [64, 64, 1024, 1024]

            def nothing(i, j):
                pass

            def multiplied(name, i, j):
                dve.wait_ge(mm_done, 4 * (BASE[name] + i) + j + 1)

            def col(c):
                return vec[:, c:c + 1]

            def gains(n):
                return vec[:, V_NORM + KD * n:V_NORM + KD * n + KD]

            dve.wait_ge(vec_in, 16)
            dve.tensor_scalar(sinkn[:], vec[:, V_SINK1:V_SINK1 + 16], -1.0, None, ALU.mult)
            dve.wait_ge(c_hi, 1)
            dve.tensor_tensor(cL[:], silu_c[:], cH[:].bitcast(F32), ALU.subtract).then_inc(c_lo, 1)
            for j in range(4):
                split(0, j, 1024)

            def evac_ada(name, tile0):
                def evac(i, j):
                    if j in (1, 3):
                        multiplied(name, i, j)
                        m = 4 * i + j - 1 + tile0
                        dve.tensor_tensor(mods[:, ds(m, 2), :], acc[:, j - 1:j + 1, 0:2],
                                          vec[:, ds(V_BADA + m, 2)].unsqueeze(-1).broadcast_to([P, 2, 2]),
                                          ALU.add).then_inc(acc_free[j // 2], 1)
                return evac

            pipeline("ada1", 1024, evac_ada("ada1", 0), MG)

            def norm_inv(n, width):
                dve.wait_ge(rms_ready, n + 1)
                link(dve.reciprocal(inv[:, 0:width], rms[:, 0:width]))

            dve.wait_ge(acc_free[0], USE["win0"])
            dve.wait_ge(acc_free[1], USE["win0"])
            for c in range(2):
                ins = dve.scalar_tensor_tensor(out=gmod[:, :, c], in0=mods[:, 8:16, c], scalar=1.0, in1=gains(N_PRE),
                                               op0=ALU.add, op1=ALU.mult)
            link(ins)
            norm_inv(0, 512)

            def pre_lower(n):
                k, c = divmod(n, 2)
                s = slice(T * c, T * c + T)
                dve.wait_ge(nh_ready, n + 1)
                dve.scalar_tensor_tensor(out=n5L[:, k, s], in0=sq5[:, k, s], scalar=mods[:, k, c:c + 1],
                                         in1=n5H[:, k, s].bitcast(F32), op0=ALU.add,
                                         op1=ALU.subtract).then_inc(nl_ready, 1)

            for n in range(2 * KD):
                k, c = divmod(n, 2)
                s = slice(T * c, T * c + T)
                dve.scalar_tensor_tensor(out=sq5[:, k, s], in0=R[:, k, META:TM] if c == 0 else ctxT[:, k, :],
                                         scalar=gmod[:, k, c:c + 1], in1=inv[:, s], op0=ALU.mult,
                                         op1=ALU.mult).then_inc(xn_ready, 1)
                if n >= 2:
                    pre_lower(n - 2)
            pre_lower(14)
            pre_lower(15)

            def evac_win0(i, j):
                if j == 1:
                    multiplied("win0", i, j)
                    dve.tensor_tensor(gt[:], acc[:, 0, 0:64].rearrange("p (t n) -> p t n", t=4),
                                      vec[:, V_BG:V_BG + 16].unsqueeze(1).broadcast_to([P, 4, 16]),
                                      ALU.add).then_inc(acc_free[0], 1)

            def evac_win1(i, j):
                if j == 3:
                    multiplied("win1", i, j)
                    dve.wait_ge(pads, 1)
                    for t in range(2):
                        ins = dve.tensor_copy(cink[:, t, :, 1:T + 1], acc[:, 2 + t, :].rearrange("p (s t) -> p s t", s=2))
                    ins.then_inc(acc_free[1], 1)

            def evac_win2(i, j):
                if j == 3:
                    multiplied("win2", i, j)
                    dve.tensor_copy(mvT[:, 2:4, :], acc[:, 2:4, :]).then_inc(acc_free[1], 1)

            def evac_win3(i, j):
                if j == 3:
                    multiplied("win3", i, j)
                    dve.tensor_scalar(qT[:, 2:4, :], acc[:, 2:4, 0:T], QS, None, ALU.mult).then_inc(acc_free[1], 1)

            pipeline("win0", 1024, evac_win0, K4)
            dve.wait_ge(gt_log, 1)
            for a in range(2):
                f = gt[:, :, 8 * a + 4:8 * a + 8]
                ins = dve.scalar_tensor_tensor(out=f, in0=f, scalar=0.0, in1=glog[:, :, a, :], op0=ALU.min,
                                               op1=ALU.subtract)
            ins.then_inc(lf_ready, 1)
            pipeline("ada2a", 1024, evac_ada("ada2a", 16), K4)
            pipeline("win1", 1024, evac_win1, K4)
            pipeline("ada2b", 1024, evac_ada("ada2b", 24), K4)
            pipeline("win2", 1024, evac_win2, K4)
            pipeline("ada2c", 1024, evac_ada("ada2c", 32), K4)
            pipeline("win3", 1024, evac_win3, K4)
            pipeline("ada2d", 1024, evac_ada("ada2d", 40), K4)
            for s in range(2):
                dve.wait_ge(acc_free[s], USE["win4"])
            dve.scalar_tensor_tensor(out=gmod[:, :, 2], in0=mods[:, 32:40, 0], scalar=1.0, in1=gains(N_PREF),
                                     op0=ALU.add, op1=ALU.mult)
            dve.tensor_tensor(gmod[:, :, 3], mods[:, 16:24, 0], gains(N_POST), ALU.mult)
            link(dve.tensor_tensor(gmod[:, :, 4], mods[:, 40:48, 0], gains(N_POSTF), ALU.mult))
            pipeline("win4", 1024, nothing, K4)

            dve.wait_ge(acc_free[0], USE["win1"] + 1)
            dve.wait_ge(acc_free[1], USE["win1"] + 1)
            for n in range(4):
                src, dst = (cink[:, n], mk[:, n, :].rearrange("p (s t) -> p s t", s=2)) if n < 2 else \
                    (cinq[:, n - 2:n - 1], mq[:, n - 2:n - 1, :])
                w = V_CONV + 3 * ((n + 2) % 4)
                link(dve.tensor_scalar(dst, src[:, :, 1:T + 1], col(w + 1), None, ALU.mult))
                link(dve.scalar_tensor_tensor(out=dst, in0=src[:, :, 0:T], scalar=col(w), in1=dst, op0=ALU.mult,
                                              op1=ALU.add))
                dve.scalar_tensor_tensor(out=dst, in0=src[:, :, 2:T + 2], scalar=col(w + 2), in1=dst, op0=ALU.mult,
                                         op1=ALU.add).then_inc(conv_ready, 1)

            X, C = slice(0, T), slice(T, 512)

            def timed(ap, d):
                return ap if d == 0 else ap[:, ::-1]

            dve.wait_ge(c1_in, 16)
            dve.wait_ge(cst_in, 16)
            dve.wait_ge(rows_ps, 1)
            for d in range(2):
                for s in (X, C):
                    ins = dve.tensor_tensor_scan(timed(bR[:, d, s], d), onerow[0:4, :], timed(wk[0:4, 2 * d + 1, s], d), 0.0,
                                                 ALU.mult, ALU.add)
            link(ins)
            for d in range(2):
                ins = dve.tensor_tensor(rR[:, d, :], wk[0:4, 2 * d, :], bR[:, d, :], ALU.subtract)
            link(ins)
            for d in range(2):
                ins = dve.tensor_tensor_scan(timed(MR[:, d, C], d), timed(rR[:, d, C], d), timed(rR[:, d, C], d), 0.0,
                                             ALU.max, ALU.max)
            link(ins)
            last = (511, T)
            for d in range(2):
                e = slice(last[d], last[d] + 1)
                ins = dve.tensor_tensor(m0[:, d:d + 1], bR[:, d, e], MR[:, d, e], ALU.add)
            link(ins)
            for d in range(2):
                e = slice(last[d], last[d] + 1)
                dve.tensor_tensor_scan(timed(MR[:, d, X], d), timed(rR[:, d, X], d), timed(rR[:, d, X], d), m0[:, d:d + 1],
                                       ALU.max, ALU.max)
                dve.tensor_scalar(D16[:, 4 * d:4 * d + 4], ident[0:4, 0:4], MR[:, d, e], None, ALU.mult)
                ins = dve.tensor_scalar(D16[:, 8 + 4 * d:12 + 4 * d], ident[0:4, 0:4], m0[:, d:d + 1], None, ALU.mult)
            link(ins)
            dve.tensor_tensor(bR[:, :, X], bR[:, :, X], MR[:, :, X], ALU.add).then_inc(rows_ready, 1)
            dve.wait_ge(cols_ps, 1)
            dve.tensor_copy(bc16[:], wk[:, 0, 32:48])
            link(dve.tensor_copy(rcol[:], wk[:, 0, 0:32].rearrange("p (t n) -> p t n", t=4)))
            dve.tensor_tensor(wkx[:], rcol[:, 2:4, :], bc16[:, 0:8].unsqueeze(1).broadcast_to([P, 2, 8]),
                              ALU.subtract).then_inc(wk_arg, 1)

            dve.wait_ge(rope_ps, 1)
            jobs = [(kT[:, X], kvraw[:, 0, X], acc[:, 0, X])]
            jobs += [(qT[:, t, :], qT[:, t, :], acc[:, (t + 1) // 2, X if t % 2 else C]) for t in range(4)]
            dve.tensor_copy(kT[:, C], kvraw[:, 0, C])
            for n, (dst, src, part) in enumerate(jobs):
                dve.tensor_tensor(t1[:, n % 2, :], part, sinT, ALU.mult)
                link(dve.tensor_tensor(dst, src, cosT, ALU.mult))
                ins = dve.tensor_tensor(dst, dst, t1[:, n % 2, :], ALU.add)
            ins.then_inc(rope_ready, 1)

            dve.wait_ge(wk_ready, 1)
            dve.wait_ge(ktok_ready, 1)
            for d in range(2):
                ins = dve.tensor_tensor(kw[:, d].rearrange("p t (h e) -> p t h e", h=4),
                                        ktok[:].rearrange("p t (h e) -> p t h e", h=4),
                                        wkx[:, :, 4 * d:4 * d + 4].unsqueeze(-1).broadcast_to([P, 2, 4, HD]), ALU.mult)
            ins.then_inc(kw_ready, 1)
            for n in range(4):
                dve.wait_ge(cst_ps, n + 1)
                b = CST_BANKS[n]
                dve.tensor_copy(Cst[0:64, n, 0:P], b[0:64, 0:P])
                dve.tensor_copy(Cst[64:128, n, 0:P], b[64:128, P:T])
                dve.tensor_copy(Cst[:, n, P:T], b[:, T:T + P]).then_inc(cst_ready, 1)

            def softmax_sum(n, sm):
                dve.wait_ge(p_exp, n + 1)
                c = slice(n, n + 1)
                link(dve.tensor_tensor(rinv[:, c], rsum[:, c], esink[:, c], ALU.add))
                link(dve.reciprocal(rinv[:, c], rinv[:, c]))
                dve.tensor_scalar(sm, sm, rinv[:, c], None, ALU.mult).then_inc(p_norm, 1)

            def heads_lower(n, hp):
                dve.wait_ge(oh_ready, n + 1)
                dve.tensor_tensor(mixL[:, hp, :], wk[:, 3, 0:T], mixH[:, hp, :].bitcast(F32),
                                  ALU.subtract).then_inc(ol_ready, 1)

            for u in range(18):
                if u < 16:
                    hp, b, par = UNITS[u]
                    h = 2 * hp + par
                    dve.wait_ge(s_ps, u + 1)
                    if u >= 2:
                        dve.wait_ge(pt_ps, u - 1)
                    dve.tensor_tensor_reduce(Sm[:, u % 2, :], wk[:, u % 2, :], winmask[:, b, :], 1.0, sinkn[:, h:h + 1],
                                             ALU.add, ALU.min, negm[:, u:u + 1]).then_inc(s_max, 1)
                if u >= 2 and (u - 2) % 4 == 3:
                    heads_lower((u - 2) // 4, (u - 2) // 4)
                if u % 2 == 1 and u >= 3:
                    v = u // 2 - 1
                    h, d, _ = order(v)
                    dve.wait_ge(nd_ps, v + 1)
                    link(dve.tensor_tensor(den1[:], acc[:, 2, T:512], emt[:, v % 2, :], ALU.max))
                    link(dve.scalar_tensor_tensor(out=den1[:], in0=acc[:, 2, T:512], scalar=-1.0, in1=den1[:],
                                                  op0=ALU.mult, op1=ALU.max))
                    link(dve.reciprocal(den1[:], den1[:]))
                    if d == 0:
                        dve.tensor_tensor(hT[:, h, :], acc[:, 2, 0:T], den1[:], ALU.mult).then_inc(nd_used, 1)
                    else:
                        dve.tensor_tensor(den1[:], acc[:, 2, 0:T], den1[:], ALU.mult).then_inc(nd_used, 1)
                        dve.wait_ge(nd_used, v + 1)
                        dve.tensor_tensor(hT[:, h, :], hT[:, h, :], den1[:], ALU.add).then_inc(hsum_ready, 1)
                if u % 2 == 1 and u < 16:
                    v = u // 2
                    h, d, (full, part, t0) = order(v)
                    c = 4 * d + h
                    dve.wait_ge(mw_ready, v + 1)
                    dve.scalar_tensor_tensor(out=zE[:, 0:T], in0=acc[:, 1, 0:T], scalar=rcol[:, full, c:c + 1],
                                             in1=ordf if d == 0 else ordb, op0=ALU.subtract, op1=ALU.max)
                    dve.scalar_tensor_tensor(out=zE[:, T:384], in0=acc[:, 1, t0:t0 + P], scalar=rcol[:, part, c:c + 1],
                                             in1=ordf[:, 0:P] if d == 0 else ordlow, op0=ALU.subtract,
                                             op1=ALU.max).then_inc(z_ready, 1)
                    if v >= 1:
                        dve.wait_ge(nd_ps, v)
                    dve.scalar_tensor_tensor(out=qw[lanes(h), :], in0=mq[lanes(h), h // 2, :], scalar=HD ** -0.5,
                                             in1=wint[lanes(h), :], op0=ALU.mult, op1=ALU.mult).then_inc(qw_ready, 1)
                if 1 <= u <= 16:
                    softmax_sum(u - 1, Sm[:, (u - 1) % 2, :])
                if u % 2 == 0 and 2 <= u <= 16:
                    v = u // 2 - 1
                    h, d, (full, part, t0) = order(v)
                    dve.wait_ge(e_ready, v + 1)
                    dve.wait_ge(ms_ps, h + 1)
                    dve.scalar_tensor_tensor(out=Aw[:, 0:T], in0=acc[:, 0, T * full:T * full + T], scalar=HD ** -0.5,
                                             in1=zE[:, 0:T], op0=ALU.mult, op1=ALU.mult)
                    dve.scalar_tensor_tensor(out=Aw[:, T:384], in0=acc[:, 0, T * part + t0:T * part + t0 + P],
                                             scalar=HD ** -0.5, in1=zE[:, T:384], op0=ALU.mult,
                                             op1=ALU.mult).then_inc(a_ready, 1)

            for hp in range(2):
                dve.wait_ge(hrms, hp + 1)
                link(dve.reciprocal(pT[:, hp, :], pT[:, hp, :]))
                for h in (2 * hp, 2 * hp + 1):
                    link(dve.scalar_tensor_tensor(out=hT[:, h, :], in0=hT[:, h, :], scalar=col(V_GML + h),
                                                  in1=pT[:, hp, T * (h % 2):T * (h % 2) + T], op0=ALU.mult, op1=ALU.mult))
                    dve.tensor_tensor(hT[:, h, :], hT[:, h, :], sgo[:, h, :], ALU.mult).then_inc(mlo_ready, 1)
            for h in range(4):
                dve.wait_ge(mlh_ready, h + 1)
                dve.tensor_tensor(mixL[:, 4 + h, :], hT[:, h, :], mixH[:, 4 + h, :].bitcast(F32),
                                  ALU.subtract).then_inc(mll_ready, 1)

            def post_norm(n, gain):
                norm_inv(n, T)
                for k in range(KD):
                    link(dve.scalar_tensor_tensor(out=Y[:, k, :], in0=Y[:, k, :], scalar=gmod[:, k, gain:gain + 1],
                                                  in1=inv[:, 0:T], op0=ALU.mult, op1=ALU.mult))
                    dve.tensor_tensor(R[:, k, META:TM], R[:, k, META:TM], Y[:, k, :], ALU.add).then_inc(r_ready, 1)

            def split_norm(n, first, width, t0, gain, shift):
                norm_inv(n, width)

                def lower(k):
                    dve.wait_ge(nh_ready, first + k + 1)
                    if shift is None:
                        ins = dve.tensor_tensor(nL[:, k, 0:width], sq[:, k, 0:width], nH[:, k, 0:width].bitcast(F32),
                                                ALU.subtract)
                    else:
                        ins = dve.scalar_tensor_tensor(out=nL[:, k, 0:width], in0=sq[:, k, 0:width],
                                                       scalar=mods[:, shift + k, 0:1], in1=nH[:, k, 0:width].bitcast(F32),
                                                       op0=ALU.add, op1=ALU.subtract)
                    ins.then_inc(nl_ready, 1)

                for k in range(KD):
                    dve.scalar_tensor_tensor(out=sq[:, k, 0:width], in0=R[:, k, t0:t0 + width], scalar=gain(k),
                                             in1=inv[:, 0:width], op0=ALU.mult, op1=ALU.mult).then_inc(xn_ready, 1)
                    if k >= 2:
                        lower(k - 2)
                lower(KD - 2)
                lower(KD - 1)

            def gate_up(name, f, width, ahead):
                def evac(i, j):
                    if j == 3:
                        multiplied(name, i, j)
                        dve.wait_ge(acc_free[0], USE[name] + i + 1)
                        dve.wait_ge(lo_ready, 4 * (BASE[name] + i) + 8)
                        dve.tensor_tensor(hbuf[:, :, 0:width], sg[:, :, 0:width], acc[:, 2:4, 0:width],
                                          ALU.mult).then_inc(acc_free[1], 1)
                        dve.wait_ge(gh_ready, COUNT[name] * f + i + 1)
                        dve.tensor_tensor(gL[:, ds(2 * i, 2), 0:width], hbuf[:, :, 0:width],
                                          gH[:, ds(2 * i, 2), 0:width].bitcast(F32), ALU.subtract).then_inc(gl_ready, 1)
                pipeline(name, 1024, evac, ahead)

            def evac_half(name, width, t0):
                def evac(i, j):
                    if j in (1, 3):
                        multiplied(name, i, j)
                        k = ds(2 * i + j // 2, 1)
                        dve.scalar_tensor_tensor(out=R[:, k, t0:t0 + width], in0=acc[:, j - 1:j, 0:width], scalar=0.5,
                                                 in1=R[:, k, t0:t0 + width], op0=ALU.mult,
                                                 op1=ALU.add).then_inc(acc_free[j // 2], 1)
                return evac

            pipeline("wout", 1024, nothing, K4)
            post_norm(1, 3)
            split_norm(2, 16, T, META, lambda k: gmod[:, k, 2:3], 24)
            gate_up("gu0", 0, T, DN)
            pipeline("dn0", SLOT, nothing, K4)
            post_norm(3, 4)
            split_norm(4, 24, TM, 0, lambda k: col(V_NORM + KD * N_F1 + k), None)
            gate_up("gu1", 1, TM, DN)
            pipeline("dn1", SLOT, evac_half("dn1", TM, 0), MG)
            dve.wait_ge(acc_free[1], USE["in2k"])
            split_norm(5, 32, TM, 0, lambda k: col(V_NORM + KD * N_MIX + k), None)
            for i in range(COUNT["in2k"]):
                for j in range(4):
                    split(BASE["in2k"] + i + 1, j, 1024)
            pipeline("in2g", 1024, nothing, K4)

            dve.wait_ge(z_abs, 1)
            for t in range(2):
                ins = dve.tensor_scalar(tB[:, t, :], wk[:, t, 0:TM], col(V_GB + t), 0.0, ALU.add, ALU.min)
            link(ins)
            dve.wait_ge(z_ln, 1)
            link(dve.tensor_tensor(tB[:], tB[:], tA[:], ALU.subtract))
            dve.wait_ge(c2_in, 48)
            for t in range(2):
                ins = dve.tensor_tensor_scan(tC[:, t, :], reset, tB[:, t, :], 0.0, ALU.mult, ALU.add)
            link(ins)
            dve.tensor_copy(blast[:], tC[:, :, META - 1:META + 192:64]).then_inc(b_ready, 1)
            dve.wait_ge(eb_ready, 1)
            dve.wait_ge(b_ready, 1)
            for t in range(2):
                dve.tensor_scalar(tC[:, t, 0:META], tC[:, t, 0:META], blast[:, t, 0:1], None, ALU.subtract)
                f = tC[:, t, META:META + 192].rearrange("p (c i) -> p c i", c=3)
                ins = dve.tensor_tensor(f, f, blast[:, t, 1:4].unsqueeze(-1).broadcast_to([P, 3, 64]), ALU.subtract)
            ins.then_inc(bl_ready, 1)
            dve.scalar_tensor_tensor(out=gqT[:], in0=gqT[:], scalar=HD ** -0.5, in1=tA[:, :, META:TM], op0=ALU.mult,
                                     op1=ALU.mult)
            dve.wait_ge(ed_ready, 1)
            dve.tensor_tensor(kdT[:, :, 0:208], gkT[:, :, 0:208], tC[:, :, 0:208], ALU.mult).then_inc(kd_ready, 1)
            dve.wait_ge(kd_ready, 1)
            dve.tensor_tensor(gkT[:], gkT[:], tB[:], ALU.mult).then_inc(qk_ready, 1)

            for u in range(18):
                if u < 16:
                    hp, b, par = UNITS[u]
                    h = 2 * hp + par
                    nk = META + P * (b + 1)
                    dve.wait_ge(s_ps, 16 + u + 1)
                    dve.wait_ge(bias_ready, h + 1)
                    if u >= 2:
                        dve.wait_ge(pt_ps, 16 + u - 1)
                    dve.tensor_tensor_reduce(Sm2[:, u % 2, 0:nk], wk[:, u % 2, 0:nk], bias2[:, h % 2, b, 0:nk], 1.0,
                                             sinkn[:, 8 + h:9 + h], ALU.add, ALU.min,
                                             negm[:, 16 + u:17 + u]).then_inc(s_max, 1)
                if u >= 2 and (u - 2) % 4 == 3:
                    heads_lower(4 + (u - 2) // 4, (u - 2) // 4)
                if 1 <= u <= 16:
                    softmax_sum(16 + u - 1, Sm2[:, (u - 1) % 2, 0:META + P * (UNITS[u - 1][1] + 1)])

            for c in range(4):
                dve.wait_ge(kv_ps, c + 1)
                for t in range(2):
                    for q in range(2):
                        s = slice(64 * q, 64 * q + 64)
                        new = acc[s, c, T * t + P * q:T * t + P * q + P]
                        if c == 0:
                            ins = dve.tensor_copy(St[s, 0, t, :], new)
                        else:
                            e = chunk(c)[1] - 1
                            ins = dve.scalar_tensor_tensor(out=St[s, c, t, :], in0=St[s, c - 1, t, :],
                                                           scalar=tA[s, t, e:e + 1], in1=new, op0=ALU.mult, op1=ALU.add)
                ins.then_inc(st_ready, 1)
                dve.wait_ge(st_ready, c + 1)
            dve.wait_ge(zero2, 1)
            for n in range(2):
                dve.wait_ge(at_ps, n + 1)
                dve.copy_predicated(attm[:, 2 * n:2 * n + 2].rearrange("p h c i -> p (h c) i"), causal[0:64],
                                    wk[0:64, n, :].rearrange("p (m i) -> p m i", m=8)).then_inc(at_ready, 1)
            grt = (tC, kdT)
            for n in range(2):
                dve.wait_ge(grms, n + 1)
                link(dve.reciprocal(grt[n][:, :, 0:T], grt[n][:, :, 0:T]))
                for i in (2 * n, 2 * n + 1):
                    link(dve.scalar_tensor_tensor(out=og[:, i, 0:T], in0=og[:, i, 0:T], scalar=col(V_GO),
                                                  in1=grt[n][:, i % 2, 0:T], op0=ALU.mult, op1=ALU.mult))
                    dve.tensor_tensor(og[:, i, 0:T], og[:, i, 0:T], grT[:, HEADS[i], :], ALU.mult).then_inc(yb_ready, 1)
            for n, h in enumerate(HEADS):
                dve.wait_ge(ybh_ready, n + 1)
                dve.tensor_tensor(mixL[:, 4 + h, :], og[:, n, 0:T], mixH[:, 4 + h, :].bitcast(F32),
                                  ALU.subtract).then_inc(ybl_ready, 1)

            def evac_bra(i, j):
                s = 2 * (j % 2)
                multiplied("bra", i, j)
                dve.tensor_tensor(gab[:, 2 * j:2 * j + 2, :], gab[:, 2 * j:2 * j + 2, :], acc[:, s:s + 2, 0:T],
                                  ALU.mult).then_inc(acc_free[j % 2], 1)

            def evac_brb(i, j):
                s = 2 * (j % 2)
                a, b = gab[:, 2 * j:2 * j + 2, :], gab[:, KD + 2 * j:KD + 2 * j + 2, :]
                multiplied("brb", i, j)
                dve.tensor_tensor(b, b, acc[:, s:s + 2, 0:T], ALU.mult).then_inc(acc_free[j % 2], 1)
                dve.wait_ge(acc_free[j % 2], USE["brb"] + j // 2 + 1)
                dve.tensor_tensor(a, a, b, ALU.add).then_inc(mx_sum, 1)
                dve.wait_ge(mxh_ready, j + 1)
                dve.tensor_tensor(nL[:, 2 * j:2 * j + 2, 0:T], a, nH[:, 2 * j:2 * j + 2, 0:T].bitcast(F32),
                                  ALU.subtract).then_inc(mxl_ready, 1)

            pipeline("bra", 1024, evac_bra, K4)
            pipeline("brb", 1024, evac_brb, K4)

            def evac_wout2(i, j):
                if j in (1, 3):
                    multiplied("wout2", i, j)
                    k = ds(4 * i + j - 1, 2)
                    dve.tensor_tensor(R[:, k, META:TM], R[:, k, META:TM], acc[:, j - 1:j + 1, 0:T],
                                      ALU.add).then_inc(acc_free[j // 2], 1)

            pipeline("wout2", 1024, evac_wout2, K4)
            dve.wait_ge(acc_free[1], USE["gu2"])
            split_norm(6, 40, T, META, lambda k: col(V_NORM + KD * N_F2 + k), None)
            gate_up("gu2", 2, T, DN)
            pipeline("dn2", SLOT, evac_half("dn2", T, META), None)

            norm_inv(7, T)
            for k in range(KD):
                dve.scalar_tensor_tensor(out=Y[:, k, :], in0=R[:, k, META:TM], scalar=col(V_NORM + KD * N_FIN + k),
                                         in1=inv[:, 0:T], op0=ALU.mult, op1=ALU.mult).then_inc(out_ready, 1)

        @block.tensor
        def _(pe):
            def split_mm(out_, wH, wL, xH, xL, start, stop):
                pe.matmul(out_, wH, xH, start=start, stop=False)
                pe.matmul(out_, wH, xL, start=False, stop=False)
                return pe.matmul(out_, wL, xH, start=False, stop=stop)

            def set_free(s, use):
                if not (isinstance(use, int) and use == 0):
                    pe.wait_ge(acc_free[s], use)

            def arrived(g, j):
                pe.wait_ge(lo_ready, 4 * g + j + 1)

            def pair(g, use, s, xH, xL, n, ready=None):
                set_free(s, use)
                for q in range(2):
                    j = 2 * s + q
                    arrived(g, j)
                    if ready:
                        pe.wait_ge(ready[0], ready[1] + ready[2] * (q + 1))
                    for kk in range(4):
                        k = 4 * q + kk
                        for m in range(2):
                            w = slice(256 * kk + P * m, 256 * kk + P * m + P)
                            ins = split_mm(acc[:, 2 * s + m, 0:n], hi[:, j, w], lo[:, j, w], xH(k), xL(k),
                                           k == 0, k == KD - 1)
                    ins.then_inc(mm_done, 1)

            def pairs(name, xs, n, ready=None):
                with pe.Fori(0, COUNT[name]) as i:
                    for s in range(2):
                        pair(BASE[name] + i, USE[name] + i, s, *xs, n, ready)

            def sum_squares(n, src, width, waits):
                for w in waits:
                    pe.wait_ge(*w)
                for k in range(KD):
                    ins = pe.matmul(wk[:, 0, 0:width], ones, src[:, k, 0:width], start=k == 0, stop=k == KD - 1)
                ins.then_inc(ssq_ps, 1)

            pe.wait_ge(cst_in, 16)
            pe.wait_ge(c_lo, 1)
            cond = (lambda k: cH[:, 2 * k:2 * k + 2], lambda k: cL[:, 2 * k:2 * k + 2])
            for s in range(2):
                pair(0, 0, s, *cond, 2)
            sum_squares(0, sq5, 512, [(sq_ready, 8)])
            with pe.Fori(1, COUNT["ada1"]) as i:
                for s in range(2):
                    pair(i, i, s, *cond, 2)

            both = (lambda k: n5H[:, k, :], lambda k: n5L[:, k, :])
            frames = (lambda k: n5H[:, k, 0:T], lambda k: n5L[:, k, 0:T])
            g = BASE["win0"]
            set_free(0, USE["win0"])
            arrived(g, 1)
            pe.wait_ge(nl_ready, 16)
            for t in range(4):
                for k in range(KD):
                    j, c = k // 4, slice(16 * (k % 4), 16 * (k % 4) + 16)
                    xs = slice(P * t, P * t + P)
                    ins = split_mm(acc[:, 0, 16 * t:16 * t + 16], n5H[:, k, xs], n5L[:, k, xs], hi[:, j, c], lo[:, j, c],
                                   k == 0, k == KD - 1)
                    if t == 3 and k % 4 == 3:
                        ins.then_inc(mm_done, 1)
            pair(g, USE["win0"], 1, *both, 512)
            for n, (xs, width) in enumerate(((both, 512), (both, 512), (frames, T), (frames, T))):
                pairs("ada2" + "abcd"[n], cond, 2)
                for s in range(2):
                    pair(BASE[f"win{n + 1}"], USE[f"win{n + 1}"], s, *xs, width)

            pe.wait_ge(lf_ready, 1)
            for q in range(4):
                for t in range(4):
                    ins = pe.transpose(wk[0:4, q, P * t:P * t + P], gt[:, t, 4 * q:4 * q + 4], ident)
            ins.then_inc(rows_ps, 1)
            pe.wait_ge(c1_in, 16)
            for s in range(2):
                pe.wait_ge(acc_free[s], USE["wout"])
            pe.matmul(acc[:, 0, 0:T], perm, kvraw[:, 0, 0:T], start=True, stop=True)
            for t in range(4):
                ins = pe.matmul(acc[:, (t + 1) // 2, T * ((t + 1) % 2):T * ((t + 1) % 2) + T], perm, qT[:, t, :],
                                start=True, stop=True)
            ins.then_inc(rope_ps, 1)
            for t in range(4):
                ins = pe.transpose(acc[:, 3, P * t:P * t + P], kvraw[:, 1, P * t:P * t + P], ident)
            ins.then_inc(avt_ps, 1)
            pe.wait_ge(rows_ready, 1)
            for t in range(4):
                for d in range(2):
                    pe.transpose(wk[:, 0, 8 * t + 4 * d:8 * t + 4 * d + 4], rR[:, d, P * t:P * t + P], ident[0:4, 0:4])
            pe.matmul(wk[:, 0, 32:48], ones[0:4, :], D16[:], start=True, stop=True).then_inc(cols_ps, 1)
            for t in (2, 3, 0, 1):
                if t == 1:
                    pe.wait_ge(rope_ready, 1)
                for h in range(4):
                    ins = pe.transpose(MV_BANKS[t][:, P * h:P * h + P], mvT[:, h, P * t:P * t + P], ident)
                ins.then_inc(mvt_ps, 1)
            pe.wait_ge(mqk_ready, 2)
            for t in range(2):
                for n in range(2):
                    ins = pe.transpose(acc[:, 0, T * t + P * n:T * t + P * n + P], mk[:, n, T + P * t:T + P * t + P], ident)
            ins.then_inc(kt_ps, 1)
            pe.matmul(acc[:, 2, :], swap, kT[:], start=True, stop=True).then_inc(ks_ps, 1)
            pe.wait_ge(kw_ready, 1)
            pe.wait_ge(vtok_ready, 4)
            pe.wait_ge(avz_ready, 1)
            for n in range(4):
                d, hp = divmod(n, 2)
                for part in range(2):
                    for t in range(2):
                        lhs = kw[:, d, t, P * hp:P * hp + P]
                        if part == 0:
                            pe.matmul(CST_BANKS[n][:, 0:T], lhs, vtok[:, 2 + t, T * hp:T * hp + T], start=t == 0, stop=t == 1)
                        else:
                            ins = pe.matmul(CST_BANKS[n][:, T:T + P], lhs, ones, start=t == 0, stop=t == 1)
                ins.then_inc(cst_ps, 1)

            def transposed_out(n, u, par, b, keys, first, last):
                for i, (v, p) in enumerate(keys):
                    ins = pe.matmul(wk[:, 3, P * b:P * b + P], v, p, start=par == 0 and i == 0,
                                    stop=par == 1 and i == len(keys) - 1)
                if b == 1 and par == 1:
                    ins.then_inc(o_ps, 1)

            pe.wait_ge(cst_ready, 4)
            pe.wait_ge(ks_ready, 1)
            pe.wait_ge(mqk_ready, 4)
            for u in range(17):
                if u < 16:
                    hp, b, par = UNITS[u]
                    h = 2 * hp + par
                    keys = kT if h // 4 == h % 2 else kTs
                    if u >= 2:
                        pe.wait_ge(s_max, u - 1)
                    pe.matmul(wk[:, u % 2, :], qT[lanes(h), hp, P * b:P * b + P], keys[lanes(h), :],
                              start=True, stop=True).then_inc(s_ps, 1)
                if u % 2 == 1:
                    v = u // 2
                    h, d, _ = order(v)
                    if d == 0:
                        if v >= 1:
                            pe.wait_ge(a_ready, v)
                        for s in range(2):
                            ins = pe.matmul(acc[:, 0, T * s:T * s + T], mk[lanes(h), h // 2, P * s:P * s + P],
                                            mq[lanes(h), h // 2, :], start=True, stop=True)
                        ins.then_inc(ms_ps, 1)
                    if v >= 1:
                        pe.wait_ge(z_ready, v)
                    pe.matmul(acc[:, 1, 0:T], sel4[0:4, h, :], MR[:, d, 0:T], start=True, stop=True)
                    pe.matmul(acc[:, 1, T:512], sel4[0:4, h, :], bR[:, d, 0:T], start=True, stop=True).then_inc(mb_ps, 1)
                if u >= 1:
                    hp, b, par = UNITS[u - 1]
                    pe.wait_ge(p_norm, u)
                    if u >= 2:
                        pe.wait_ge(pt_ready, u - 1)
                    for t in range(4):
                        ins = pe.transpose(wk[:, 2, P * t:P * t + P], Sm[:, (u - 1) % 2, P * t:P * t + P], ident)
                    ins.then_inc(pt_ps, 1)
                if u % 2 == 0 and u >= 2:
                    v = u // 2 - 1
                    h, d, (full, part, t0) = order(v)
                    pe.wait_ge(a_ready, v + 1)
                    pe.wait_ge(qw_ready, v + 1)
                    if v >= 1:
                        pe.wait_ge(nd_used, v)
                    for o, lhs in ((0, lambda s: vtok[:, s, P * h:P * h + P]), (T, lambda s: ones)):
                        pe.matmul(acc[:, 2, o:o + T], lhs(full), Aw[:, 0:T], start=True, stop=False)
                        pe.matmul(acc[:, 2, o + t0:o + t0 + P], lhs(part), Aw[:, T:384], start=False, stop=False)
                        ins = pe.matmul(acc[:, 2, o:o + T], Cst[lanes(h), 2 * d + h // 2, o // 2:o // 2 + P],
                                        qw[lanes(h), :], start=False, stop=True)
                    ins.then_inc(nd_ps, 1)
                if u >= 1:
                    pe.wait_ge(pt_ready, u)
                    if b == 0 and par == 0 and hp >= 1:
                        pe.wait_ge(ol_ready, hp)
                    g4 = (2 * hp + par) // 4
                    vs = slice(64, 192) if par == 0 else slice(0, P)
                    transposed_out(hp, u, par, b, [(avz[:, t, g4, vs], pT[:, (u - 1) % 2, P * t:P * t + P])
                                                   for t in range(4)], 0, 0)

            for hp in range(2):
                pe.wait_ge(hsq_ready, hp + 1)
                pe.matmul(acc[:, 1 + 2 * hp, :], ones, Sm[:, hp, :], start=True, stop=True).then_inc(hss_ps, 1)

            def gate_up(name, first, t0, width):
                xs = (lambda k: nH[:, k, t0:t0 + width], lambda k: nL[:, k, t0:t0 + width])
                pairs(name, xs, width, (nl_ready, first, 4))

            def down(name, f, width):
                with pe.Fori(0, COUNT[name]) as i:
                    for j in range(4):
                        s = j // 2
                        if j % 2 == 0:
                            set_free(s, USE[name] + i)
                        arrived(BASE[name] + i, j)
                        pe.wait_ge(gl_ready, 11 * f + (6 if j % 2 == 0 else 11))
                        for kk in range(HALF):
                            k = HALF * (j % 2) + kk
                            w = slice(P * kk, P * kk + P)
                            ins = split_mm(acc[:, 2 * s, 0:width], hi[:, j, w], lo[:, j, w], gH[:, k, 0:width],
                                           gL[:, k, 0:width], k == 0, k == KH - 1)
                        ins.then_inc(mm_done, 1)

            pe.wait_ge(ol_ready, 4)
            pe.wait_ge(mll_ready, 4)
            mixed = (lambda k: mixH[:, k, :], lambda k: mixL[:, k, :])
            pairs("wout", mixed, T)
            sum_squares(1, sq, T, [(acc_free[s], USE["gu0"]) for s in range(2)])
            sum_squares(2, sq, T, [(sq_ready, 16)])
            gate_up("gu0", 16, 0, T)
            down("dn0", 0, T)
            sum_squares(3, sq, T, [(acc_free[s], USE["gu1"]) for s in range(2)])
            sum_squares(4, sq, TM, [(sq_ready, 24)])
            gate_up("gu1", 24, 0, TM)
            down("dn1", 1, TM)
            sum_squares(5, sq, TM, [(sq_ready, 32)])

            allT = (lambda k: nH[:, k, :], lambda k: nL[:, k, :])
            frames = (lambda k: nH[:, k, META:TM], lambda k: nL[:, k, META:TM])
            g = BASE["in2k"]
            set_free(0, USE["in2k"])
            for q in range(2):
                arrived(g, q)
                pe.wait_ge(nl_ready, 32 + 4 * (q + 1))
                for kk in range(4):
                    k, w = 4 * q + kk, slice(16 * kk, 16 * kk + 16)
                    ins = split_mm(acc[0:16, 0, 0:TM], hi[:, q, w], lo[:, q, w], nH[:, k, :], nL[:, k, :], k == 0, k == KD - 1)
                ins.then_inc(mm_done, 1)
            pair(g, USE["in2k"], 1, *allT, TM)
            for n, (a, b) in enumerate(((allT, frames), (allT, allT), (frames, frames), (frames, frames))):
                for s, xs in enumerate((a, b)):
                    pair(g + 1 + n, USE["in2k"] + 1 + n, s, *xs, TM if xs is allT else T)
            pairs("in2g", frames, T)

            pe.wait_ge(c2_in, 48)
            for s in range(2):
                pe.wait_ge(acc_free[s], USE["bra"])
            for t in range(2):
                ins = pe.matmul(wk[:, t, 0:TM], gatew[:, P * t:P * t + P], glT[:], start=True, stop=True)
            ins.then_inc(z_ps, 1)
            pe.transpose(acc[0:META, 0, 0:P], kvraw2[:, 1, 0:META], ident)
            for t in range(2):
                ins = pe.transpose(acc[:, 0, P + P * t:2 * P + P * t], kvraw2[:, 1, META + P * t:META + P * t + P], ident)
            ins.then_inc(av2_ps, 1)
            pe.matmul(acc[:, 1, 0:TM], swap, kvraw2[:, 0, :], start=True, stop=True).then_inc(ks2_ps, 1)
            for c in range(5):
                a, e = chunk(c)
                if c == 4:
                    pe.wait_ge(gvt_ready, 1)
                for h in range(4):
                    ins = pe.transpose(GV_BANKS[c][0:e - a, P * h:P * h + P], gvT[:, h, a:e], ident)
                ins.then_inc(gvt_ps, 1)

            pe.wait_ge(eb_ready, 1)
            pe.wait_ge(ks2_ready, 1)
            pe.wait_ge(av2_ready, 1)
            pe.wait_ge(gvt_ready, 5)
            for u in range(17):
                if u < 16:
                    hp, b, par = UNITS[u]
                    h = 2 * hp + par
                    keys = kvraw2[:, 0, :] if h // 4 == h % 2 else kS2
                    nk = META + P * (b + 1)
                    if u >= 2:
                        pe.wait_ge(s_max, 16 + u - 1)
                    pe.matmul(wk[:, u % 2, 0:nk], qT2[lanes(h), hp, P * b:P * b + P], keys[lanes(h), 0:nk],
                              start=True, stop=True).then_inc(s_ps, 1)
                if u >= 1:
                    hp, b, par = UNITS[u - 1]
                    sm, pt = Sm2[:, (u - 1) % 2, :], pT2[:, (u - 1) % 2, :]
                    pe.wait_ge(p_norm, 16 + u)
                    if u >= 2:
                        pe.wait_ge(pt_ready, 16 + u - 1)
                    pe.transpose(wk[0:META, 2, 0:P], sm[:, 0:META], ident)
                    for t in range(b + 1):
                        ins = pe.transpose(wk[:, 2, P + P * t:2 * P + P * t], sm[:, META + P * t:META + P * t + P], ident)
                    ins.then_inc(pt_ps, 1)
                    pe.wait_ge(pt_ready, 16 + u)
                    if b == 0 and par == 0 and hp >= 1:
                        pe.wait_ge(ol_ready, 4 + hp)
                    g4 = (2 * hp + par) // 4
                    vs = slice(64, 192) if par == 0 else slice(0, P)
                    keys = [(avz2[0:META, 0, g4, vs], pt[0:META, 0:P])]
                    keys += [(avz2[:, 1 + t, g4, vs], pt[:, P + P * t:2 * P + P * t]) for t in range(b + 1)]
                    transposed_out(hp, u, par, b, keys, 0, 0)

            pe.wait_ge(kd_ready, 1)
            for c in range(4):
                a, e = chunk(c)
                for t in range(2):
                    o = T * (c % 2) + P * t
                    ins = pe.transpose(wk[0:e - a, c // 2, o:o + P], kdT[:, t, a:e], ident)
                if c % 2:
                    ins.then_inc(kdt_ps, 1)
            for c in range(4):
                n = chunk(c)[1] - chunk(c)[0]
                pe.wait_ge(kdt_ready, c // 2 + 1)
                for t in range(2):
                    ins = pe.matmul(acc[:, c, T * t:T * t + T], kdtok[0:n, c, P * t:P * t + P],
                                    gvtok[0:n, c, T * t:T * t + T], start=True, stop=True)
                ins.then_inc(kv_ps, 1)
            pe.wait_ge(qk_ready, 1)
            for n, h in enumerate(HEADS):
                for c in range(4):
                    a, e = chunk(c + 1)
                    o = T * (n % 2) + 64 * c
                    ins = pe.matmul(wk[0:64, n // 2, o:o + 64], gkT[lanes(h), h // 2, a:e],
                                    gqT[lanes(h), h // 2, 64 * c:64 * c + 64], start=True, stop=True)
                if n % 2:
                    ins.then_inc(at_ps, 1)
            fences = 0

            def fence(h, ins):
                nonlocal fences
                if h % 2:
                    fences += 1
                    ins.then_inc(rows_done, 1)
                    pe.wait_ge(rows_done, fences)

            pe.wait_ge(st_ready, 4)
            for bank in range(2):
                pe.wait_ge(at_ready, bank + 1)
                for n in (2 * bank, 2 * bank + 1):
                    h = HEADS[n]
                    for c in range(4):
                        o = acc[:, bank, T * (n % 2) + 64 * c:T * (n % 2) + 64 * c + 64]
                        fence(h, pe.matmul(o, gvtok[:, c + 1, P * h:P * h + P], attm[:, n, c, :], start=True, stop=False))
                        ins = pe.matmul(o, St[lanes(h), c, h // 2, :], gqT[lanes(h), h // 2, 64 * c:64 * c + 64],
                                        start=False, stop=True)
                        if (n, c) in ((1, 3), (3, 3)):
                            ins.then_inc(go_ps, 1)
                        else:
                            fence(h, ins)
            for n, src in enumerate((tA, tB)):
                pe.wait_ge(go_ready, n + 1)
                pe.matmul(acc[:, 2 + n, :], ones, src[:, :, 0:T], start=True, stop=True).then_inc(gss_ps, 1)

            pe.wait_ge(ol_ready, 8)
            for name, k0 in (("bra", 0), ("brb", 4)):
                if k0:
                    pe.wait_ge(ybl_ready, 4)
                for j in range(4):
                    s = j % 2
                    set_free(s, USE[name] + j // 2)
                    if name == "bra" and j == 0:
                        pe.wait_ge(grms, 2)
                    arrived(BASE[name], j)
                    for kk in range(4):
                        for m in range(2):
                            w = slice(256 * kk + P * m, 256 * kk + P * m + P)
                            ins = split_mm(acc[:, 2 * s + m, 0:T], hi[:, j, w], lo[:, j, w], mixH[:, k0 + kk, :],
                                           mixL[:, k0 + kk, :], kk == 0, kk == 3)
                    ins.then_inc(mm_done, 1)
            pairs("wout2", (lambda k: nH[:, k, 0:T], lambda k: nL[:, k, 0:T]), T, (mxl_ready, 0, 2))
            sum_squares(6, sq, T, [(sq_ready, 36)])
            gate_up("gu2", 40, 0, T)
            down("dn2", 2, T)
            sum_squares(7, sq, T, [(sq_ready, 44)])


_WEIGHTS = ["w_ada", "w_in", "w_out", "w_ffn_in", "w_ffn_out", "ffn1_w_gate_2", "ffn1_w_up_2", "ffn1_w_down_2", "w_in_2",
            "gla_gate_w_2", "w_branch_att_2", "w_branch_gla_2", "w_out_2", "ffn2_w_gate_2", "ffn2_w_up_2", "ffn2_w_down_2"]


def kernel(**inputs):
    import numpy as _np
    import concourse.bacc as _bacc
    from concourse import mybir as _mybir
    from concourse.bass_utils import run_bass_kernel_spmd as _run

    a = {n: _np.asarray(v) for n, v in inputs.items()}

    def cols(v):
        return v.reshape(-1, P).T

    def tokens(x):
        return x.reshape(-1, KD, P).transpose(2, 1, 0)

    def every(v):
        return _np.broadcast_to(v.reshape(1, -1), (P, v.size))

    norms = ("g_pre_mix", "g_post_mix", "g_pre_ffn", "g_post_ffn", "ffn1_norm_2", "mix_norm_2", "ffn2_norm_2", "final_norm_2")
    parts = [_np.stack([cols(a["c"]), cols(a["c_ctx"])], -1).reshape(P, -1), cols(a["b_ada"])]
    parts += [cols(a[n]) for n in norms]
    parts += [a["w_conv_qk"][0].T.reshape(4, P, 3).transpose(1, 0, 2).reshape(P, -1), cols(a["g_mlstm_out"])]
    parts += [cols(a["gla_gate_b_2"]), cols(a["gla_out_norm_2"])]
    parts += [every(a["attn_sink"]), every(a["att_sinks_2"]), every(a["b_gates"])]
    host = {"vecs": _np.concatenate(parts, 1)}
    host["hT"] = tokens(_np.concatenate([a["meta_tokens_2"], a["x"][0]], 0))
    host["ctxT"] = tokens(a["ctx"][0])
    host["cst"], host["c1"], host["c2"], host["causal"] = shape_constants()
    for n in _WEIGHTS:
        host[n] = a[n][0]

    nc = _bacc.Bacc("TRN2", target_bir_lowering=False, num_devices=1)
    arrays, dr = {}, {}
    for n, v in host.items():
        v = _np.ascontiguousarray(v)
        arrays[f"in_{n}"] = v
        dr[n] = nc.dram_tensor(f"in_{n}", v.shape, _mybir.dt.from_np(v.dtype), kind="ExternalInput").ap()
    out = nc.dram_tensor("out_0", (P, KD, T), _mybir.dt.float32, kind="ExternalOutput").ap()
    program(nc, dr, out)
    r = _run(nc, [arrays], core_ids=[0])
    y = r.results[0]["out_0"]
    return _np.ascontiguousarray(y.transpose(2, 1, 0)).reshape(1, T, D)
```

```python
from contextlib import ExitStack

import numpy as np
import concourse.bass as bass
from concourse import mybir

F32 = mybir.dt.float32
F32R = mybir.dt.float32r
U32 = mybir.dt.uint32
ACT = mybir.ActivationFunctionType
ALU = mybir.AluOpType
ds = bass.ds

P = 128
D = 1024
KD = D // P
T = 256
L = 256
META = 16
TM = META + T
HID = 2816
KH = HID // P
EPS = 1e-6
BIG = 1e30
HD = 64
NHEAD = 8
HALF = KH // 2
SLOT = HALF * P
RING = 4
QS = -(HD ** -0.5)

V_C, V_BADA, V_NORM, V_CONV, V_GML, V_GB, V_GO = 0, 16, 64, 128, 140, 144, 146
V_SINK1, V_SINK2, V_BG, NV = 147, 155, 163, 164
N_PRE, N_POST, N_PREF, N_POSTF, N_F1, N_MIX, N_F2, N_FIN = range(8)

PHASES = [("ada1", 4), ("win0", 1), ("win1", 1), ("win2", 1), ("win3", 1), ("win4", 1), ("ada2", 8), ("wout", 2),
          ("gu0", 11), ("dn0", 4), ("gu1", 11), ("dn1", 4), ("in2k", 5), ("in2g", 4), ("bra", 1), ("brb", 1),
          ("wout2", 2), ("gu2", 11), ("dn2", 4)]
ADA = ("ada1", "ada2")
COUNT = dict(PHASES)
BASE, USE = {}, {}
RING_AT, BEFORE = {}, {}
_its, _use, _ring, _last = {True: 0, False: 0}, 0, 0, None
for _name, _n in PHASES:
    BASE[_name], USE[_name] = _its[_name in ADA], _use
    RING_AT[_name], BEFORE[_name] = _ring, _last
    _its[_name in ADA] += _n
    _ring += _n
    _last = _name
    if _name not in ADA:
        _use += _n * (2 if _name in ("bra", "brb") else 1)


def ring_lead(g):
    name = [n for n, _ in PHASES if n not in ADA and BASE[n] <= g][-1]
    return RING_AT[name] - BASE[name]


def shape_constants():
    f = np.float32
    p = np.arange(P)
    ident = np.eye(P, dtype=f)
    ones = np.ones((P, P), f)
    perm = np.zeros((P, P), f)
    for d in range(P):
        if d % 32 < 16:
            perm[d + 16, d] = -1.0
        else:
            perm[d - 16, d] = 1.0
    swap = np.zeros((P, P), f)
    swap[p, (p + HD) % P] = 1.0
    tok = np.arange(T)
    inv_freq = np.power(f(10000.0), -np.arange(16, dtype=f) / f(16)).astype(f)
    pos = np.where((p % HD < 32)[:, None], (tok // 64)[None, :], (tok % 64)[None, :]).astype(f)
    ang = (pos * inv_freq[p % 16][:, None]).astype(f)
    win = np.zeros((P, 2, 512), f)
    for b in range(2):
        q = b * P + p
        win[:, b, 0:T] = np.where(np.abs(q[:, None] - tok[None, :]) <= 128, 0.0, BIG)
    up = np.where(p[:, None] <= p[None, :], 0.0, BIG).astype(f)
    low = np.where(p[:, None] >= p[None, :], 0.0, BIG).astype(f)
    zero = np.zeros((P, P), f)
    ordf = np.concatenate([up, zero], 1)
    ordb = np.concatenate([zero, low], 1)
    sel = np.zeros((P, 4, P), f)
    for h in range(4):
        sel[h, h, :] = 1.0
    one_row = np.ones((P, 256), f)
    first = [a.reshape(P, -1) for a in (perm, np.cos(ang), np.sin(ang), win, ordf, ordb, low, sel, one_row)]
    dist = np.full((P, 2, TM), BIG, f)
    for b in range(2):
        q = b * P + p
        dist[:, b, 0:META] = 0.0
        gap = (q // 64)[:, None] - (tok // 64)[None, :]
        dist[:, b, META:] = np.where((gap >= 0) & (gap <= 2), np.abs(q[:, None] - tok[None, :]), BIG)
    reset = np.ones((P, TM), f)
    reset[:, [0] + [META + 64 * c for c in range(4)]] = 0.0
    second = [a.reshape(P, -1) for a in (dist, reset)]
    causal = np.zeros((P, 8, 64), np.uint32)
    causal[0:64] = (np.arange(64)[:, None] <= np.arange(64)[None, :])[:, None, :]
    cat = lambda xs: np.ascontiguousarray(np.concatenate(xs, 1).astype(f))
    return cat([ident, ones, swap]), cat(first), cat(second), causal


def program(nc, dr, out):
    with ExitStack() as root:
        def sbuf(stack, name, shape, dt=F32):
            return stack.enter_context(nc.sbuf_tensor(name, shape, dt))

        def sem(name):
            return root.enter_context(nc.semaphore(name))

        cst = sbuf(root, "cst", [P, 3 * P])
        ident, ones, swap = cst[:, 0:P], cst[:, P:2 * P], cst[:, 2 * P:3 * P]
        vec = sbuf(root, "vec", [P, NV])
        mods = sbuf(root, "mods", [P, 48, 2])
        gmod = sbuf(root, "gmod", [P, KD, 5])
        silu_c = sbuf(root, "silu_c", [P, 16])
        warm = sbuf(root, "warm", [1, 8])
        R = sbuf(root, "R", [P, KD, TM])
        raw = sbuf(root, "raw", [P, RING, SLOT])
        hi = sbuf(root, "hi", [P, RING, SLOT], F32R)
        lo = sbuf(root, "lo", [P, RING, SLOT], F32R)
        mixH = sbuf(root, "mixH", [P, KD, T], F32R)
        mixL = sbuf(root, "mixL", [P, KD, T], F32R)
        inv = sbuf(root, "inv", [P, 512])
        rms = sbuf(root, "rms", [P, 512])
        sinkn = sbuf(root, "sinkn", [P, 16])
        negm = sbuf(root, "negm", [P, 32])
        rsum = sbuf(root, "rsum", [P, 32])
        esink = sbuf(root, "esink", [P, 32])
        rinv = sbuf(root, "rinv", [P, 32])

        blk1 = ExitStack()
        c1 = sbuf(blk1, "c1", [P, 3072])
        o = 0
        def c1_take(n):
            nonlocal o
            o += n
            return c1[:, o - n:o]
        perm, cosT, sinT = c1_take(P), c1_take(T), c1_take(T)
        winmask = c1_take(1024).rearrange("p (b k) -> p b k", b=2)
        ordf, ordb, ordlow = c1_take(256), c1_take(256), c1_take(P)
        sel4 = c1_take(512).rearrange("p (h m) -> p h m", h=4)
        onerow = c1_take(256)
        kvraw = sbuf(blk1, "kvraw", [P, 2, 512])
        cinq = sbuf(blk1, "cinq", [P, 2, T + 2])
        cink = sbuf(blk1, "cink", [P, 2, 2, T + 2])
        mvT = sbuf(blk1, "mvT", [P, 4, 512])
        qT = sbuf(blk1, "qT", [P, 4, T])
        sgo = sbuf(blk1, "sgo", [P, 4, T])
        gt = sbuf(blk1, "gt", [16, 512])
        glog = sbuf(blk1, "glog", [16, 512])
        nrm1 = ExitStack()
        n5H = sbuf(nrm1, "n5H", [P, KD, 512], F32R)
        n5L = sbuf(nrm1, "n5L", [P, KD, 512], F32R)
        sq5 = sbuf(nrm1, "sq5", [P, KD, 512])
        ctxT = sbuf(nrm1, "ctxT", [P, KD, L])
        nrm1.close()
        mx1 = ExitStack()
        mq = sbuf(mx1, "mq", [P, 2, T])
        mk = sbuf(mx1, "mk", [P, 2, 512])
        kT = sbuf(mx1, "kT", [P, 512])
        kTs = sbuf(mx1, "kTs", [P, 512])
        avz = sbuf(mx1, "avz", [P, 4, 2, 192])
        vtok = sbuf(mx1, "vtok", [P, 4, 512])
        ktok = sbuf(mx1, "ktok", [P, 2, T])
        kw = sbuf(mx1, "kw", [P, 2, 2, T])
        Cst = sbuf(mx1, "Cst", [P, 4, 256])
        bR = sbuf(mx1, "bR", [4, 2, 512])
        rR = sbuf(mx1, "rR", [4, 2, 512])
        MR = sbuf(mx1, "MR", [4, 2, 512])
        m0 = sbuf(mx1, "m0", [4, 2])
        D16 = sbuf(mx1, "D16", [4, 16])
        rcol = sbuf(mx1, "rcol", [P, 4, 8])
        bc16 = sbuf(mx1, "bc16", [P, 16])
        wkx = sbuf(mx1, "wkx", [P, 2, 8])
        Sm = sbuf(mx1, "Sm", [P, 3, 512])
        pT = sbuf(mx1, "pT", [P, 2, 512])
        t1 = sbuf(mx1, "t1", [P, 2, T])
        hn = kw[:].rearrange("p d t e -> p d (t e)")
        hT = sbuf(mx1, "hT", [P, 4, T])
        den1 = sbuf(mx1, "den1", [P, T])
        emt = sbuf(mx1, "emt", [P, 2, T])
        row1 = mvT[0:2, :, :]
        zE = mvT[:, 0, 0:384]
        Aw = mvT[:, 1, 0:384]
        wint = mvT[:, 2, 0:T]
        qw = t1
        row2 = mvT[0:1, 3, :]
        mx1.close()
        blk1.close()

        ffn = ExitStack()
        nH = sbuf(ffn, "nH", [P, KD, TM], F32R)
        nL = sbuf(ffn, "nL", [P, KD, TM], F32R)
        ffn2 = ExitStack()
        sq = sbuf(ffn2, "sq", [P, KD, TM])
        Y = sbuf(ffn2, "Y", [P, KD, T])
        gH = sbuf(ffn2, "gH", [P, KH, TM], F32R)
        gL = sbuf(ffn2, "gL", [P, KH, TM], F32R)
        sg = sbuf(ffn2, "sg", [P, 2, TM])
        hbuf = sbuf(ffn2, "hbuf", [P, 2, TM])
        ffn2.close()
        blk2 = ExitStack()
        c2 = sbuf(blk2, "c2", [P, 3 * TM])
        dist = c2[:, 0:2 * TM].rearrange("p (b k) -> p b k", b=2)
        reset = c2[:, 2 * TM:3 * TM]
        causal = sbuf(blk2, "causal", [P, 8, 64], U32)
        gatew = sbuf(blk2, "gatew", [16, 256])
        glT = sbuf(blk2, "glT", [16, TM])
        kvraw2 = sbuf(blk2, "kvraw2", [P, 2, TM])
        gkT = sbuf(blk2, "gkT", [P, 2, TM])
        gqT = sbuf(blk2, "gqT", [P, 2, T])
        gvT = sbuf(blk2, "gvT", [P, 4, TM])
        qT2 = sbuf(blk2, "qT2", [P, 4, T])
        grT = sbuf(blk2, "grT", [P, 4, T])
        gab = sbuf(blk2, "gab", [P, 2 * KD, T])
        tA = sbuf(blk2, "tA", [P, 2, TM])
        tB = sbuf(blk2, "tB", [P, 2, TM])
        tC = sbuf(blk2, "tC", [P, 2, TM])
        blast = sbuf(blk2, "blast", [P, 2, 4])
        kdT = sbuf(blk2, "kdT", [P, 2, TM])
        kS2 = sbuf(blk2, "kS2", [P, TM])
        avz2 = sbuf(blk2, "avz2", [P, 3, 2, 192])
        gvtok = sbuf(blk2, "gvtok", [64, 5, 512])
        kdtok = sbuf(blk2, "kdtok", [64, 4, 256])
        St = sbuf(blk2, "St", [P, 4, 2, P])
        attm = sbuf(blk2, "attm", [64, 4, 4, 64])
        bias2 = sbuf(blk2, "bias2", [P, 2, 2, TM])
        Sm2 = sbuf(blk2, "Sm2", [P, 2, TM])
        pT2 = sbuf(blk2, "pT2", [P, 2, 384])
        og = gvT
        blk2.close()
        ffn.close()

        acc = root.enter_context(nc.psum_tensor("acc", [P, 4, 512], F32))
        wk = root.enter_context(nc.psum_tensor("wk", [P, 4, 512], F32))

        vec_in, tok_in, cst_in, c1_in, c2_in = (sem(n) for n in ("vec_in", "tok_in", "cst_in", "c1_in", "c2_in"))
        raw_ready = [sem(f"raw_ready{j}") for j in range(RING)]
        hi_ready, lo_ready = sem("hi_ready"), sem("lo_ready")
        mm_done = sem("mm_done")
        acc_free = [sem("acc_free0"), sem("acc_free1")]
        act_chain, dve_chain = sem("act_chain"), sem("dve_chain")
        silu_ready, mods_ready = sem("silu_ready"), sem("mods_ready")
        ada_done, ada_row, ada_cols, ada_used = sem("ada_done"), sem("ada_row"), sem("ada_cols"), sem("ada_used")
        sq_ready, ssq_ps, rms_ready = sem("sq_ready"), sem("ssq_ps"), sem("rms_ready")
        xn_ready, nh_ready, nl_ready = sem("xn_ready"), sem("nh_ready"), sem("nl_ready")
        y_scaled, r_ready = sem("y_scaled"), sem("r_ready")
        gh_ready, gl_ready = sem("gh_ready"), sem("gl_ready")
        mx_sum, mxh_ready, mxl_ready = sem("mx_sum"), sem("mxh_ready"), sem("mxl_ready")
        out_ready, out_sent = sem("out_ready"), sem("out_sent")
        pads, zero2, bias_ready = sem("pads"), sem("zero2"), sem("bias_ready")
        s_ps, s_max, p_exp, p_norm = sem("s_ps"), sem("s_max"), sem("p_exp"), sem("p_norm")
        pt_ps, pt_ready, o_ps, oh_ready, ol_ready = (sem(n) for n in ("pt_ps", "pt_ready", "o_ps", "oh_ready", "ol_ready"))
        gt_log, lf_ready, rows_ps, rows_ready = sem("gt_log"), sem("lf_ready"), sem("rows_ps"), sem("rows_ready")
        cols_ps, wk_arg, wk_ready = sem("cols_ps"), sem("wk_arg"), sem("wk_ready")
        rope_ps, rope_ready, avt_ps, avz_ready = sem("rope_ps"), sem("rope_ready"), sem("avt_ps"), sem("avz_ready")
        mvt_ps, vtok_ready, conv_ready, mqk_ready = sem("mvt_ps"), sem("vtok_ready"), sem("conv_ready"), sem("mqk_ready")
        kt_ps, ktok_ready, ks_ps, ks_ready = sem("kt_ps"), sem("ktok_ready"), sem("ks_ps"), sem("ks_ready")
        kw_ready, cst_ps, cst_ready = sem("kw_ready"), sem("cst_ps"), sem("cst_ready")
        ms_ps, mb_ps, mw_ready, z_ready, e_ready = (sem(n) for n in ("ms_ps", "mb_ps", "mw_ready", "z_ready", "e_ready"))
        a_ready, qw_ready, nd_ps, nd_used = sem("a_ready"), sem("qw_ready"), sem("nd_ps"), sem("nd_used")
        hsum_ready, hsq_ready, hss_ps, hrms = sem("hsum_ready"), sem("hsq_ready"), sem("hss_ps"), sem("hrms")
        mlo_ready, mlh_ready, mll_ready = sem("mlo_ready"), sem("mlh_ready"), sem("mll_ready")
        z_ps, z_abs, z_ln, b_ready, eb_ready = (sem(n) for n in ("z_ps", "z_abs", "z_ln", "b_ready", "eb_ready"))
        bl_ready, ed_ready, kd_ready, qk_ready = sem("bl_ready"), sem("ed_ready"), sem("kd_ready"), sem("qk_ready")
        gvt_ps, gvt_ready, kdt_ps, kdt_ready = sem("gvt_ps"), sem("gvt_ready"), sem("kdt_ps"), sem("kdt_ready")
        kv_ps, st_ready, at_ps, at_ready = sem("kv_ps"), sem("st_ready"), sem("at_ps"), sem("at_ready")
        go_cross = sem("go_cross")
        go_ps, go_sum, go_ready, gss_ps, grms = sem("go_ps"), sem("go_sum"), sem("go_ready"), sem("gss_ps"), sem("grms")
        yb_ready, ybh_ready, ybl_ready = sem("yb_ready"), sem("ybh_ready"), sem("ybl_ready")
        gates_ready = sem("gates_ready")
        ks2_ps, ks2_ready, av2_ps, av2_ready = sem("ks2_ps"), sem("ks2_ready"), sem("av2_ps"), sem("av2_ready")

        epsc = EPS
        GV_BANKS = [wk[:, 2, :], wk[:, 3, :], acc[:, 2, :], acc[:, 3, :], wk[:, 2, :]]
        MV_BANKS = {2: wk[:, 1, :], 3: wk[:, 2, :], 0: wk[:, 3, :], 1: acc[:, 1, :]}
        CST_BANKS = [wk[:, 1, :], wk[:, 2, :], wk[:, 3, :], acc[:, 3, :]]
        HEADS = (0, 2, 1, 3)
        UNITS = [(hp, b, par) for hp in range(4) for b in range(2) for par in range(2)]

        def chunk(c):
            return (0, META) if c == 0 else (META + 64 * (c - 1), META + 64 * c)

        def lanes(h):
            return slice(HD * (h % 2), HD * (h % 2) + HD)

        def order(v):
            h, d = divmod(v, 2)
            return h, d, (0, 1, P) if d == 0 else (1, 0, 0)

        block = root.enter_context(nc.Block())

        @block.sync
        def _(sp):
            def freed(name, i, j):
                before = BEFORE[name] if isinstance(i, int) and i == 0 else name
                if before:
                    last = BASE[before] + (COUNT[before] if before != name else i)
                    sp.wait_ge(ada_done if before in ADA else lo_ready, 4 * last + j - 3)

            def load(name, i, j, src):
                freed(name, i, j)
                w = 1
                for n in src.shape[1:]:
                    w *= n
                dst = raw[:, j, 0:w].rearrange("p (k m) -> p k m", m=src.shape[2])
                sp.dma_start(dst, src).then_inc(raw_ready[j], 16)

            def panel(w, col, q, width=256):
                return w[512 * q:512 * q + 512, ds(col, width)].rearrange("(k p) m -> p k m", p=P)

            def columns(name, i, w, cols):
                for j in range(4):
                    load(name, i, j, panel(w, cols[j // 2], j % 2))

            def ada(name, i, col):
                for j in range(4):
                    load(name, i, j, dr["w_ada"][256 * j:256 * j + 256, ds(col, 512)].rearrange("(k p) m -> p k m", p=P))

            def down(name, w):
                with sp.Fori(0, COUNT[name]) as i:
                    for j in range(4):
                        rows = w[SLOT * (j % 2):SLOT * (j % 2) + SLOT, ds(256 * i + P * (j // 2), P)]
                        load(name, i, j, rows.rearrange("(k p) m -> p k m", p=P))

            def gate_up(name, wg, wu, up0):
                with sp.Fori(0, COUNT[name]) as i:
                    for j in range(4):
                        load(name, i, j, panel(wg, 256 * i, j) if j < 2 else panel(wu, 256 * i + up0, j - 2))

            for i in range(COUNT["ada1"]):
                ada("ada1", i, 512 * i)
            w = dr["w_in"]
            load("win0", 0, 0, panel(w, 512, 0))
            load("win0", 0, 1, panel(w, 512, 1))
            load("win0", 0, 2, panel(w, 2304, 0, 16))
            load("win0", 0, 3, panel(w, 2304, 1, 16))
            for n, cols in enumerate(((768, 1024), (1280, 1536), (0, 256), (1792, 2048))):
                columns(f"win{n + 1}", 0, w, cols)
            ada("ada2", 0, 2048)
            with sp.Fori(1, COUNT["ada2"]) as i:
                ada("ada2", i, 512 * i + 2048)
            for i in range(COUNT["wout"]):
                columns("wout", i, dr["w_out"], (512 * i, 512 * i + 256))
            gate_up("gu0", dr["w_ffn_in"], dr["w_ffn_in"], HID)
            down("dn0", dr["w_ffn_out"])
            gate_up("gu1", dr["ffn1_w_gate_2"], dr["ffn1_w_up_2"], 0)
            down("dn1", dr["ffn1_w_down_2"])
            w = dr["w_in_2"]
            load("in2k", 0, 0, panel(w, 2304, 0, 16))
            load("in2k", 0, 1, panel(w, 2304, 1, 16))
            load("in2k", 0, 2, panel(w, 512, 0))
            load("in2k", 0, 3, panel(w, 512, 1))
            for n, cols in enumerate(((1024, 768), (1280, 1536), (0, 256), (1792, 2048))):
                columns("in2k", 1 + n, w, cols)
            with sp.Fori(0, COUNT["in2g"]) as i:
                columns("in2g", i, w, (512 * i + 2320, 512 * i + 2576))
            for name, wb in (("bra", dr["w_branch_att_2"]), ("brb", dr["w_branch_gla_2"])):
                for j in range(4):
                    load(name, 0, j, panel(wb, 256 * j, 0))
            with sp.Fori(0, COUNT["wout2"]) as i:
                columns("wout2", i, dr["w_out_2"], (512 * i, 512 * i + 256))
            gate_up("gu2", dr["ffn2_w_gate_2"], dr["ffn2_w_up_2"], 0)
            down("dn2", dr["ffn2_w_down_2"])
            for k in range(KD):
                sp.wait_ge(out_ready, k + 1)
                sp.dma_start(out[:, k, :], Y[:, k, :]).then_inc(out_sent, 16)
            sp.wait_ge(out_sent, 16 * KD)

        @block.gpsimd
        def _(pool):
            pool.memset(cinq[:], 0.0)
            pool.memset(cink[:], 0.0).then_inc(pads, 1)
            pool.wait_ge(mm_done, 4 * BASE["win4"] + 4)
            pool.memset(avz[:], 0.0).then_inc(pads, 1)
            pool.wait_ge(mm_done, 4 * BASE["in2k"] + 2)
            pool.dma_start(c2[:], dr["c2"]).then_inc(c2_in, 16)
            pool.dma_start(causal[:], dr["causal"]).then_inc(c2_in, 16)
            pool.dma_start(gatew[:], dr["gla_gate_w_2"]).then_inc(c2_in, 16)
            pool.memset(avz2[:], 0.0)
            pool.memset(attm[:], 0.0).then_inc(zero2, 1)
            pool.wait_ge(c2_in, 48)
            for h in range(NHEAD):
                if h >= 2:
                    pool.wait_ge(s_max, 16 + 4 * (h // 2 - 1) + 2 + h % 2 + 1)
                pool.tensor_scalar(bias2[:, h % 2], dist, 2.0 ** -(h + 1), None, ALU.mult).then_inc(bias_ready, 1)

        @block.scalar
        def _(act):
            chain = 0

            def link(ins):
                nonlocal chain
                chain += 1
                ins.then_inc(act_chain, 1)
                act.wait_ge(act_chain, chain)

            def split(g, j, width, lead):
                act.wait_ge(raw_ready[j], 16 * (g + lead) + 16)
                if not (isinstance(g, int) and g == 0):
                    act.wait_ge(mm_done, 4 * g + j - 3)
                act.activation(hi[:, j, 0:width], raw[:, j, 0:width], ACT.Copy).then_inc(hi_ready, 1)

            def pipeline(name, width, evac, ahead, evac_first=False):
                first, n = BASE[name], COUNT[name]
                if n > 1:
                    with act.Fori(1, n) as i:
                        for j in range(4):
                            split(first + i, j, width, ring_lead(first))
                            evac(i - 1, j)
                for j in range(4):
                    if evac_first:
                        evac(n - 1, j)
                    if ahead:
                        split(first + n, j, ahead[j], ring_lead(first + n))
                    if not evac_first:
                        evac(n - 1, j)

            K4 = [1024] * 4
            DN = [SLOT] * 4
            MG = [64, 64, 1024, 1024]
            WG = [1024, 1024, 64, 64]

            def nothing(i, j):
                pass

            def multiplied(name, i, j):
                act.wait_ge(mm_done, 4 * (BASE[name] + i) + j + 1)

            act.dma_start(vec[:], dr["vecs"]).then_inc(vec_in, 16)
            act.dma_start(R[:], dr["hT"]).then_inc(tok_in, 16)
            act.dma_start(ctxT[:], dr["ctxT"]).then_inc(tok_in, 16)
            act.dma_start(cst[:], dr["cst"]).then_inc(cst_in, 16)

            act.wait_ge(vec_in, 16)
            act.activation(silu_c[:], vec[:, V_C:V_C + 16], ACT.Silu).then_inc(silu_ready, 1)
            act.wait_ge(tok_in, 32)
            for k in range(0, KD, 2):
                act.activation(sq5[:, k:k + 2, 0:T], R[:, k:k + 2, META:TM], ACT.Square).then_inc(sq_ready, 1)
                act.activation(sq5[:, k:k + 2, T:512], ctxT[:, k:k + 2, :], ACT.Square).then_inc(sq_ready, 1)

            def load_sqrt(n):
                act.activation(warm[:, n:n + 1], ident[0:1, 0:1], ACT.Sqrt)

            def norm_rms(n, width):
                act.wait_ge(ssq_ps, n + 1)
                act.activation(rms[:, 0:width], wk[:, 0, 0:width], ACT.Sqrt, bias=epsc,
                               scale=1.0 / D).then_inc(rms_ready, 1)

            norm_rms(0, 512)
            for a in range(4):
                act.wait_ge(ada_done, 4 * a + 4)
                act.activation(row1[:, a, :], acc[0:2, a, :], ACT.Copy).then_inc(ada_row, 1)
            for n in range(2 * KD):
                k, c = divmod(n, 2)
                if n in (4, 8):
                    split(0, n // 4 - 1, 1024, ring_lead(0))
                act.wait_ge(xn_ready, n + 1)
                act.activation(n5H[:, k, T * c:T * c + T], sq5[:, k, T * c:T * c + T], ACT.Copy).then_inc(nh_ready, 1)
            for j in (2, 3):
                split(0, j, WG[j], ring_lead(0))
            act.dma_start(c1[:], dr["c1"]).then_inc(c1_in, 16)

            def evac_win0(i, j):
                if j == 1:
                    multiplied("win0", i, j)
                    act.activation(kvraw[:], acc[:, 0:2, :], ACT.Copy).then_inc(acc_free[0], 1)
                if j == 3:
                    multiplied("win0", i, j)
                    act.activation(gt[:], acc[0:16, 2, :], ACT.Identity, bias=vec[0:16, V_BG:V_BG + 1])
                    act.activation(glog[:], acc[0:16, 2, :], ACT.Abs, bias=vec[0:16, V_BG:V_BG + 1]).then_inc(acc_free[1], 1)
                    act.wait_ge(acc_free[1], USE["win0"] + 1)

            def evac_win1(i, j):
                if j == 1:
                    multiplied("win1", i, j)
                    act.wait_ge(pads, 1)
                    act.activation(cinq[:, :, 1:T + 1], acc[:, 0:2, 0:T], ACT.Copy).then_inc(acc_free[0], 1)

            def evac_win2(i, j):
                if j == 1:
                    multiplied("win2", i, j)
                    act.activation(mvT[:, 0:2, :], acc[:, 0:2, :], ACT.Copy).then_inc(acc_free[0], 1)

            def evac_win3(i, j):
                if j == 1:
                    multiplied("win3", i, j)
                    act.activation(qT[:, 0:2, :], acc[:, 0:2, 0:T], ACT.Copy, scale=QS).then_inc(acc_free[0], 1)

            def evac_win4(i, j):
                if j in (1, 3):
                    multiplied("win4", i, j)
                    act.activation(sgo[:, j - 1:j + 1, :], acc[:, j - 1:j + 1, 0:T],
                                   ACT.Sigmoid).then_inc(acc_free[j // 2], 1)

            pipeline("win0", 1024, evac_win0, K4)
            link(act.activation(glog[:], glog[:], ACT.Exp, scale=-1.0))
            act.activation(glog[:], glog[:], ACT.Ln, bias=1.0).then_inc(gt_log, 1)
            pipeline("win1", 1024, evac_win1, K4)
            pipeline("win2", 1024, evac_win2, K4)
            pipeline("win3", 1024, evac_win3, K4)
            pipeline("win4", 1024, evac_win4, None)

            for n, a in enumerate((mk[:, 0, :], mk[:, 1, :], mq[:, 0, :], mq[:, 1, :])):
                act.wait_ge(conv_ready, n + 1)
                act.activation(a, a, ACT.Silu).then_inc(mqk_ready, 1)
            act.wait_ge(pads, 2)
            act.wait_ge(avt_ps, 1)
            act.activation(avz[:, :, :, 64:128], acc[:, 3, :].rearrange("p (t g d) -> p t g d", t=4, g=2),
                           ACT.Copy).then_inc(avz_ready, 1)
            for n, t in enumerate((2, 3, 0, 1)):
                act.wait_ge(mvt_ps, n + 1)
                act.activation(vtok[:, t, :], MV_BANKS[t], ACT.Copy).then_inc(vtok_ready, 1)
            act.wait_ge(kt_ps, 1)
            act.activation(ktok[:], acc[:, 0, :].rearrange("p (t d) -> p t d", t=2), ACT.Copy).then_inc(ktok_ready, 1)
            act.wait_ge(wk_arg, 1)
            act.activation(wkx[:], wkx[:], ACT.Exp).then_inc(wk_ready, 1)
            act.wait_ge(ks_ps, 1)
            act.activation(kTs[:], acc[:, 2, :], ACT.Copy).then_inc(ks_ready, 1)

            def exp_scores(n, sm, sink):
                act.wait_ge(s_max, n + 1)
                act.activation(sm, sm, ACT.Exp, bias=negm[:, n:n + 1], scale=-1.0, accum_out=rsum[:, n:n + 1])
                act.activation(esink[:, n:n + 1], sink, ACT.Exp, bias=negm[:, n:n + 1], scale=-1.0).then_inc(p_exp, 1)

            def heads_out(n, hp):
                act.wait_ge(o_ps, n + 1)
                act.activation(mixH[:, hp, :], wk[:, 3, 0:T], ACT.Copy).then_inc(oh_ready, 1)

            for u in range(18):
                if 1 <= u <= 8:
                    act.wait_ge(z_ready, u)
                    act.activation(zE, zE, ACT.Exp, scale=-1.0).then_inc(e_ready, 1)
                if u >= 2 and (u - 2) % 4 == 3:
                    heads_out((u - 2) // 4, (u - 2) // 4)
                if 1 <= u <= 16:
                    act.wait_ge(pt_ps, u)
                    act.activation(pT[:, (u - 1) % 2, :], wk[:, 2, :], ACT.Copy).then_inc(pt_ready, 1)
                if u < 8:
                    v = u
                    h, d, _ = order(v)
                    act.wait_ge(mb_ps, v + 1)
                    if v >= 1:
                        act.wait_ge(qw_ready, v)
                    if v >= 2:
                        act.wait_ge(nd_used, v - 1)
                    act.activation(wint[lanes(h), :], acc[lanes(h), 1, 0:T], ACT.Exp, scale=-1.0,
                                   bias=bc16[lanes(h), 8 + 4 * d + h:9 + 4 * d + h])
                    act.activation(emt[:, v % 2, :], acc[:, 1, T:512], ACT.Exp, scale=-1.0).then_inc(mw_ready, 1)
                if u < 16:
                    hp, b, par = UNITS[u]
                    exp_scores(u, Sm[:, u % 3, :], sinkn[:, 2 * hp + par:2 * hp + par + 1])
                if 8 <= u < 16:
                    act.wait_ge(ada_done, 16 + 4 * (u - 8) + 4)
                    act.activation(row2, acc[0:1, 3, :], ACT.Copy).then_inc(ada_row, 1)
                if u in (10, 11):
                    hp = u - 10
                    act.wait_ge(hsum_ready, 2 * hp + 2)
                    act.activation(hn[:, hp, :], hT[:, 2 * hp:2 * hp + 2, :].rearrange("p h t -> p (h t)"),
                                   ACT.Square).then_inc(hsq_ready, 1)
                if u == 12:
                    for hp in range(2):
                        act.wait_ge(hss_ps, hp + 1)
                        act.activation(hn[:, hp, :], acc[:, hp, :], ACT.Sqrt, bias=epsc, scale=1.0 / P).then_inc(hrms, 1)
                if u == 15:
                    for h in range(4):
                        act.wait_ge(mlo_ready, h + 1)
                        act.activation(mixH[:, 4 + h, :], hT[:, h, :], ACT.Copy).then_inc(mlh_ready, 1)
            for j in range(4):
                split(BASE["wout"], j, 1024, ring_lead(BASE["wout"]))

            def copy_square(name, i, s, n, width):
                act.activation(Y[:, n, :], acc[:, 2 * s:2 * s + width, 0:T], ACT.Copy)
                act.activation(sq[:, n, 0:T], acc[:, 2 * s:2 * s + width, 0:T], ACT.Square).then_inc(acc_free[s], 1)

            def evac_wout(i, j):
                if j in (1, 3):
                    multiplied("wout", i, j)
                    copy_square("wout", i, j // 2, ds(4 * i + j - 1, 2), 2)

            def evac_dn0(i, j):
                if j in (1, 3):
                    multiplied("dn0", i, j)
                    copy_square("dn0", i, j // 2, ds(2 * i + j // 2, 1), 1)

            def square_r(k, width, t0, wait):
                act.wait_ge(*wait)
                act.activation(sq[:, k, 0:width], R[:, k, t0:t0 + width], ACT.Square).then_inc(sq_ready, 1)

            def gate_up(name, f, width, ahead):
                def evac(i, j):
                    if j == 1:
                        multiplied(name, i, j)
                        act.wait_ge(acc_free[1], USE[name] + i)
                        act.activation(sg[:, :, 0:width], acc[:, 0:2, 0:width], ACT.Silu).then_inc(acc_free[0], 1)
                    if j == 3:
                        act.wait_ge(acc_free[1], USE[name] + i + 1)
                        act.activation(gH[:, ds(2 * i, 2), 0:width], hbuf[:, :, 0:width], ACT.Copy).then_inc(gh_ready, 1)
                pipeline(name, 1024, evac, ahead)

            def normed(first, width, shift):
                for k in range(KD):
                    act.wait_ge(xn_ready, first + k + 1)
                    if shift is None:
                        act.activation(nH[:, k, 0:width], sq[:, k, 0:width], ACT.Copy).then_inc(nh_ready, 1)
                    else:
                        act.activation(nH[:, k, 0:width], sq[:, k, 0:width], ACT.Identity,
                                       bias=mods[:, shift + k, 0:1]).then_inc(nh_ready, 1)

            load_sqrt(0)
            pipeline("wout", 1024, evac_wout, K4, True)
            norm_rms(1, T)
            for k in range(KD):
                square_r(k, T, META, (r_ready, k + 1))
            norm_rms(2, T)
            normed(16, T, 24)
            gate_up("gu0", 0, T, DN)
            load_sqrt(1)
            pipeline("dn0", SLOT, evac_dn0, K4, True)
            norm_rms(3, T)
            for k in range(KD):
                square_r(k, TM, 0, (r_ready, 8 + k + 1))
            norm_rms(4, TM)
            normed(24, TM, None)
            gate_up("gu1", 1, TM, DN)

            def evac_dn(name, width, t0):
                def evac(i, j):
                    if j in (1, 3):
                        square_r(ds(2 * i + j // 2, 1), width, t0, (acc_free[j // 2], USE[name] + i + 1))
                return evac

            load_sqrt(2)
            pipeline("dn1", SLOT, evac_dn("dn1", TM, 0), MG, True)
            norm_rms(5, TM)
            normed(32, TM, None)

            def evac_in2k(i, j):
                if j not in (1, 3):
                    return
                s = j // 2
                multiplied("in2k", i, j)
                src = acc[:, 2 * s:2 * s + 2, 0:TM]
                if i == 0 and s == 0:
                    ins = act.activation(glT[:], acc[0:16, 0, 0:TM], ACT.Copy)
                elif i == 0:
                    ins = act.activation(kvraw2[:], src, ACT.Copy)
                elif i == 1:
                    ins = act.activation(gkT[:] if s == 0 else gqT[:], src if s == 0 else src[:, :, 0:T], ACT.Copy)
                elif i == 2:
                    ins = act.activation(gvT[:, 2 * s:2 * s + 2, :], src, ACT.Copy)
                elif i == 3:
                    ins = act.activation(qT2[:, 2 * s:2 * s + 2, :], src[:, :, 0:T], ACT.Copy, scale=QS)
                else:
                    ins = act.activation(grT[:, 2 * s:2 * s + 2, :], src[:, :, 0:T], ACT.Silu)
                ins.then_inc(acc_free[s], 1)

            first = BASE["in2k"]
            for i in range(COUNT["in2k"]):
                for j in range(4):
                    split(first + i + 1, j, 1024, ring_lead(first))
                    evac_in2k(i, j)

            act.wait_ge(z_ps, 1)
            for t in range(2):
                ins = act.activation(tA[:, t, :], wk[:, t, 0:TM], ACT.Abs, bias=vec[:, V_GB + t:V_GB + t + 1])
            ins.then_inc(z_abs, 1)
            act.wait_ge(z_abs, 1)
            link(act.activation(tA[:], tA[:], ACT.Exp, scale=-1.0))
            act.activation(tA[:], tA[:], ACT.Ln, bias=1.0).then_inc(z_ln, 1)
            act.wait_ge(zero2, 1)
            act.wait_ge(av2_ps, 1)
            act.activation(avz2[0:META, 0, :, 64:128], acc[0:META, 0, 0:P].rearrange("p (g d) -> p g d", g=2), ACT.Copy)
            act.activation(avz2[:, 1:3, :, 64:128], acc[:, 0, P:3 * P].rearrange("p (t g d) -> p t g d", t=2, g=2),
                           ACT.Copy).then_inc(av2_ready, 1)
            act.wait_ge(ks2_ps, 1)
            act.activation(kS2[:], acc[:, 1, 0:TM], ACT.Copy).then_inc(ks2_ready, 1)
            for c in range(5):
                act.wait_ge(gvt_ps, c + 1)
                n = chunk(c)[1] - chunk(c)[0]
                act.activation(gvtok[0:n, c, :], GV_BANKS[c][0:n, :], ACT.Copy).then_inc(gvt_ready, 1)
            act.wait_ge(b_ready, 1)
            act.activation(tA[:], tC[:], ACT.Exp, scale=1.0 / 16)
            act.activation(tB[:], tC[:], ACT.Exp, scale=-1.0 / 16).then_inc(eb_ready, 1)
            act.wait_ge(bl_ready, 1)
            act.activation(tC[:, :, 0:208], tC[:, :, 0:208], ACT.Exp, scale=-1.0 / 16).then_inc(ed_ready, 1)

            for u in range(17):
                if u < 16:
                    hp, b, par = UNITS[u]
                    nk = META + P * (b + 1)
                    exp_scores(16 + u, Sm2[:, u % 2, 0:nk], sinkn[:, 8 + 2 * hp + par:9 + 2 * hp + par])
                if u >= 1:
                    n = u + 3
                    split(BASE["in2g"] + n // 4, n % 4, 1024, ring_lead(BASE["in2g"]))
                    b = UNITS[u - 1][1]
                    act.wait_ge(pt_ps, 16 + u)
                    act.activation(pT2[0:META, (u - 1) % 2, 0:P], wk[0:META, 2, 0:P], ACT.Copy)
                    act.activation(pT2[:, (u - 1) % 2, P:P * (b + 2)], wk[:, 2, P:P * (b + 2)],
                                   ACT.Copy).then_inc(pt_ready, 1)
                    if (u - 1) % 4 == 3:
                        heads_out(4 + (u - 1) // 4, (u - 1) // 4)
                    if u % 2 == 0:
                        p = u // 2 - 1
                        multiplied("in2g", p // 2, 2 * (p % 2) + 1)
                        act.activation(gab[:, 2 * p:2 * p + 2, :], acc[:, 2 * (p % 2):2 * (p % 2) + 2, 0:T],
                                       ACT.Copy).then_inc(acc_free[p % 2], 1)

            act.wait_ge(kdt_ps, 1)
            act.activation(kdtok[0:META, 0, :], wk[0:META, 0, 0:T], ACT.Copy)
            act.activation(kdtok[:, 1, :], wk[0:64, 0, T:512], ACT.Copy).then_inc(kdt_ready, 1)
            act.wait_ge(kdt_ps, 2)
            act.activation(kdtok[:, 2:4, :], wk[0:64, 1, :].rearrange("p (c d) -> p c d", c=2),
                           ACT.Copy).then_inc(kdt_ready, 1)
            act.wait_ge(acc_free[1], USE["bra"])
            for n in range(2):
                act.activation(gab[:, KD * n:KD * n + KD, :], gab[:, KD * n:KD * n + KD, :], ACT.Sigmoid).then_inc(gates_ready, 1)
            gsq = (tA, tB)
            grt = (tC, kdT)
            act.wait_ge(go_ps, 1)
            act.activation(og[:, 0:2, 0:T], acc[:, 0, :].rearrange("p (h t) -> p h t", h=2), ACT.Copy)
            act.activation(gsq[0][:, :, 0:T], acc[:, 0, :].rearrange("p (h t) -> p h t", h=2), ACT.Square).then_inc(go_ready, 1)
            act.wait_ge(go_ps, 2)
            act.activation(og[:, 2:4, 0:T], acc[:, 1, :].rearrange("p (h t) -> p h t", h=2), ACT.Copy).then_inc(go_cross, 1)
            act.wait_ge(go_sum, 1)
            act.activation(gsq[1][:, :, 0:T], og[:, 2:4, 0:T], ACT.Square).then_inc(go_ready, 1)
            for n in range(2):
                act.wait_ge(gss_ps, n + 1)
                act.activation(grt[n][:, :, 0:T], wk[:, 2 + n, :].rearrange("p (h t) -> p h t", h=2), ACT.Sqrt, bias=epsc,
                               scale=1.0 / P).then_inc(grms, 1)
            for n, h in enumerate(HEADS):
                act.wait_ge(yb_ready, n + 1)
                act.activation(mixH[:, 4 + h, :], og[:, n, 0:T], ACT.Copy).then_inc(ybh_ready, 1)

            pipeline("bra", 1024, nothing, K4)

            def evac_brb(i, j):
                act.wait_ge(mx_sum, j + 1)
                act.activation(nH[:, 2 * j:2 * j + 2, 0:T], gab[:, 2 * j:2 * j + 2, :], ACT.Copy).then_inc(mxh_ready, 1)

            pipeline("brb", 1024, evac_brb, K4)

            def evac_wout2(i, j):
                if j in (1, 3):
                    square_r(ds(4 * i + j - 1, 2), T, META, (acc_free[j // 2], USE["wout2"] + i + 1))

            load_sqrt(3)
            pipeline("wout2", 1024, evac_wout2, K4, True)
            norm_rms(6, T)
            normed(40, T, None)
            gate_up("gu2", 2, T, DN)
            load_sqrt(4)
            pipeline("dn2", SLOT, evac_dn("dn2", T, META), None, True)
            norm_rms(7, T)

        @block.vector
        def _(dve):
            chain = 0

            def link(ins):
                nonlocal chain
                chain += 1
                ins.then_inc(dve_chain, 1)
                dve.wait_ge(dve_chain, chain)

            def split(g, j, width):
                dve.wait_ge(hi_ready, 4 * g + j + 1)
                dve.tensor_tensor(lo[:, j, 0:width], raw[:, j, 0:width], hi[:, j, 0:width].bitcast(F32),
                                  ALU.subtract).then_inc(lo_ready, 1)

            def pipeline(name, width, evac, ahead, evac_first=False):
                first, n = BASE[name], COUNT[name]
                if n > 1:
                    with dve.Fori(1, n) as i:
                        for j in range(4):
                            split(first + i, j, width)
                            evac(i - 1, j)
                for j in range(4):
                    if evac_first:
                        evac(n - 1, j)
                    if ahead:
                        split(first + n, j, ahead[j])
                    if not evac_first:
                        evac(n - 1, j)

            K4 = [1024] * 4
            DN = [SLOT] * 4
            MG = [64, 64, 1024, 1024]
            WG = [1024, 1024, 64, 64]

            def nothing(i, j):
                pass

            def multiplied(name, i, j):
                dve.wait_ge(mm_done, 4 * (BASE[name] + i) + j + 1)

            def col(c):
                return vec[:, c:c + 1]

            def gains(n):
                return vec[:, V_NORM + KD * n:V_NORM + KD * n + KD]

            dve.wait_ge(vec_in, 16)
            dve.tensor_scalar(sinkn[:], vec[:, V_SINK1:V_SINK1 + 16], -1.0, None, ALU.mult)

            def norm_inv(n, width):
                dve.wait_ge(rms_ready, n + 1)
                link(dve.reciprocal(inv[:, 0:width], rms[:, 0:width]))

            norm_inv(0, 512)
            for k in range(KD):
                dve.tensor_tensor(sq5[:, k, 0:T], R[:, k, META:TM], inv[:, 0:T], ALU.mult)
                ins = dve.tensor_tensor(sq5[:, k, T:512], ctxT[:, k, :], inv[:, T:512], ALU.mult)
            dve.wait_ge(ada_cols, 1)
            link(dve.tensor_tensor(mods[:, 0:16, :], wk[:, 1, 0:32].rearrange("p (m c) -> p m c", c=2),
                                   vec[:, V_BADA:V_BADA + 16].unsqueeze(-1).broadcast_to([P, 16, 2]), ALU.add))
            for c in range(2):
                ins = dve.scalar_tensor_tensor(out=gmod[:, :, c], in0=mods[:, 8:16, c], scalar=1.0, in1=gains(N_PRE),
                                               op0=ALU.add, op1=ALU.mult)
            link(ins)

            def pre_lower(n):
                k, c = divmod(n, 2)
                s = slice(T * c, T * c + T)
                dve.wait_ge(nh_ready, n + 1)
                dve.tensor_tensor(n5L[:, k, s], sq5[:, k, s], n5H[:, k, s].bitcast(F32), ALU.subtract).then_inc(nl_ready, 1)

            for n in range(2 * KD):
                k, c = divmod(n, 2)
                s = slice(T * c, T * c + T)
                if n in (4, 8):
                    split(0, n // 4 - 1, 1024)
                dve.tensor_scalar(sq5[:, k, s], sq5[:, k, s], gmod[:, k, c:c + 1], mods[:, k, c:c + 1], ALU.mult,
                                  ALU.add).then_inc(xn_ready, 1)
                if n >= 2:
                    pre_lower(n - 2)
            pre_lower(14)
            pre_lower(15)
            for j in (2, 3):
                split(0, j, WG[j])

            def evac_win1(i, j):
                if j == 3:
                    multiplied("win1", i, j)
                    dve.wait_ge(pads, 1)
                    for t in range(2):
                        ins = dve.tensor_copy(cink[:, t, :, 1:T + 1], acc[:, 2 + t, :].rearrange("p (s t) -> p s t", s=2))
                    ins.then_inc(acc_free[1], 1)

            def evac_win2(i, j):
                if j == 3:
                    multiplied("win2", i, j)
                    dve.tensor_copy(mvT[:, 2:4, :], acc[:, 2:4, :]).then_inc(acc_free[1], 1)

            def evac_win3(i, j):
                if j == 3:
                    multiplied("win3", i, j)
                    dve.tensor_scalar(qT[:, 2:4, :], acc[:, 2:4, 0:T], QS, None, ALU.mult).then_inc(acc_free[1], 1)

            pipeline("win0", 1024, nothing, K4)
            dve.wait_ge(gt_log, 1)
            dve.scalar_tensor_tensor(out=glog[:], in0=gt[:], scalar=0.0, in1=glog[:], op0=ALU.min,
                                     op1=ALU.subtract).then_inc(lf_ready, 1)
            pipeline("win1", 1024, evac_win1, K4)
            pipeline("win2", 1024, evac_win2, K4)
            pipeline("win3", 1024, evac_win3, K4)
            pipeline("win4", 1024, nothing, None)

            dve.wait_ge(acc_free[0], USE["win1"] + 1)
            dve.wait_ge(acc_free[1], USE["win1"] + 1)
            multiplied("win4", 0, 3)
            for n in range(4):
                src, dst = (cink[:, n], mk[:, n, :].rearrange("p (s t) -> p s t", s=2)) if n < 2 else \
                    (cinq[:, n - 2:n - 1], mq[:, n - 2:n - 1, :])
                w = V_CONV + 3 * ((n + 2) % 4)
                link(dve.tensor_scalar(dst, src[:, :, 1:T + 1], col(w + 1), None, ALU.mult))
                link(dve.scalar_tensor_tensor(out=dst, in0=src[:, :, 0:T], scalar=col(w), in1=dst, op0=ALU.mult,
                                              op1=ALU.add))
                dve.scalar_tensor_tensor(out=dst, in0=src[:, :, 2:T + 2], scalar=col(w + 2), in1=dst, op0=ALU.mult,
                                         op1=ALU.add).then_inc(conv_ready, 1)

            X, C = slice(0, T), slice(T, 512)

            def timed(ap, d):
                return ap if d == 0 else ap[:, ::-1]

            dve.wait_ge(c1_in, 16)
            dve.wait_ge(cst_in, 16)
            dve.wait_ge(rows_ps, 1)
            for d in range(2):
                for s in (X, C):
                    ins = dve.tensor_tensor_scan(timed(bR[:, d, s], d), onerow[0:4, :], timed(wk[0:4, 2 * d + 1, s], d), 0.0,
                                                 ALU.mult, ALU.add)
            link(ins)
            for d in range(2):
                ins = dve.tensor_tensor(rR[:, d, :], wk[0:4, 2 * d, :], bR[:, d, :], ALU.subtract)
            link(ins)
            for d in range(2):
                ins = dve.tensor_tensor_scan(timed(MR[:, d, C], d), timed(rR[:, d, C], d), timed(rR[:, d, C], d), 0.0,
                                             ALU.max, ALU.max)
            link(ins)
            last = (511, T)
            for d in range(2):
                e = slice(last[d], last[d] + 1)
                ins = dve.tensor_tensor(m0[:, d:d + 1], bR[:, d, e], MR[:, d, e], ALU.add)
            link(ins)
            for d in range(2):
                e = slice(last[d], last[d] + 1)
                dve.tensor_tensor_scan(timed(MR[:, d, X], d), timed(rR[:, d, X], d), timed(rR[:, d, X], d), m0[:, d:d + 1],
                                       ALU.max, ALU.max)
                dve.tensor_scalar(D16[:, 4 * d:4 * d + 4], ident[0:4, 0:4], MR[:, d, e], None, ALU.mult)
                ins = dve.tensor_scalar(D16[:, 8 + 4 * d:12 + 4 * d], ident[0:4, 0:4], m0[:, d:d + 1], None, ALU.mult)
            link(ins)
            dve.tensor_tensor(bR[:, :, X], bR[:, :, X], MR[:, :, X], ALU.add).then_inc(rows_ready, 1)
            dve.wait_ge(cols_ps, 1)
            dve.tensor_copy(bc16[:], wk[:, 0, 32:48])
            link(dve.tensor_copy(rcol[:], wk[:, 0, 0:32].rearrange("p (t n) -> p t n", t=4)))
            dve.tensor_tensor(wkx[:], rcol[:, 2:4, :], bc16[:, 0:8].unsqueeze(1).broadcast_to([P, 2, 8]),
                              ALU.subtract).then_inc(wk_arg, 1)

            dve.wait_ge(rope_ps, 1)
            jobs = [(kT[:, X], kvraw[:, 0, X], acc[:, 0, X])]
            jobs += [(qT[:, t, :], qT[:, t, :], acc[:, (t + 1) // 2, X if t % 2 else C]) for t in range(4)]
            dve.tensor_copy(kT[:, C], kvraw[:, 0, C])
            for n, (dst, src, part) in enumerate(jobs):
                dve.tensor_tensor(t1[:, n % 2, :], part, sinT, ALU.mult)
                link(dve.tensor_tensor(dst, src, cosT, ALU.mult))
                ins = dve.tensor_tensor(dst, dst, t1[:, n % 2, :], ALU.add)
            ins.then_inc(rope_ready, 1)

            dve.wait_ge(wk_ready, 1)
            dve.wait_ge(ktok_ready, 1)
            for d in range(2):
                ins = dve.tensor_tensor(kw[:, d].rearrange("p t (h e) -> p t h e", h=4),
                                        ktok[:].rearrange("p t (h e) -> p t h e", h=4),
                                        wkx[:, :, 4 * d:4 * d + 4].unsqueeze(-1).broadcast_to([P, 2, 4, HD]), ALU.mult)
            ins.then_inc(kw_ready, 1)
            for n in range(4):
                dve.wait_ge(cst_ps, n + 1)
                b = CST_BANKS[n]
                dve.tensor_copy(Cst[0:64, n, 0:P], b[0:64, 0:P])
                dve.tensor_copy(Cst[64:128, n, 0:P], b[64:128, P:T])
                dve.tensor_copy(Cst[:, n, P:T], b[:, T:T + P]).then_inc(cst_ready, 1)

            def softmax_sum(n, sm):
                dve.wait_ge(p_exp, n + 1)
                c = slice(n, n + 1)
                link(dve.tensor_tensor(rinv[:, c], rsum[:, c], esink[:, c], ALU.add))
                link(dve.reciprocal(rinv[:, c], rinv[:, c]))
                dve.tensor_scalar(sm, sm, rinv[:, c], None, ALU.mult).then_inc(p_norm, 1)

            def heads_lower(n, hp):
                dve.wait_ge(oh_ready, n + 1)
                dve.tensor_tensor(mixL[:, hp, :], wk[:, 3, 0:T], mixH[:, hp, :].bitcast(F32),
                                  ALU.subtract).then_inc(ol_ready, 1)

            for u in range(18):
                if 1 <= u <= 16:
                    softmax_sum(u - 1, Sm[:, (u - 1) % 3, :])
                if 9 <= u <= 16:
                    a = u - 9
                    m = 16 + 4 * a
                    dve.wait_ge(ada_cols, a + 2)
                    dve.tensor_tensor(mods[:, m:m + 4, 0], acc[:, 3, 0:4], vec[:, V_BADA + m:V_BADA + m + 4],
                                      ALU.add).then_inc(ada_used, 1)
                if 1 <= u <= 8:
                    v = u - 1
                    h, d, (full, part, t0) = order(v)
                    dve.wait_ge(e_ready, v + 1)
                    dve.wait_ge(ms_ps, h + 1)
                    if v >= 1:
                        dve.wait_ge(nd_ps, v)
                    dve.scalar_tensor_tensor(out=Aw[:, 0:T], in0=acc[:, 0, T * full:T * full + T], scalar=HD ** -0.5,
                                             in1=zE[:, 0:T], op0=ALU.mult, op1=ALU.mult)
                    dve.scalar_tensor_tensor(out=Aw[:, T:384], in0=acc[:, 0, T * part + t0:T * part + t0 + P],
                                             scalar=HD ** -0.5, in1=zE[:, T:384], op0=ALU.mult,
                                             op1=ALU.mult).then_inc(a_ready, 1)
                if 2 <= u <= 9:
                    v = u - 2
                    h, d, _ = order(v)
                    dve.wait_ge(nd_ps, v + 1)
                    link(dve.tensor_tensor(den1[:], acc[:, 2, T:512], emt[:, v % 2, :], ALU.max))
                    link(dve.scalar_tensor_tensor(out=den1[:], in0=acc[:, 2, T:512], scalar=-1.0, in1=den1[:],
                                                  op0=ALU.mult, op1=ALU.max))
                    link(dve.reciprocal(den1[:], den1[:]))
                    if d == 0:
                        dve.tensor_tensor(hT[:, h, :], acc[:, 2, 0:T], den1[:], ALU.mult).then_inc(nd_used, 1)
                    else:
                        dve.tensor_tensor(den1[:], acc[:, 2, 0:T], den1[:], ALU.mult).then_inc(nd_used, 1)
                        dve.wait_ge(nd_used, v + 1)
                        dve.tensor_tensor(hT[:, h, :], hT[:, h, :], den1[:], ALU.add).then_inc(hsum_ready, 1)
                if u < 16:
                    hp, b, par = UNITS[u]
                    h = 2 * hp + par
                    dve.wait_ge(s_ps, u + 1)
                    if u >= 3:
                        dve.wait_ge(pt_ps, u - 2)
                    dve.tensor_tensor_reduce(Sm[:, u % 3, :], wk[:, u % 2, :], winmask[:, b, :], 1.0, sinkn[:, h:h + 1],
                                             ALU.add, ALU.min, negm[:, u:u + 1]).then_inc(s_max, 1)
                if u >= 2 and (u - 2) % 4 == 3:
                    heads_lower((u - 2) // 4, (u - 2) // 4)
                if u < 8:
                    v = u
                    h, d, (full, part, t0) = order(v)
                    c = 4 * d + h
                    dve.wait_ge(mw_ready, v + 1)
                    if v >= 1:
                        dve.wait_ge(a_ready, v)
                    dve.scalar_tensor_tensor(out=zE[:, 0:T], in0=acc[:, 1, 0:T], scalar=rcol[:, full, c:c + 1],
                                             in1=ordf if d == 0 else ordb, op0=ALU.subtract, op1=ALU.max)
                    dve.scalar_tensor_tensor(out=zE[:, T:384], in0=acc[:, 1, t0:t0 + P], scalar=rcol[:, part, c:c + 1],
                                             in1=ordf[:, 0:P] if d == 0 else ordlow, op0=ALU.subtract,
                                             op1=ALU.max).then_inc(z_ready, 1)
                    if v >= 2:
                        dve.wait_ge(nd_ps, v - 1)
                    dve.scalar_tensor_tensor(out=qw[lanes(h), v % 2, :], in0=mq[lanes(h), h // 2, :], scalar=HD ** -0.5,
                                             in1=wint[lanes(h), :], op0=ALU.mult, op1=ALU.mult).then_inc(qw_ready, 1)
                if u in (13, 14):
                    hp = u - 13
                    dve.wait_ge(hrms, hp + 1)
                    link(dve.reciprocal(hn[:, hp, :], hn[:, hp, :]))
                    for h in (2 * hp, 2 * hp + 1):
                        link(dve.scalar_tensor_tensor(out=hT[:, h, :], in0=hT[:, h, :], scalar=col(V_GML + h),
                                                      in1=hn[:, hp, T * (h % 2):T * (h % 2) + T], op0=ALU.mult, op1=ALU.mult))
                        dve.tensor_tensor(hT[:, h, :], hT[:, h, :], sgo[:, h, :], ALU.mult).then_inc(mlo_ready, 1)
                if u == 16:
                    for h in range(4):
                        dve.wait_ge(mlh_ready, h + 1)
                        dve.tensor_tensor(mixL[:, 4 + h, :], hT[:, h, :], mixH[:, 4 + h, :].bitcast(F32),
                                          ALU.subtract).then_inc(mll_ready, 1)

            for j in range(4):
                split(BASE["wout"], j, 1024)
            dve.wait_ge(ada_used, 8)
            dve.scalar_tensor_tensor(out=gmod[:, :, 2], in0=mods[:, 32:40, 0], scalar=1.0, in1=gains(N_PREF),
                                     op0=ALU.add, op1=ALU.mult)
            dve.tensor_tensor(gmod[:, :, 3], mods[:, 16:24, 0], gains(N_POST), ALU.mult)
            link(dve.tensor_tensor(gmod[:, :, 4], mods[:, 40:48, 0], gains(N_POSTF), ALU.mult))

            def post_norm(n, gain):
                norm_inv(n, T)
                for k in range(KD + 1):
                    if k < KD:
                        dve.scalar_tensor_tensor(out=Y[:, k, :], in0=Y[:, k, :], scalar=gmod[:, k, gain:gain + 1],
                                                 in1=inv[:, 0:T], op0=ALU.mult, op1=ALU.mult).then_inc(y_scaled, 1)
                    if k >= 1:
                        dve.wait_ge(y_scaled, KD * (gain - 3) + k)
                        dve.tensor_tensor(R[:, k - 1, META:TM], R[:, k - 1, META:TM], Y[:, k - 1, :],
                                          ALU.add).then_inc(r_ready, 1)

            def split_norm(n, first, width, t0, gain, shift):
                norm_inv(n, width)

                def lower(k):
                    dve.wait_ge(nh_ready, first + k + 1)
                    if shift is None:
                        ins = dve.tensor_tensor(nL[:, k, 0:width], sq[:, k, 0:width], nH[:, k, 0:width].bitcast(F32),
                                                ALU.subtract)
                    else:
                        ins = dve.scalar_tensor_tensor(out=nL[:, k, 0:width], in0=sq[:, k, 0:width],
                                                       scalar=mods[:, shift + k, 0:1], in1=nH[:, k, 0:width].bitcast(F32),
                                                       op0=ALU.add, op1=ALU.subtract)
                    ins.then_inc(nl_ready, 1)

                for k in range(KD):
                    dve.scalar_tensor_tensor(out=sq[:, k, 0:width], in0=R[:, k, t0:t0 + width], scalar=gain(k),
                                             in1=inv[:, 0:width], op0=ALU.mult, op1=ALU.mult).then_inc(xn_ready, 1)
                    if k >= 2:
                        lower(k - 2)
                lower(KD - 2)
                lower(KD - 1)

            def gate_up(name, f, width, ahead):
                def evac(i, j):
                    if j == 3:
                        multiplied(name, i, j)
                        dve.wait_ge(acc_free[0], USE[name] + i + 1)
                        dve.wait_ge(lo_ready, 4 * (BASE[name] + i) + 8)
                        dve.tensor_tensor(hbuf[:, :, 0:width], sg[:, :, 0:width], acc[:, 2:4, 0:width],
                                          ALU.mult).then_inc(acc_free[1], 1)
                        dve.wait_ge(gh_ready, COUNT[name] * f + i + 1)
                        dve.tensor_tensor(gL[:, ds(2 * i, 2), 0:width], hbuf[:, :, 0:width],
                                          gH[:, ds(2 * i, 2), 0:width].bitcast(F32), ALU.subtract).then_inc(gl_ready, 1)
                pipeline(name, 1024, evac, ahead)

            def evac_half(name, width, t0):
                def evac(i, j):
                    if j in (1, 3):
                        multiplied(name, i, j)
                        k = ds(2 * i + j // 2, 1)
                        dve.scalar_tensor_tensor(out=R[:, k, t0:t0 + width], in0=acc[:, j - 1:j, 0:width], scalar=0.5,
                                                 in1=R[:, k, t0:t0 + width], op0=ALU.mult,
                                                 op1=ALU.add).then_inc(acc_free[j // 2], 1)
                return evac

            pipeline("wout", 1024, nothing, K4, True)
            post_norm(1, 3)
            split_norm(2, 16, T, META, lambda k: gmod[:, k, 2:3], 24)
            gate_up("gu0", 0, T, DN)
            pipeline("dn0", SLOT, nothing, K4, True)
            post_norm(3, 4)
            split_norm(4, 24, TM, 0, lambda k: col(V_NORM + KD * N_F1 + k), None)
            gate_up("gu1", 1, TM, DN)
            pipeline("dn1", SLOT, evac_half("dn1", TM, 0), MG, True)
            dve.wait_ge(acc_free[1], USE["in2k"])
            split_norm(5, 32, TM, 0, lambda k: col(V_NORM + KD * N_MIX + k), None)
            for i in range(COUNT["in2k"]):
                for j in range(4):
                    split(BASE["in2k"] + i + 1, j, 1024)
            dve.wait_ge(z_abs, 1)
            for t in range(2):
                ins = dve.tensor_scalar(tB[:, t, :], wk[:, t, 0:TM], col(V_GB + t), 0.0, ALU.add, ALU.min)
            link(ins)
            dve.wait_ge(z_ln, 1)
            link(dve.tensor_tensor(tB[:], tB[:], tA[:], ALU.subtract))
            dve.wait_ge(c2_in, 48)
            for t in range(2):
                ins = dve.tensor_tensor_scan(tC[:, t, :], reset, tB[:, t, :], 0.0, ALU.mult, ALU.add)
            link(ins)
            dve.tensor_copy(blast[:], tC[:, :, META - 1:META + 192:64]).then_inc(b_ready, 1)
            dve.wait_ge(eb_ready, 1)
            dve.wait_ge(b_ready, 1)
            for t in range(2):
                dve.tensor_scalar(tC[:, t, 0:META], tC[:, t, 0:META], blast[:, t, 0:1], None, ALU.subtract)
                f = tC[:, t, META:META + 192].rearrange("p (c i) -> p c i", c=3)
                ins = dve.tensor_tensor(f, f, blast[:, t, 1:4].unsqueeze(-1).broadcast_to([P, 3, 64]), ALU.subtract)
            ins.then_inc(bl_ready, 1)
            dve.scalar_tensor_tensor(out=gqT[:], in0=gqT[:], scalar=HD ** -0.5, in1=tA[:, :, META:TM], op0=ALU.mult,
                                     op1=ALU.mult)
            dve.wait_ge(ed_ready, 1)
            dve.tensor_tensor(kdT[:, :, 0:208], gkT[:, :, 0:208], tC[:, :, 0:208], ALU.mult).then_inc(kd_ready, 1)
            dve.wait_ge(kd_ready, 1)
            dve.tensor_tensor(gkT[:], gkT[:], tB[:], ALU.mult).then_inc(qk_ready, 1)

            for u in range(18):
                if 1 <= u <= 16:
                    softmax_sum(16 + u - 1, Sm2[:, (u - 1) % 2, 0:META + P * (UNITS[u - 1][1] + 1)])
                if u < 16:
                    hp, b, par = UNITS[u]
                    h = 2 * hp + par
                    nk = META + P * (b + 1)
                    dve.wait_ge(s_ps, 16 + u + 1)
                    dve.wait_ge(bias_ready, h + 1)
                    if u >= 2:
                        dve.wait_ge(pt_ps, 16 + u - 1)
                    dve.tensor_tensor_reduce(Sm2[:, u % 2, 0:nk], wk[:, u % 2, 0:nk], bias2[:, h % 2, b, 0:nk], 1.0,
                                             sinkn[:, 8 + h:9 + h], ALU.add, ALU.min,
                                             negm[:, 16 + u:17 + u]).then_inc(s_max, 1)
                if u >= 2 and (u - 2) % 4 == 3:
                    heads_lower(4 + (u - 2) // 4, (u - 2) // 4)
                if 1 <= u <= 16:
                    split(BASE["in2g"] + (u + 3) // 4, (u + 3) % 4, 1024)

            for c in range(4):
                dve.wait_ge(kv_ps, c + 1)
                for t in range(2):
                    for q in range(2):
                        s = slice(64 * q, 64 * q + 64)
                        new = acc[s, c, T * t + P * q:T * t + P * q + P]
                        if c == 0:
                            ins = dve.tensor_copy(St[s, 0, t, :], new)
                        else:
                            e = chunk(c)[1] - 1
                            ins = dve.scalar_tensor_tensor(out=St[s, c, t, :], in0=St[s, c - 1, t, :],
                                                           scalar=tA[s, t, e:e + 1], in1=new, op0=ALU.mult, op1=ALU.add)
                ins.then_inc(st_ready, 1)
                dve.wait_ge(st_ready, c + 1)
            dve.wait_ge(zero2, 1)
            for n in range(2):
                dve.wait_ge(at_ps, n + 1)
                dve.copy_predicated(attm[:, 2 * n:2 * n + 2].rearrange("p h c i -> p (h c) i"), causal[0:64],
                                    wk[0:64, n, :].rearrange("p (m i) -> p m i", m=8)).then_inc(at_ready, 1)
            grt = (tC, kdT)
            dve.wait_ge(go_cross, 1)
            dve.tensor_tensor(og[:, 2:4, 0:T], og[:, 2:4, 0:T], acc[:, 3, :].rearrange("p (h t) -> p h t", h=2),
                              ALU.add).then_inc(go_sum, 1)
            for n in range(2):
                dve.wait_ge(grms, n + 1)
                link(dve.reciprocal(grt[n][:, :, 0:T], grt[n][:, :, 0:T]))
                for i in (2 * n, 2 * n + 1):
                    link(dve.scalar_tensor_tensor(out=og[:, i, 0:T], in0=og[:, i, 0:T], scalar=col(V_GO),
                                                  in1=grt[n][:, i % 2, 0:T], op0=ALU.mult, op1=ALU.mult))
                    dve.tensor_tensor(og[:, i, 0:T], og[:, i, 0:T], grT[:, HEADS[i], :], ALU.mult).then_inc(yb_ready, 1)
            for n, h in enumerate(HEADS):
                dve.wait_ge(ybh_ready, n + 1)
                dve.tensor_tensor(mixL[:, 4 + h, :], og[:, n, 0:T], mixH[:, 4 + h, :].bitcast(F32),
                                  ALU.subtract).then_inc(ybl_ready, 1)

            def evac_bra(i, j):
                s = 2 * (j % 2)
                multiplied("bra", i, j)
                if j == 0:
                    dve.wait_ge(gates_ready, 2)
                dve.tensor_tensor(gab[:, 2 * j:2 * j + 2, :], gab[:, 2 * j:2 * j + 2, :], acc[:, s:s + 2, 0:T],
                                  ALU.mult).then_inc(acc_free[j % 2], 1)

            def evac_brb(i, j):
                s = 2 * (j % 2)
                a, b = gab[:, 2 * j:2 * j + 2, :], gab[:, KD + 2 * j:KD + 2 * j + 2, :]
                multiplied("brb", i, j)
                dve.tensor_tensor(b, b, acc[:, s:s + 2, 0:T], ALU.mult).then_inc(acc_free[j % 2], 1)
                dve.wait_ge(acc_free[j % 2], USE["brb"] + j // 2 + 1)
                dve.tensor_tensor(a, a, b, ALU.add).then_inc(mx_sum, 1)
                dve.wait_ge(mxh_ready, j + 1)
                dve.tensor_tensor(nL[:, 2 * j:2 * j + 2, 0:T], a, nH[:, 2 * j:2 * j + 2, 0:T].bitcast(F32),
                                  ALU.subtract).then_inc(mxl_ready, 1)

            pipeline("bra", 1024, evac_bra, K4)
            pipeline("brb", 1024, evac_brb, K4)

            def evac_wout2(i, j):
                if j in (1, 3):
                    multiplied("wout2", i, j)
                    k = ds(4 * i + j - 1, 2)
                    dve.tensor_tensor(R[:, k, META:TM], R[:, k, META:TM], acc[:, j - 1:j + 1, 0:T],
                                      ALU.add).then_inc(acc_free[j // 2], 1)

            pipeline("wout2", 1024, evac_wout2, K4, True)
            dve.wait_ge(acc_free[1], USE["gu2"])
            split_norm(6, 40, T, META, lambda k: col(V_NORM + KD * N_F2 + k), None)
            gate_up("gu2", 2, T, DN)
            pipeline("dn2", SLOT, evac_half("dn2", T, META), None, True)

            norm_inv(7, T)
            for k in range(KD):
                dve.scalar_tensor_tensor(out=Y[:, k, :], in0=R[:, k, META:TM], scalar=col(V_NORM + KD * N_FIN + k),
                                         in1=inv[:, 0:T], op0=ALU.mult, op1=ALU.mult).then_inc(out_ready, 1)

        @block.tensor
        def _(pe):
            def split_mm(out_, wH, wL, xH, xL, start, stop):
                pe.matmul(out_, wH, xH, start=start, stop=False)
                pe.matmul(out_, wH, xL, start=False, stop=False)
                return pe.matmul(out_, wL, xH, start=False, stop=stop)

            def set_free(s, use):
                if not (isinstance(use, int) and use == 0):
                    pe.wait_ge(acc_free[s], use)

            def arrived(g, j):
                pe.wait_ge(lo_ready, 4 * g + j + 1)

            def pair(g, use, s, xH, xL, n, ready=None):
                set_free(s, use)
                for q in range(2):
                    half(g, s, q, xH, xL, n, ready)

            def half(g, s, q, xH, xL, n, ready=None):
                j = 2 * s + q
                arrived(g, j)
                for kk in range(4):
                    k = 4 * q + kk
                    if ready:
                        pe.wait_ge(ready[0], ready[1] + int(ready[2] * k) + (1 if ready[2] < 1 else ready[2]))
                    for m in range(2):
                        w = slice(256 * kk + P * m, 256 * kk + P * m + P)
                        ins = split_mm(acc[:, 2 * s + m, 0:n], hi[:, j, w], lo[:, j, w], xH(k), xL(k),
                                       k == 0, k == KD - 1)
                ins.then_inc(mm_done, 1)

            def pairs(name, xs, n, ready=None):
                with pe.Fori(0, COUNT[name]) as i:
                    for s in range(2):
                        pair(BASE[name] + i, USE[name] + i, s, *xs, n, ready)

            def sum_squares(n, src, width, squared):
                for k in range(KD):
                    pe.wait_ge(*squared(k))
                    ins = pe.matmul(wk[:, 0, 0:width], ones, src[:, k, 0:width], start=k == 0, stop=k == KD - 1)
                ins.then_inc(ssq_ps, 1)

            def ada(name, a, j, out_, n):
                pe.wait_ge(raw_ready[j], 16 * (RING_AT[name] + a) + 16)
                for kk in range(2):
                    k = 2 * j + kk
                    ins = pe.matmul(out_[0:n, :], silu_c[:, 2 * k:2 * k + n], raw[:, j, 512 * kk:512 * kk + 512],
                                    start=k == 0, stop=k == KD - 1)
                ins.then_inc(ada_done, 1)

            pe.wait_ge(silu_ready, 1)
            for a in range(4):
                for j in range(4):
                    ada("ada1", a, j, acc[:, a, :], 2)
                if a == 1:
                    pe.wait_ge(cst_in, 16)
                    sum_squares(0, sq5, 512, lambda k: (sq_ready, 2 * (k // 2) + 2))
            pe.wait_ge(ada_row, 4)
            for m in range(16):
                ins = pe.transpose(wk[:, 1, 2 * m:2 * m + 2], row1[:, m // 4, P * (m % 4):P * (m % 4) + P], ident[0:2, 0:2])
            ins.then_inc(ada_cols, 1)

            both = (lambda k: n5H[:, k, :], lambda k: n5L[:, k, :])
            frames = (lambda k: n5H[:, k, 0:T], lambda k: n5L[:, k, 0:T])
            g = BASE["win0"]
            pair(g, 0, 0, *both, 512, (nl_ready, 0, 2))
            for q in range(2):
                arrived(g, 2 + q)
                for kk in range(4):
                    k, w = 4 * q + kk, slice(16 * kk, 16 * kk + 16)
                    ins = split_mm(acc[0:16, 2, :], hi[:, 2 + q, w], lo[:, 2 + q, w], n5H[:, k, :], n5L[:, k, :],
                                   k == 0, k == KD - 1)
                ins.then_inc(mm_done, 1)
            for n, (xs, width) in enumerate(((both, 512), (both, 512), (frames, T), (frames, T))):
                for s in range(2):
                    pair(BASE[f"win{n + 1}"], USE[f"win{n + 1}"], s, *xs, width)

            pe.wait_ge(lf_ready, 1)
            for q in range(4):
                ins = pe.matmul(wk[0:4, q, :], ident[0:16, 4 * q:4 * q + 4], (glog if q % 2 else gt)[:], start=True, stop=True)
            ins.then_inc(rows_ps, 1)
            pe.wait_ge(c1_in, 16)
            for s in range(2):
                pe.wait_ge(acc_free[s], USE["wout"])
            pe.matmul(acc[:, 0, 0:T], perm, kvraw[:, 0, 0:T], start=True, stop=True)
            for t in range(4):
                ins = pe.matmul(acc[:, (t + 1) // 2, T * ((t + 1) % 2):T * ((t + 1) % 2) + T], perm, qT[:, t, :],
                                start=True, stop=True)
            ins.then_inc(rope_ps, 1)
            for t in range(4):
                ins = pe.transpose(acc[:, 3, P * t:P * t + P], kvraw[:, 1, P * t:P * t + P], ident)
            ins.then_inc(avt_ps, 1)
            pe.wait_ge(rows_ready, 1)
            for t in range(4):
                for d in range(2):
                    pe.transpose(wk[:, 0, 8 * t + 4 * d:8 * t + 4 * d + 4], rR[:, d, P * t:P * t + P], ident[0:4, 0:4])
            pe.matmul(wk[:, 0, 32:48], ones[0:4, :], D16[:], start=True, stop=True).then_inc(cols_ps, 1)
            for t in (2, 3, 0, 1):
                if t == 1:
                    pe.wait_ge(rope_ready, 1)
                for h in range(4):
                    ins = pe.transpose(MV_BANKS[t][:, P * h:P * h + P], mvT[:, h, P * t:P * t + P], ident)
                ins.then_inc(mvt_ps, 1)
            pe.wait_ge(mqk_ready, 2)
            for t in range(2):
                for n in range(2):
                    ins = pe.transpose(acc[:, 0, T * t + P * n:T * t + P * n + P], mk[:, n, T + P * t:T + P * t + P], ident)
            ins.then_inc(kt_ps, 1)
            pe.matmul(acc[:, 2, :], swap, kT[:], start=True, stop=True).then_inc(ks_ps, 1)
            pe.wait_ge(kw_ready, 1)
            pe.wait_ge(vtok_ready, 4)
            pe.wait_ge(avz_ready, 1)
            for n in range(4):
                d, hp = divmod(n, 2)
                for part in range(2):
                    for t in range(2):
                        lhs = kw[:, d, t, P * hp:P * hp + P]
                        if part == 0:
                            pe.matmul(CST_BANKS[n][:, 0:T], lhs, vtok[:, 2 + t, T * hp:T * hp + T], start=t == 0, stop=t == 1)
                        else:
                            ins = pe.matmul(CST_BANKS[n][:, T:T + P], lhs, ones, start=t == 0, stop=t == 1)
                ins.then_inc(cst_ps, 1)

            def transposed_out(par, b, keys):
                for i, (v, p) in enumerate(keys):
                    ins = pe.matmul(wk[:, 3, P * b:P * b + P], v, p, start=par == 0 and i == 0,
                                    stop=par == 1 and i == len(keys) - 1)
                if b == 1 and par == 1:
                    ins.then_inc(o_ps, 1)

            pe.wait_ge(cst_ready, 4)
            pe.wait_ge(ks_ready, 1)
            pe.wait_ge(mqk_ready, 4)
            for u in range(17):
                if u >= 9:
                    pe.wait_ge(ada_row, 4 + u - 8)
                    for m in range(4):
                        ins = pe.transpose(acc[:, 3, m:m + 1], row2[:, P * m:P * m + P], ident[0:1, 0:1])
                    ins.then_inc(ada_cols, 1)
                if u < 16:
                    hp, b, par = UNITS[u]
                    h = 2 * hp + par
                    keys = kT if h // 4 == h % 2 else kTs
                    if u >= 2:
                        pe.wait_ge(s_max, u - 1)
                    pe.matmul(wk[:, u % 2, :], qT[lanes(h), hp, P * b:P * b + P], keys[lanes(h), :],
                              start=True, stop=True).then_inc(s_ps, 1)
                if u >= 1:
                    hp, b, par = UNITS[u - 1]
                    pe.wait_ge(p_norm, u)
                    if u >= 2:
                        pe.wait_ge(pt_ready, u - 1)
                    for t in range(4):
                        ins = pe.transpose(wk[:, 2, P * t:P * t + P], Sm[:, (u - 1) % 3, P * t:P * t + P], ident)
                    ins.then_inc(pt_ps, 1)
                if u < 8:
                    v = u
                    h, d, _ = order(v)
                    if d == 0:
                        if v >= 1:
                            pe.wait_ge(a_ready, v)
                        for s in range(2):
                            ins = pe.matmul(acc[:, 0, T * s:T * s + T], mk[lanes(h), h // 2, P * s:P * s + P],
                                            mq[lanes(h), h // 2, :], start=True, stop=True)
                        ins.then_inc(ms_ps, 1)
                    if v >= 1:
                        pe.wait_ge(z_ready, v)
                    pe.matmul(acc[:, 1, 0:T], sel4[0:4, h, :], MR[:, d, 0:T], start=True, stop=True)
                    pe.matmul(acc[:, 1, T:512], sel4[0:4, h, :], bR[:, d, 0:T], start=True, stop=True).then_inc(mb_ps, 1)
                if 1 <= u <= 8:
                    v = u - 1
                    h, d, (full, part, t0) = order(v)
                    pe.wait_ge(a_ready, v + 1)
                    pe.wait_ge(qw_ready, v + 1)
                    if v >= 1:
                        pe.wait_ge(nd_used, v)
                    for o, lhs in ((0, lambda s: vtok[:, s, P * h:P * h + P]), (T, lambda s: ones)):
                        pe.matmul(acc[:, 2, o:o + T], lhs(full), Aw[:, 0:T], start=True, stop=False)
                        pe.matmul(acc[:, 2, o + t0:o + t0 + P], lhs(part), Aw[:, T:384], start=False, stop=False)
                        ins = pe.matmul(acc[:, 2, o:o + T], Cst[lanes(h), 2 * d + h // 2, o // 2:o // 2 + P],
                                        qw[lanes(h), v % 2, :], start=False, stop=True)
                    ins.then_inc(nd_ps, 1)
                if 8 <= u < 16:
                    a = u - 8
                    if a >= 1:
                        pe.wait_ge(ada_used, a)
                    for j in range(4):
                        ada("ada2", a, j, acc[:, 3, :], 1)
                if u == 12:
                    for hp in range(2):
                        pe.wait_ge(hsq_ready, hp + 1)
                        pe.matmul(acc[:, hp, :], ones, hn[:, hp, :], start=True, stop=True).then_inc(hss_ps, 1)
                if u >= 1:
                    pe.wait_ge(pt_ready, u)
                    hp, b, par = UNITS[u - 1]
                    if b == 0 and par == 0 and hp >= 1:
                        pe.wait_ge(ol_ready, hp)
                    g4 = (2 * hp + par) // 4
                    vs = slice(64, 192) if par == 0 else slice(0, P)
                    transposed_out(par, b, [(avz[:, t, g4, vs], pT[:, (u - 1) % 2, P * t:P * t + P])
                                                   for t in range(4)])

            def gate_up(name, first, t0, width):
                xs = (lambda k: nH[:, k, t0:t0 + width], lambda k: nL[:, k, t0:t0 + width])
                pairs(name, xs, width, (nl_ready, first, 1))

            def down(name, f, width):
                with pe.Fori(0, COUNT[name]) as i:
                    for j in range(4):
                        s = j // 2
                        if j % 2 == 0:
                            set_free(s, USE[name] + i)
                        arrived(BASE[name] + i, j)
                        pe.wait_ge(gl_ready, 11 * f + (6 if j % 2 == 0 else 11))
                        for kk in range(HALF):
                            k = HALF * (j % 2) + kk
                            w = slice(P * kk, P * kk + P)
                            ins = split_mm(acc[:, 2 * s, 0:width], hi[:, j, w], lo[:, j, w], gH[:, k, 0:width],
                                           gL[:, k, 0:width], k == 0, k == KH - 1)
                        ins.then_inc(mm_done, 1)

            pe.wait_ge(mll_ready, 4)
            pe.wait_ge(ol_ready, 4)
            mixed = (lambda k: mixH[:, k, :], lambda k: mixL[:, k, :])
            pairs("wout", mixed, T)
            sum_squares(1, sq, T, lambda k: (acc_free[k % 4 // 2], USE["wout"] + k // 4 + 1))
            sum_squares(2, sq, T, lambda k: (sq_ready, 8 + k + 1))
            gate_up("gu0", 16, 0, T)
            down("dn0", 0, T)
            sum_squares(3, sq, T, lambda k: (acc_free[k % 2], USE["dn0"] + k // 2 + 1))
            sum_squares(4, sq, TM, lambda k: (sq_ready, 16 + k + 1))
            gate_up("gu1", 24, 0, TM)
            down("dn1", 1, TM)
            sum_squares(5, sq, TM, lambda k: (sq_ready, 24 + k + 1))

            allT = (lambda k: nH[:, k, :], lambda k: nL[:, k, :])
            frames = (lambda k: nH[:, k, META:TM], lambda k: nL[:, k, META:TM])
            g = BASE["in2k"]
            set_free(0, USE["in2k"])
            for q in range(2):
                arrived(g, q)
                pe.wait_ge(nl_ready, 32 + 4 * (q + 1))
                for kk in range(4):
                    k, w = 4 * q + kk, slice(16 * kk, 16 * kk + 16)
                    ins = split_mm(acc[0:16, 0, 0:TM], hi[:, q, w], lo[:, q, w], nH[:, k, :], nL[:, k, :], k == 0, k == KD - 1)
                ins.then_inc(mm_done, 1)
            pair(g, USE["in2k"], 1, *allT, TM)
            for n, (a, b) in enumerate(((allT, frames), (allT, allT), (frames, frames), (frames, frames))):
                for s, xs in enumerate((a, b)):
                    pair(g + 1 + n, USE["in2k"] + 1 + n, s, *xs, TM if xs is allT else T)

            pe.wait_ge(c2_in, 48)
            for s in range(2):
                pe.wait_ge(acc_free[s], USE["in2g"])
            for t in range(2):
                ins = pe.matmul(wk[:, t, 0:TM], gatew[:, P * t:P * t + P], glT[:], start=True, stop=True)
            ins.then_inc(z_ps, 1)
            pe.transpose(acc[0:META, 0, 0:P], kvraw2[:, 1, 0:META], ident)
            for t in range(2):
                ins = pe.transpose(acc[:, 0, P + P * t:2 * P + P * t], kvraw2[:, 1, META + P * t:META + P * t + P], ident)
            ins.then_inc(av2_ps, 1)
            pe.matmul(acc[:, 1, 0:TM], swap, kvraw2[:, 0, :], start=True, stop=True).then_inc(ks2_ps, 1)
            for c in range(5):
                a, e = chunk(c)
                if c == 4:
                    pe.wait_ge(gvt_ready, 1)
                for h in range(4):
                    ins = pe.transpose(GV_BANKS[c][0:e - a, P * h:P * h + P], gvT[:, h, a:e], ident)
                ins.then_inc(gvt_ps, 1)

            pe.wait_ge(eb_ready, 1)
            pe.wait_ge(ks2_ready, 1)
            pe.wait_ge(av2_ready, 1)
            pe.wait_ge(gvt_ready, 5)
            for u in range(17):
                if u < 16:
                    hp, b, par = UNITS[u]
                    h = 2 * hp + par
                    keys = kvraw2[:, 0, :] if h // 4 == h % 2 else kS2
                    nk = META + P * (b + 1)
                    if u >= 2:
                        pe.wait_ge(s_max, 16 + u - 1)
                    pe.matmul(wk[:, u % 2, 0:nk], qT2[lanes(h), hp, P * b:P * b + P], keys[lanes(h), 0:nk],
                              start=True, stop=True).then_inc(s_ps, 1)
                if u >= 1:
                    hp, b, par = UNITS[u - 1]
                    sm, pt = Sm2[:, (u - 1) % 2, :], pT2[:, (u - 1) % 2, :]
                    pe.wait_ge(p_norm, 16 + u)
                    if u >= 2:
                        pe.wait_ge(pt_ready, 16 + u - 1)
                    pe.transpose(wk[0:META, 2, 0:P], sm[:, 0:META], ident)
                    for t in range(b + 1):
                        ins = pe.transpose(wk[:, 2, P + P * t:2 * P + P * t], sm[:, META + P * t:META + P * t + P], ident)
                    ins.then_inc(pt_ps, 1)
                if u < 16:
                    i, s, q = u // 4, u // 2 % 2, u % 2
                    if q == 0:
                        set_free(s, USE["in2g"] + i)
                    half(BASE["in2g"] + i, s, q, *frames, T)
                if u >= 1:
                    pe.wait_ge(pt_ready, 16 + u)
                    if b == 0 and par == 0 and hp >= 1:
                        pe.wait_ge(ol_ready, 4 + hp)
                    g4 = (2 * hp + par) // 4
                    vs = slice(64, 192) if par == 0 else slice(0, P)
                    keys = [(avz2[0:META, 0, g4, vs], pt[0:META, 0:P])]
                    keys += [(avz2[:, 1 + t, g4, vs], pt[:, P + P * t:2 * P + P * t]) for t in range(b + 1)]
                    transposed_out(par, b, keys)

            pe.wait_ge(kd_ready, 1)
            for c in range(4):
                a, e = chunk(c)
                for t in range(2):
                    o = T * (c % 2) + P * t
                    ins = pe.transpose(wk[0:e - a, c // 2, o:o + P], kdT[:, t, a:e], ident)
                if c % 2:
                    ins.then_inc(kdt_ps, 1)
            for c in range(4):
                n = chunk(c)[1] - chunk(c)[0]
                pe.wait_ge(kdt_ready, c // 2 + 1)
                for t in range(2):
                    ins = pe.matmul(acc[:, c, T * t:T * t + T], kdtok[0:n, c, P * t:P * t + P],
                                    gvtok[0:n, c, T * t:T * t + T], start=True, stop=True)
                ins.then_inc(kv_ps, 1)
            pe.wait_ge(qk_ready, 1)
            for n, h in enumerate(HEADS):
                for c in range(4):
                    a, e = chunk(c + 1)
                    o = T * (n % 2) + 64 * c
                    ins = pe.matmul(wk[0:64, n // 2, o:o + 64], gkT[lanes(h), h // 2, a:e],
                                    gqT[lanes(h), h // 2, 64 * c:64 * c + 64], start=True, stop=True)
                if n % 2:
                    ins.then_inc(at_ps, 1)
            pe.wait_ge(st_ready, 4)
            for bank in range(2):
                pe.wait_ge(at_ready, bank + 1)
                for n in (2 * bank, 2 * bank + 1):
                    h = HEADS[n]
                    for c in range(4):
                        o = slice(T * (n % 2) + 64 * c, T * (n % 2) + 64 * c + 64)
                        pe.matmul(acc[:, bank, o], gvtok[:, c + 1, P * h:P * h + P], attm[:, n, c, :], start=True, stop=bank == 1)
                        ins = pe.matmul(acc[:, 3 * bank, o], St[lanes(h), c, h // 2, :],
                                        gqT[lanes(h), h // 2, 64 * c:64 * c + 64], start=bank == 1, stop=True)
                ins.then_inc(go_ps, 1)
            for n, src in enumerate((tA, tB)):
                pe.wait_ge(go_ready, n + 1)
                pe.matmul(wk[:, 2 + n, :], ones, src[:, :, 0:T], start=True, stop=True).then_inc(gss_ps, 1)

            pe.wait_ge(ol_ready, 8)
            for name, k0 in (("bra", 0), ("brb", 4)):
                if k0:
                    pe.wait_ge(ybl_ready, 4)
                for j in range(4):
                    s = j % 2
                    set_free(s, USE[name] + j // 2)
                    if name == "bra" and j == 0:
                        pe.wait_ge(grms, 2)
                    arrived(BASE[name], j)
                    for kk in range(4):
                        for m in range(2):
                            w = slice(256 * kk + P * m, 256 * kk + P * m + P)
                            ins = split_mm(acc[:, 2 * s + m, 0:T], hi[:, j, w], lo[:, j, w], mixH[:, k0 + kk, :],
                                           mixL[:, k0 + kk, :], kk == 0, kk == 3)
                    ins.then_inc(mm_done, 1)
            pairs("wout2", (lambda k: nH[:, k, 0:T], lambda k: nL[:, k, 0:T]), T, (mxl_ready, 0, 0.5))
            sum_squares(6, sq, T, lambda k: (sq_ready, 32 + k // 2 + 1))
            gate_up("gu2", 40, 0, T)
            down("dn2", 2, T)
            sum_squares(7, sq, T, lambda k: (sq_ready, 36 + k + 1))


_WEIGHTS = ["w_ada", "w_in", "w_out", "w_ffn_in", "w_ffn_out", "ffn1_w_gate_2", "ffn1_w_up_2", "ffn1_w_down_2", "w_in_2",
            "gla_gate_w_2", "w_branch_att_2", "w_branch_gla_2", "w_out_2", "ffn2_w_gate_2", "ffn2_w_up_2", "ffn2_w_down_2"]


def kernel(**inputs):
    import numpy as _np
    import concourse.bacc as _bacc
    from concourse import mybir as _mybir
    from concourse.bass_utils import run_bass_kernel_spmd as _run

    a = {n: _np.asarray(v) for n, v in inputs.items()}

    def cols(v):
        return v.reshape(-1, P).T

    def tokens(x):
        return x.reshape(-1, KD, P).transpose(2, 1, 0)

    def every(v):
        return _np.broadcast_to(v.reshape(1, -1), (P, v.size))

    norms = ("g_pre_mix", "g_post_mix", "g_pre_ffn", "g_post_ffn", "ffn1_norm_2", "mix_norm_2", "ffn2_norm_2", "final_norm_2")
    parts = [_np.stack([cols(a["c"]), cols(a["c_ctx"])], -1).reshape(P, -1), cols(a["b_ada"])]
    parts += [cols(a[n]) for n in norms]
    parts += [a["w_conv_qk"][0].T.reshape(4, P, 3).transpose(1, 0, 2).reshape(P, -1), cols(a["g_mlstm_out"])]
    parts += [cols(a["gla_gate_b_2"]), cols(a["gla_out_norm_2"])]
    parts += [every(a["attn_sink"]), every(a["att_sinks_2"]), _np.concatenate([a["b_gates"].reshape(16, 1), _np.zeros((P - 16, 1), _np.float32)])]
    host = {"vecs": _np.concatenate(parts, 1)}
    host["hT"] = tokens(_np.concatenate([a["meta_tokens_2"], a["x"][0]], 0))
    host["ctxT"] = tokens(a["ctx"][0])
    host["cst"], host["c1"], host["c2"], host["causal"] = shape_constants()
    for n in _WEIGHTS:
        host[n] = a[n][0]

    nc = _bacc.Bacc("TRN2", target_bir_lowering=False, num_devices=1)
    arrays, dr = {}, {}
    for n, v in host.items():
        v = _np.ascontiguousarray(v)
        arrays[f"in_{n}"] = v
        dr[n] = nc.dram_tensor(f"in_{n}", v.shape, _mybir.dt.from_np(v.dtype), kind="ExternalInput").ap()
    out = nc.dram_tensor("out_0", (P, KD, T), _mybir.dt.float32, kind="ExternalOutput").ap()
    program(nc, dr, out)
    r = _run(nc, [arrays], core_ids=[0])
    y = r.results[0]["out_0"]
    return _np.ascontiguousarray(y.transpose(2, 1, 0)).reshape(1, T, D)
```

```python
from contextlib import ExitStack

import numpy as np
import concourse.bass as bass
from concourse import mybir

F32 = mybir.dt.float32
F32R = mybir.dt.float32r
U32 = mybir.dt.uint32
ACT = mybir.ActivationFunctionType
ALU = mybir.AluOpType
ds = bass.ds

P = 128
D = 1024
KD = D // P
T = 256
L = 256
META = 16
TM = META + T
HID = 2816
KH = HID // P
EPS = 1e-6
BIG = 1e30
HD = 64
NHEAD = 8
HALF = KH // 2
SLOT = HALF * P
RING = 4
QS = -(HD ** -0.5)

V_C, V_BADA, V_NORM, V_CONV, V_GML, V_GB, V_GO = 0, 16, 64, 128, 140, 144, 146
V_SINK1, V_SINK2, V_BG, NV = 147, 155, 163, 164
N_PRE, N_POST, N_PREF, N_POSTF, N_F1, N_MIX, N_F2, N_FIN = range(8)

PHASES = [("ada1", 4), ("win0", 1), ("win1", 1), ("win2", 1), ("win3", 1), ("win4", 1), ("ada2", 7), ("wout", 2), ("ada3", 1),
          ("gu0", 11), ("dn0", 4), ("gu1", 11), ("dn1", 4), ("in2k", 5), ("in2g", 4), ("brb", 1), ("bra", 1),
          ("wout2", 2), ("gu2", 11), ("dn2", 4)]
ADA = ("ada1", "ada2", "ada3")
COUNT = dict(PHASES)
BASE, USE = {}, {}
RING_AT, BEFORE = {}, {}
_its, _use, _ring, _last = {True: 0, False: 0}, 0, 0, None
for _name, _n in PHASES:
    BASE[_name], USE[_name] = _its[_name in ADA], _use
    RING_AT[_name], BEFORE[_name] = _ring, _last
    _its[_name in ADA] += _n
    _ring += _n
    _last = _name
    if _name not in ADA:
        _use += _n * (2 if _name in ("bra", "brb") else 1)


def ring_lead(g):
    name = [n for n, _ in PHASES if n not in ADA and BASE[n] <= g][-1]
    return RING_AT[name] - BASE[name]


def shape_constants():
    f = np.float32
    p = np.arange(P)
    ident = np.eye(P, dtype=f)
    ones = np.ones((P, P), f)
    perm = np.zeros((P, P), f)
    for d in range(P):
        if d % 32 < 16:
            perm[d + 16, d] = -1.0
        else:
            perm[d - 16, d] = 1.0
    swap = np.zeros((P, P), f)
    swap[p, (p + HD) % P] = 1.0
    tok = np.arange(T)
    inv_freq = np.power(f(10000.0), -np.arange(16, dtype=f) / f(16)).astype(f)
    pos = np.where((p % HD < 32)[:, None], (tok // 64)[None, :], (tok % 64)[None, :]).astype(f)
    ang = (pos * inv_freq[p % 16][:, None]).astype(f)
    win = np.zeros((P, 2, 512), f)
    for b in range(2):
        q = b * P + p
        win[:, b, 0:T] = np.where(np.abs(q[:, None] - tok[None, :]) <= 128, 0.0, BIG)
    up = np.where(p[:, None] <= p[None, :], 0.0, BIG).astype(f)
    low = np.where(p[:, None] >= p[None, :], 0.0, BIG).astype(f)
    zero = np.zeros((P, P), f)
    ordf = np.concatenate([up, zero], 1)
    ordb = np.concatenate([zero, low], 1)
    sel = np.zeros((P, 4, P), f)
    for h in range(4):
        sel[h, h, :] = 1.0
    one_row = np.ones((P, 256), f)
    first = [a.reshape(P, -1) for a in (perm, np.cos(ang), np.sin(ang), win, ordf, ordb, low, sel, one_row)]
    dist = np.full((P, 2, TM), BIG, f)
    for b in range(2):
        q = b * P + p
        dist[:, b, 0:META] = 0.0
        gap = (q // 64)[:, None] - (tok // 64)[None, :]
        dist[:, b, META:] = np.where((gap >= 0) & (gap <= 2), np.abs(q[:, None] - tok[None, :]), BIG)
    reset = np.ones((P, TM), f)
    reset[:, [0] + [META + 64 * c for c in range(4)]] = 0.0
    second = [a.reshape(P, -1) for a in (dist, reset)]
    causal = np.zeros((P, 8, 64), np.uint32)
    causal[0:64] = (np.arange(64)[:, None] <= np.arange(64)[None, :])[:, None, :]
    cat = lambda xs: np.ascontiguousarray(np.concatenate(xs, 1).astype(f))
    return cat([ident, ones, swap]), cat(first), cat(second), causal


def program(nc, dr, out):
    with ExitStack() as root:
        def sbuf(stack, name, shape, dt=F32):
            return stack.enter_context(nc.sbuf_tensor(name, shape, dt))

        def sem(name):
            return root.enter_context(nc.semaphore(name))

        cst = sbuf(root, "cst", [P, 3 * P])
        ident, ones, swap = cst[:, 0:P], cst[:, P:2 * P], cst[:, 2 * P:3 * P]
        vec = sbuf(root, "vec", [P, NV])
        mods = sbuf(root, "mods", [P, 48, 2])
        gmod = sbuf(root, "gmod", [P, KD, 5])
        silu_c = sbuf(root, "silu_c", [P, 16])
        warm = sbuf(root, "warm", [1, 8])
        R = sbuf(root, "R", [P, KD, TM])
        raw = sbuf(root, "raw", [P, RING, SLOT])
        hi = sbuf(root, "hi", [P, RING, SLOT], F32R)
        lo = sbuf(root, "lo", [P, RING, SLOT], F32R)
        mixH = sbuf(root, "mixH", [P, KD, T], F32R)
        mixL = sbuf(root, "mixL", [P, KD, T], F32R)
        inv = sbuf(root, "inv", [P, 512])
        rms = sbuf(root, "rms", [P, 512])
        sinkn = sbuf(root, "sinkn", [P, 16])
        negm = sbuf(root, "negm", [P, 32])
        rsum = sbuf(root, "rsum", [P, 32])
        esink = sbuf(root, "esink", [P, 32])
        rinv = sbuf(root, "rinv", [P, 32])

        blk1 = ExitStack()
        c1 = sbuf(blk1, "c1", [P, 3072])
        o = 0
        def c1_take(n):
            nonlocal o
            o += n
            return c1[:, o - n:o]
        perm, cosT, sinT = c1_take(P), c1_take(T), c1_take(T)
        winmask = c1_take(1024).rearrange("p (b k) -> p b k", b=2)
        ordf, ordb, ordlow = c1_take(256), c1_take(256), c1_take(P)
        sel4 = c1_take(512).rearrange("p (h m) -> p h m", h=4)
        onerow = c1_take(256)
        kvraw = sbuf(blk1, "kvraw", [P, 2, 512])
        cinq = sbuf(blk1, "cinq", [P, 2, T + 2])
        cink = sbuf(blk1, "cink", [P, 2, 2, T + 2])
        mvT = sbuf(blk1, "mvT", [P, 4, 512])
        qT = sbuf(blk1, "qT", [P, 4, T])
        sgo = sbuf(blk1, "sgo", [P, 4, T])
        gt = sbuf(blk1, "gt", [16, 512])
        glog = sbuf(blk1, "glog", [16, 512])
        nrm1 = ExitStack()
        n5H = sbuf(nrm1, "n5H", [P, KD, 512], F32R)
        n5L = sbuf(nrm1, "n5L", [P, KD, 512], F32R)
        sq5 = sbuf(nrm1, "sq5", [P, KD, 512])
        ctxT = sbuf(nrm1, "ctxT", [P, KD, L])
        nrm1.close()
        mx1 = ExitStack()
        avz = sbuf(mx1, "avz", [P, 4, 2, 192])
        ktok = sbuf(mx1, "ktok", [P, 2, T])
        kw = sbuf(mx1, "kw", [P, 2, 2, T])
        hn = kw[:].rearrange("p d t e -> p d (t e)")
        Cst = sbuf(mx1, "Cst", [P, 4, 256])
        Sm = sbuf(mx1, "Sm", [P, 3, 512])
        pT = sbuf(mx1, "pT", [P, 2, 512])
        hT = sbuf(mx1, "hT", [P, 4, T])
        den1 = sbuf(mx1, "den1", [P, T])
        emt = sbuf(mx1, "emt", [P, 2, T])
        mq = sbuf(mx1, "mq", [P, 2, T])
        mk = sbuf(mx1, "mk", [P, 2, 512])
        kT = sbuf(mx1, "kT", [P, 512])
        kTs = sbuf(mx1, "kTs", [P, 512])
        vtok = sbuf(mx1, "vtok", [P, 4, 512])
        bR = sbuf(mx1, "bR", [4, 2, 512])
        rR = sbuf(mx1, "rR", [4, 2, 512])
        MR = sbuf(mx1, "MR", [4, 2, 512])
        m0 = sbuf(mx1, "m0", [4, 2])
        D16 = sbuf(mx1, "D16", [4, 16])
        rcol = sbuf(mx1, "rcol", [P, 4, 8])
        bc16 = sbuf(mx1, "bc16", [P, 16])
        wkx = sbuf(mx1, "wkx", [P, 2, 8])
        t1 = sbuf(mx1, "t1", [P, 2, T])
        row1 = mvT[0:2, :, :]
        zE = mvT[:, 0, 0:384]
        Aw = mvT[:, 1, 0:384]
        wint = mvT[:, 2, 0:T]
        qw = t1
        row2 = mvT[0:1, 3, :]
        mx1.close()
        blk1.close()

        ffn = ExitStack()
        nH = sbuf(ffn, "nH", [P, KD, TM], F32R)
        nL = sbuf(ffn, "nL", [P, KD, TM], F32R)
        ffn2 = ExitStack()
        sq = sbuf(ffn2, "sq", [P, KD, TM])
        Y = sbuf(ffn2, "Y", [P, KD, T])
        xg = sbuf(ffn2, "xg", [P, KD, TM])
        gH = sbuf(ffn2, "gH", [P, KH, TM], F32R)
        gL = sbuf(ffn2, "gL", [P, KH, TM], F32R)
        sg = sbuf(ffn2, "sg", [P, 2, TM])
        hbuf = sbuf(ffn2, "hbuf", [P, 2, TM])
        ffn2.close()
        blk2 = ExitStack()
        c2 = sbuf(blk2, "c2", [P, 3 * TM])
        dist = c2[:, 0:2 * TM].rearrange("p (b k) -> p b k", b=2)
        reset = c2[:, 2 * TM:3 * TM]
        causal = sbuf(blk2, "causal", [P, 8, 64], U32)
        gatew = sbuf(blk2, "gatew", [16, 256])
        glT = sbuf(blk2, "glT", [16, TM])
        kvraw2 = sbuf(blk2, "kvraw2", [P, 2, TM])
        gkT = sbuf(blk2, "gkT", [P, 2, TM])
        gqT = sbuf(blk2, "gqT", [P, 2, T])
        gvT = sbuf(blk2, "gvT", [P, 4, TM])
        qT2 = sbuf(blk2, "qT2", [P, 4, T])
        grT = sbuf(blk2, "grT", [P, 4, T])
        gab = sbuf(blk2, "gab", [P, 2 * KD, T])
        tA = sbuf(blk2, "tA", [P, 2, TM])
        tB = sbuf(blk2, "tB", [P, 2, TM])
        tC = sbuf(blk2, "tC", [P, 2, TM])
        blast = sbuf(blk2, "blast", [P, 2, 4])
        kdT = sbuf(blk2, "kdT", [P, 2, TM])
        kS2 = sbuf(blk2, "kS2", [P, TM])
        avz2 = sbuf(blk2, "avz2", [P, 3, 2, 192])
        gvtok = sbuf(blk2, "gvtok", [64, 5, 512])
        kdtok = sbuf(blk2, "kdtok", [64, 4, 256])
        St = sbuf(blk2, "St", [P, 4, 2, P])
        attm = sbuf(blk2, "attm", [64, 4, 4, 64])
        bias2 = sbuf(blk2, "bias2", [P, 2, 2, TM])
        Sm2 = sbuf(blk2, "Sm2", [P, 2, TM])
        pT2 = sbuf(blk2, "pT2", [P, 2, 384])
        og = gvT
        blk2.close()
        ffn.close()

        acc = root.enter_context(nc.psum_tensor("acc", [P, 4, 512], F32))
        wk = root.enter_context(nc.psum_tensor("wk", [P, 4, 512], F32))

        vec_in, tok_in, cst_in, c1_in, c2_in = (sem(n) for n in ("vec_in", "tok_in", "cst_in", "c1_in", "c2_in"))
        raw_ready = [sem(f"raw_ready{j}") for j in range(RING)]
        hi_ready, lo_ready = sem("hi_ready"), sem("lo_ready")
        mm_done = sem("mm_done")
        acc_free = [sem("acc_free0"), sem("acc_free1")]
        act_chain, dve_chain = sem("act_chain"), sem("dve_chain")
        silu_ready = sem("silu_ready")
        ada_done, ada_row, ada_cols, ada_used = sem("ada_done"), sem("ada_row"), sem("ada_cols"), sem("ada_used")
        sq5_sum = sem("sq5_sum")
        sq_ready, ssq_ps, rms_ready = sem("sq_ready"), sem("ssq_ps"), sem("rms_ready")
        xn_ready, nh_ready, nl_ready = sem("xn_ready"), sem("nh_ready"), sem("nl_ready")
        y_scaled, r_ready = sem("y_scaled"), sem("r_ready")
        gh_ready, gl_ready = sem("gh_ready"), sem("gl_ready")
        sg_ready, half_added = sem("sg_ready"), sem("half_added")
        mx_sum, mxh_ready, mxl_ready = sem("mx_sum"), sem("mxh_ready"), sem("mxl_ready")
        out_ready, out_sent = sem("out_ready"), sem("out_sent")
        pads, zero2, bias_ready = sem("pads"), sem("zero2"), sem("bias_ready")
        s_ps, s_max, p_exp, p_norm = sem("s_ps"), sem("s_max"), sem("p_exp"), sem("p_norm")
        pt_ps, pt_ready, o_ps, oh_ready, ol_ready = (sem(n) for n in ("pt_ps", "pt_ready", "o_ps", "oh_ready", "ol_ready"))
        gt_log, lf_ready, rows_ps, rows_ready = sem("gt_log"), sem("lf_ready"), sem("rows_ps"), sem("rows_ready")
        wk_arg, wk_ready = sem("wk_arg"), sem("wk_ready")
        rope_ps, rope_ready, avt_ps, avz_ready = sem("rope_ps"), sem("rope_ready"), sem("avt_ps"), sem("avz_ready")
        mvt_ps, vtok_ready, conv_ready, mqk_ready = sem("mvt_ps"), sem("vtok_ready"), sem("conv_ready"), sem("mqk_ready")
        kt_ps, ktok_ready, ks_ps, ks_ready = sem("kt_ps"), sem("ktok_ready"), sem("ks_ps"), sem("ks_ready")
        kw_ready, cst_ps, cst_ready = sem("kw_ready"), sem("cst_ps"), sem("cst_ready")
        ms_ps, mb_ps, mw_ready, z_ready, e_ready = (sem(n) for n in ("ms_ps", "mb_ps", "mw_ready", "z_ready", "e_ready"))
        a_ready, qw_ready, nd_ps, nd_used = sem("a_ready"), sem("qw_ready"), sem("nd_ps"), sem("nd_used")
        hsum_ready, hsq_ready, hss_ps, hrms = sem("hsum_ready"), sem("hsq_ready"), sem("hss_ps"), sem("hrms")
        mlo_ready, mlh_ready, mll_ready = sem("mlo_ready"), sem("mlh_ready"), sem("mll_ready")
        z_ps, z_abs, z_ln, b_ready, eb_ready = (sem(n) for n in ("z_ps", "z_abs", "z_ln", "b_ready", "eb_ready"))
        bl_ready, ed_ready, kd_ready, qk_ready = sem("bl_ready"), sem("ed_ready"), sem("kd_ready"), sem("qk_ready")
        gvt_ps, gvt_ready, kdt_ps, kdt_ready = sem("gvt_ps"), sem("gvt_ready"), sem("kdt_ps"), sem("kdt_ready")
        kv_ps, st_ready, at_ps, at_ready = sem("kv_ps"), sem("st_ready"), sem("at_ps"), sem("at_ready")
        go_cross = sem("go_cross")
        go_ps, go_sum, go_ready, gss_ps, grms = sem("go_ps"), sem("go_sum"), sem("go_ready"), sem("gss_ps"), sem("grms")
        yb_ready, ybh_ready, ybl_ready = sem("yb_ready"), sem("ybh_ready"), sem("ybl_ready")
        gr_ready = sem("gr_ready")
        gates_ready = sem("gates_ready")
        ks2_ps, ks2_ready, av2_ps, av2_ready = sem("ks2_ps"), sem("ks2_ready"), sem("av2_ps"), sem("av2_ready")

        GV_BANKS = [wk[:, 2 + c % 2, :] for c in range(5)]
        KV_BANKS = [wk[:, (3 + c) % 4, :] for c in range(4)]
        GO_BANKS = [wk[:, 3, :], wk[:, 0, :]]
        GO_CROSS = wk[:, 1, :]
        MV_BANKS = {2: wk[:, 0, :], 3: wk[:, 1, :], 0: wk[:, 2, :], 1: wk[:, 3, :]}
        CST_BANKS = [wk[:, 1, :], wk[:, 2, :], acc[:, 2, :], acc[:, 3, :]]
        ND_BANK = [acc[:, 3, :], acc[:, 2, :]]
        HEADS = (0, 2, 1, 3)
        ADA_BANK = [acc[:, 3, :]] * 7 + [wk[:, 3, :]]
        UNITS = [(hp, b, par) for hp in range(4) for b in range(2) for par in range(2)]

        def chunk(c):
            return (0, META) if c == 0 else (META + 64 * (c - 1), META + 64 * c)

        def lanes(h):
            return slice(HD * (h % 2), HD * (h % 2) + HD)

        def order(v):
            h, d = divmod(v, 2)
            return h, d, (0, 1, P) if d == 0 else (1, 0, 0)

        block = root.enter_context(nc.Block())

        @block.sync
        def _(sp):
            def freed(name, i, j):
                before = BEFORE[name] if isinstance(i, int) and i == 0 else name
                if before:
                    last = BASE[before] + (COUNT[before] if before != name else i)
                    sp.wait_ge(ada_done if before in ADA else lo_ready, 4 * last + j - 3)

            def load(name, i, j, src):
                freed(name, i, j)
                w = 1
                for n in src.shape[1:]:
                    w *= n
                dst = raw[:, j, 0:w].rearrange("p (k m) -> p k m", m=src.shape[2])
                sp.dma_start(dst, src).then_inc(raw_ready[j], 16)

            def panel(w, col, q, width=256):
                return w[512 * q:512 * q + 512, ds(col, width)].rearrange("(k p) m -> p k m", p=P)

            def columns(name, i, w, cols):
                for j in range(4):
                    load(name, i, j, panel(w, cols[j // 2], j % 2))

            def ada(name, i, col):
                for j in range(4):
                    load(name, i, j, dr["w_ada"][256 * j:256 * j + 256, ds(col, 512)].rearrange("(k p) m -> p k m", p=P))

            def down(name, w):
                with sp.Fori(0, COUNT[name]) as i:
                    for j in range(4):
                        rows = w[SLOT * (j % 2):SLOT * (j % 2) + SLOT, ds(256 * i + P * (j // 2), P)]
                        load(name, i, j, rows.rearrange("(k p) m -> p k m", p=P))

            def gate_up(name, wg, wu, up0, behind_ada=False):
                def iteration(i):
                    for j in range(4):
                        load(name, i, j, panel(wg, 256 * i, j) if j < 2 else panel(wu, 256 * i + up0, j - 2))
                if behind_ada:
                    iteration(0)
                with sp.Fori(int(behind_ada), COUNT[name]) as i:
                    iteration(i)

            for i in range(COUNT["ada1"]):
                ada("ada1", i, 512 * i)
            w = dr["w_in"]
            load("win0", 0, 0, panel(w, 512, 0))
            load("win0", 0, 1, panel(w, 512, 1))
            load("win0", 0, 2, panel(w, 2304, 0, 16))
            load("win0", 0, 3, panel(w, 2304, 1, 16))
            for n, cols in enumerate(((768, 1024), (1280, 1536), (0, 256), (1792, 2048))):
                columns(f"win{n + 1}", 0, w, cols)
            ada("ada2", 0, 2048)
            with sp.Fori(1, COUNT["ada2"]) as i:
                ada("ada2", i, 512 * i + 2048)
            for i in range(COUNT["wout"]):
                for j in range(4):
                    load("wout", i, j, panel(dr["w_out"], 512 * i + 256 * (j // 2), (j + 1) % 2))
            ada("ada3", 0, 512 * COUNT["ada2"] + 2048)
            gate_up("gu0", dr["w_ffn_in"], dr["w_ffn_in"], HID, True)
            down("dn0", dr["w_ffn_out"])
            gate_up("gu1", dr["ffn1_w_gate_2"], dr["ffn1_w_up_2"], 0)
            down("dn1", dr["ffn1_w_down_2"])
            w = dr["w_in_2"]
            load("in2k", 0, 0, panel(w, 2304, 0, 16))
            load("in2k", 0, 1, panel(w, 2304, 1, 16))
            load("in2k", 0, 2, panel(w, 512, 0))
            load("in2k", 0, 3, panel(w, 512, 1))
            for n, cols in enumerate(((1024, 768), (1280, 1536), (0, 256), (1792, 2048))):
                columns("in2k", 1 + n, w, cols)
            with sp.Fori(0, COUNT["in2g"]) as i:
                columns("in2g", i, w, (512 * i + 2320, 512 * i + 2576))
            for name, wb in (("brb", dr["w_branch_gla_2"]), ("bra", dr["w_branch_att_2"])):
                for j in range(4):
                    load(name, 0, j, panel(wb, 256 * j, 0))
            with sp.Fori(0, COUNT["wout2"]) as i:
                columns("wout2", i, dr["w_out_2"], (512 * i, 512 * i + 256))
            gate_up("gu2", dr["ffn2_w_gate_2"], dr["ffn2_w_up_2"], 0)
            down("dn2", dr["ffn2_w_down_2"])
            for k in range(KD):
                sp.wait_ge(out_ready, k + 1)
                sp.dma_start(out[:, k, :], Y[:, k, :]).then_inc(out_sent, 16)
            sp.wait_ge(out_sent, 16 * KD)

        @block.gpsimd
        def _(pool):
            pool.memset(cinq[:], 0.0)
            pool.memset(cink[:], 0.0).then_inc(pads, 1)
            pool.wait_ge(mm_done, 4 * BASE["win4"] + 4)
            pool.memset(avz[:], 0.0).then_inc(pads, 1)
            pool.wait_ge(mm_done, 4 * BASE["in2k"] + 4)
            pool.dma_start(c2[:], dr["c2"]).then_inc(c2_in, 16)
            pool.dma_start(causal[:], dr["causal"]).then_inc(c2_in, 16)
            pool.dma_start(gatew[:], dr["gla_gate_w_2"]).then_inc(c2_in, 16)
            pool.memset(avz2[:], 0.0)
            pool.memset(attm[:], 0.0).then_inc(zero2, 1)
            pool.wait_ge(c2_in, 48)
            for h in range(NHEAD):
                if h >= 2:
                    pool.wait_ge(s_max, 16 + 4 * (h // 2 - 1) + 2 + h % 2 + 1)
                pool.tensor_scalar(bias2[:, h % 2], dist, 2.0 ** -(h + 1), None, ALU.mult).then_inc(bias_ready, 1)

        @block.scalar
        def _(act):
            chain = 0

            def link(ins):
                nonlocal chain
                chain += 1
                ins.then_inc(act_chain, 1)
                act.wait_ge(act_chain, chain)

            def split(g, j, width, lead):
                act.wait_ge(raw_ready[j], 16 * (g + lead) + 16)
                if not (isinstance(g, int) and g == 0):
                    act.wait_ge(mm_done, 4 * g + j - 3)
                act.activation(hi[:, j, 0:width], raw[:, j, 0:width], ACT.Copy).then_inc(hi_ready, 1)

            def pipeline(name, width, evac, ahead, evac_first=False, silu=False, behind=((0,), (1,), (2,), (3,))):
                first, n = BASE[name], COUNT[name]
                if n > 1:
                    with act.Fori(1, n) as i:
                        if silu:
                            act.activation(warm[:, 7:8], ident[0:1, 0:1], ACT.Silu)
                        for j in range(4):
                            split(first + i, j, width, ring_lead(first))
                            evac(i - 1, j)
                for j in range(4):
                    if evac_first or j % 2:
                        evac(n - 1, j)
                    for q in behind[j]:
                        if ahead and ahead[q]:
                            split(first + n, q, ahead[q], ring_lead(first + n))
                    if not evac_first and j % 2 == 0:
                        evac(n - 1, j)

            K4 = [1024] * 4
            DN = [SLOT] * 4
            MG = [64, 64, 1024, 1024]
            WG = [1024, 1024, 64, 64]

            def nothing(i, j):
                pass

            def multiplied(name, i, j):
                act.wait_ge(mm_done, 4 * (BASE[name] + i) + j + 1)

            act.dma_start(vec[:], dr["vecs"]).then_inc(vec_in, 16)
            act.dma_start(R[:], dr["hT"]).then_inc(tok_in, 16)
            act.dma_start(ctxT[:], dr["ctxT"]).then_inc(tok_in, 16)
            act.dma_start(cst[:], dr["cst"]).then_inc(cst_in, 16)

            act.wait_ge(vec_in, 16)
            act.activation(silu_c[:], vec[:, V_C:V_C + 16], ACT.Silu).then_inc(silu_ready, 1)
            act.wait_ge(tok_in, 32)
            for k in range(0, KD, 2):
                act.activation(sq5[:, k:k + 2, 0:T], R[:, k:k + 2, META:TM], ACT.Square).then_inc(sq_ready, 1)
                act.activation(sq5[:, k:k + 2, T:512], ctxT[:, k:k + 2, :], ACT.Square).then_inc(sq_ready, 1)

            def load_sqrt(n):
                act.activation(warm[:, n:n + 1], ident[0:1, 0:1], ACT.Sqrt)

            def norm_rms(n, width):
                act.wait_ge(ssq_ps, n + 1)
                act.activation(rms[:, 0:width], wk[:, 0, 0:width], ACT.Sqrt, bias=EPS,
                               scale=1.0 / D).then_inc(rms_ready, 1)

            norm_rms(0, 512)
            for a in range(4):
                if a == 3:
                    split(0, 0, 1024, ring_lead(0))
                act.wait_ge(ada_done, 4 * a + 4)
                act.activation(row1[:, a, :], acc[0:2, a, :], ACT.Copy).then_inc(ada_row, 1)
            for n in range(2 * KD):
                k, c = divmod(n, 2)
                if n == 6:
                    split(0, 1, 1024, ring_lead(0))
                act.wait_ge(xn_ready, n + 1)
                act.activation(n5H[:, k, T * c:T * c + T], sq5[:, k, T * c:T * c + T], ACT.Copy).then_inc(nh_ready, 1)
            for j in (2, 3):
                split(0, j, WG[j], ring_lead(0))
            act.dma_start(c1[:], dr["c1"]).then_inc(c1_in, 16)

            def evac_win0(i, j):
                if j == 1:
                    multiplied("win0", i, j)
                    act.activation(kvraw[:], acc[:, 0:2, :], ACT.Copy).then_inc(acc_free[0], 1)
                if j == 3:
                    multiplied("win0", i, j)
                    act.activation(gt[:], acc[0:16, 2, :], ACT.Identity, bias=vec[0:16, V_BG:V_BG + 1])
                    act.activation(glog[:], acc[0:16, 2, :], ACT.Abs, bias=vec[0:16, V_BG:V_BG + 1]).then_inc(acc_free[1], 1)
                    act.wait_ge(acc_free[1], USE["win0"] + 1)

            def evac_win1(i, j):
                if j == 1:
                    multiplied("win1", i, j)
                    act.wait_ge(pads, 1)
                    act.activation(cinq[:, :, 1:T + 1], acc[:, 0:2, 0:T], ACT.Copy).then_inc(acc_free[0], 1)

            def evac_win2(i, j):
                if j == 1:
                    multiplied("win2", i, j)
                    act.activation(mvT[:, 0:2, :], acc[:, 0:2, :], ACT.Copy).then_inc(acc_free[0], 1)

            def evac_win3(i, j):
                if j == 1:
                    multiplied("win3", i, j)
                    act.activation(qT[:, 0:2, :], acc[:, 0:2, 0:T], ACT.Copy, scale=QS).then_inc(acc_free[0], 1)

            def evac_win4(i, j):
                if j in (1, 3):
                    multiplied("win4", i, j)
                    act.activation(sgo[:, j - 1:j + 1, :], acc[:, j - 1:j + 1, 0:T],
                                   ACT.Sigmoid).then_inc(acc_free[j // 2], 1)

            pipeline("win0", 1024, evac_win0, K4)
            link(act.activation(glog[:], glog[:], ACT.Exp, scale=-1.0))
            act.activation(glog[:], glog[:], ACT.Ln, bias=1.0).then_inc(gt_log, 1)
            pipeline("win1", 1024, evac_win1, K4)
            pipeline("win2", 1024, evac_win2, K4)
            for n, a in enumerate((mk[:, 0, :], mk[:, 1, :], mq[:, 0, :], mq[:, 1, :])):
                act.wait_ge(conv_ready, n + 1)
                act.activation(a, a, ACT.Silu).then_inc(mqk_ready, 1)
            pipeline("win3", 1024, evac_win3, K4)
            pipeline("win4", 1024, evac_win4, None)

            act.wait_ge(kt_ps, 1)
            act.wait_ge(mm_done, 4 * BASE["win4"] + 4)
            act.activation(ktok[:], wk[:, 3, :].rearrange("p (t d) -> p t d", t=2), ACT.Copy).then_inc(ktok_ready, 1)
            act.wait_ge(wk_arg, 1)
            act.activation(wkx[:], wkx[:], ACT.Exp).then_inc(wk_ready, 1)
            for n, t in enumerate((2, 3, 0, 1)):
                act.wait_ge(mvt_ps, n + 1)
                act.activation(vtok[:, t, :], MV_BANKS[t], ACT.Copy).then_inc(vtok_ready, 1)
            act.wait_ge(pads, 2)
            act.wait_ge(avt_ps, 1)
            act.activation(avz[:, :, :, 64:128], acc[:, 0, :].rearrange("p (t g d) -> p t g d", t=4, g=2),
                           ACT.Copy).then_inc(avz_ready, 1)
            act.wait_ge(ks_ps, 1)
            act.activation(kTs[:], acc[:, 1, :], ACT.Copy).then_inc(ks_ready, 1)

            def exp_scores(n, sm, sink):
                act.wait_ge(s_max, n + 1)
                act.activation(sm, sm, ACT.Exp, bias=negm[:, n:n + 1], scale=-1.0, accum_out=rsum[:, n:n + 1])
                act.activation(esink[:, n:n + 1], sink, ACT.Exp, bias=negm[:, n:n + 1], scale=-1.0).then_inc(p_exp, 1)

            def heads_out(n, hp):
                act.wait_ge(o_ps, n + 1)
                act.activation(mixH[:, hp, :], wk[:, 3, 0:T], ACT.Copy).then_inc(oh_ready, 1)

            def ada_row2(a):
                act.wait_ge(ada_done, 16 + 4 * a + 4)
                act.activation(row2, ADA_BANK[a][0:1, :], ACT.Copy).then_inc(ada_row, 1)

            for u in range(18):
                if 1 <= u <= 8:
                    act.wait_ge(z_ready, u)
                    act.activation(zE, zE, ACT.Exp, scale=-1.0).then_inc(e_ready, 1)
                if u >= 2 and (u - 2) % 4 == 3:
                    heads_out((u - 2) // 4, (u - 2) // 4)
                if 1 <= u <= 16:
                    act.wait_ge(pt_ps, u)
                    act.activation(pT[:, (u - 1) % 2, :], wk[:, 2, :], ACT.Copy).then_inc(pt_ready, 1)
                if u < 8:
                    v = u
                    h, d, _ = order(v)
                    act.wait_ge(mb_ps, v + 1)
                    if v >= 1:
                        act.wait_ge(qw_ready, v)
                    if v >= 2:
                        act.wait_ge(nd_used, v - 1)
                    act.activation(wint[lanes(h), :], acc[lanes(h), 1, 0:T], ACT.Exp, scale=-1.0,
                                   bias=bc16[lanes(h), 8 + 4 * d + h:9 + 4 * d + h])
                    act.activation(emt[:, v % 2, :], acc[:, 1, T:512], ACT.Exp, scale=-1.0).then_inc(mw_ready, 1)
                if u < 16:
                    hp, b, par = UNITS[u]
                    exp_scores(u, Sm[:, u % 3, :], sinkn[:, 2 * hp + par:2 * hp + par + 1])
                if 8 <= u < 15:
                    ada_row2(u - 8)
                if u in (10, 11):
                    hp = u - 10
                    act.wait_ge(hsum_ready, 2 * hp + 2)
                    act.activation(hn[:, hp, :], hT[:, 2 * hp:2 * hp + 2, :].rearrange("p h t -> p (h t)"),
                                   ACT.Square).then_inc(hsq_ready, 1)
                if u == 12:
                    for hp in range(2):
                        act.wait_ge(hss_ps, hp + 1)
                        act.activation(hn[:, hp, :], acc[:, hp, :], ACT.Sqrt, bias=EPS, scale=1.0 / P).then_inc(hrms, 1)
                if u == 15:
                    for h in range(4):
                        act.wait_ge(mlo_ready, h + 1)
                        act.activation(mixH[:, 4 + h, :], hT[:, h, :], ACT.Copy).then_inc(mlh_ready, 1)
                if u >= 16:
                    for j in (2 * u - 32, 2 * u - 31):
                        split(BASE["wout"], j, 1024, ring_lead(BASE["wout"]))

            def copy_square(name, i, s, n, width):
                act.activation(Y[:, n, :], acc[:, 2 * s:2 * s + width, 0:T], ACT.Copy)
                act.activation(sq[:, n, 0:T], acc[:, 2 * s:2 * s + width, 0:T], ACT.Square).then_inc(acc_free[s], 1)

            def evac_wout(i, j):
                if j in (1, 3):
                    multiplied("wout", i, j)
                    copy_square("wout", i, j // 2, ds(4 * i + j - 1, 2), 2)

            def evac_dn0(i, j):
                if j in (1, 3):
                    multiplied("dn0", i, j)
                    copy_square("dn0", i, j // 2, ds(2 * i + j // 2, 1), 1)

            def square_r(k, width, t0, wait):
                act.wait_ge(*wait)
                act.activation(sq[:, k, 0:width], R[:, k, t0:t0 + width], ACT.Square).then_inc(sq_ready, 1)

            def gate_up(name, f, width, ahead):
                def evac(i, j):
                    if j == 1:
                        multiplied(name, i, j)
                        act.wait_ge(acc_free[1], USE[name] + i)
                        act.activation(sg[:, :, 0:width], acc[:, 0:2, 0:width], ACT.Silu).then_inc(acc_free[0], 1)
                    if j == 3:
                        act.wait_ge(acc_free[1], USE[name] + i + 1)
                        act.activation(gH[:, ds(2 * i, 2), 0:width], hbuf[:, :, 0:width], ACT.Copy).then_inc(gh_ready, 1)
                pipeline(name, 1024, evac, ahead, silu=True, behind=((0,), (1,), (), (2, 3)))

            def normed(first, width, shift, weights):
                for k in range(KD):
                    act.wait_ge(xn_ready, first + k + 1)
                    act.activation(nH[:, k, 0:width], sq[:, k, 0:width], ACT.Identity,
                                   bias=mods[:, shift + k, 0:1]).then_inc(nh_ready, 1)
                    if k >= 6:
                        split(weights, k - 4, 1024, ring_lead(weights))

            def gate_up_scaled(name, f, width, ahead):
                def evac(i, j):
                    if j == 1:
                        act.wait_ge(acc_free[0], USE[name] + i + 1)
                        act.activation(sg[:, :, 0:width], sg[:, :, 0:width], ACT.Silu).then_inc(sg_ready, 1)
                    if j == 3:
                        act.wait_ge(acc_free[1], USE[name] + i + 1)
                        act.activation(gH[:, ds(2 * i, 2), 0:width], hbuf[:, :, 0:width], ACT.Copy).then_inc(gh_ready, 1)
                pipeline(name, 1024, evac, ahead, silu=True, behind=((0,), (1,), (), (2, 3)))

            def upper(n, k, width, t0, updated):
                act.wait_ge(*updated)
                act.activation(nH[:, k, 0:width], R[:, k, t0:t0 + width], ACT.Copy,
                               scale=vec[:, V_NORM + KD * n + k:V_NORM + KD * n + k + 1]).then_inc(nh_ready, 1)

            load_sqrt(0)
            pipeline("wout", 1024, evac_wout, None, True)
            norm_rms(1, T)
            for k in range(KD):
                square_r(k, T, META, (r_ready, k + 1))
                if k in (2, 7):
                    split(BASE["gu0"], k // 7, 1024, ring_lead(BASE["gu0"]))
            norm_rms(2, T)
            ada_row2(7)
            normed(16, T, 24, BASE["gu0"])
            gate_up("gu0", 0, T, DN)
            load_sqrt(1)
            pipeline("dn0", SLOT, evac_dn0, K4[0:3] + [None], True)
            norm_rms(3, T)
            for k in range(KD):
                upper(N_F1, k, TM, 0, (r_ready, KD + k + 1))
                square_r(k, TM, 0, (r_ready, 8 + k + 1))
            split(BASE["gu1"], 3, 1024, ring_lead(BASE["gu1"]))
            norm_rms(4, TM)
            gate_up_scaled("gu1", 1, TM, DN)

            def evac_dn(added, width, t0):
                def evac(i, j):
                    if j in (1, 3):
                        square_r(ds(2 * i + j // 2, 1), width, t0, (half_added, added + 2 * i + j // 2 + 1))
                return evac

            load_sqrt(2)
            pipeline("dn1", SLOT, evac_dn(0, TM, 0), MG[0:3] + [None], True)
            for k in range(KD):
                upper(N_MIX, k, TM, 0, (half_added, k + 1))
            split(BASE["in2k"], 3, 1024, ring_lead(BASE["in2k"]))
            norm_rms(5, TM)

            def decay_logs():
                act.wait_ge(z_ps, 1)
                for t in range(2):
                    ins = act.activation(tA[:, t, :], wk[:, t, 0:TM], ACT.Abs, bias=vec[:, V_GB + t:V_GB + t + 1])
                ins.then_inc(z_abs, 1)
                act.wait_ge(z_abs, 1)
                link(act.activation(tA[:], tA[:], ACT.Exp, scale=-1.0))
                act.activation(tA[:], tA[:], ACT.Ln, bias=1.0).then_inc(z_ln, 1)

            def attention_keys():
                act.wait_ge(zero2, 1)
                act.wait_ge(av2_ps, 1)
                act.activation(avz2[0:META, 0, :, 64:128], wk[0:META, 2, 0:P].rearrange("p (g d) -> p g d", g=2), ACT.Copy)
                act.activation(avz2[:, 1:3, :, 64:128], wk[:, 2, P:3 * P].rearrange("p (t g d) -> p t g d", t=2, g=2),
                               ACT.Copy).then_inc(av2_ready, 1)
                act.wait_ge(ks2_ps, 1)
                act.activation(kS2[:], wk[:, 3, 0:TM], ACT.Copy).then_inc(ks2_ready, 1)

            def values(c):
                act.wait_ge(gvt_ps, c + 1)
                n = chunk(c)[1] - chunk(c)[0]
                act.activation(gvtok[0:n, c, :], GV_BANKS[c][0:n, :], ACT.Copy).then_inc(gvt_ready, 1)

            def decays():
                act.wait_ge(b_ready, 1)
                act.activation(tA[:], tC[:], ACT.Exp, scale=1.0 / 16)
                act.activation(tB[:], tC[:], ACT.Exp, scale=-1.0 / 16).then_inc(eb_ready, 1)

            def decays_to_last():
                act.wait_ge(bl_ready, 1)
                act.activation(tC[:, :, 0:208], tC[:, :, 0:208], ACT.Exp, scale=-1.0 / 16).then_inc(ed_ready, 1)

            def keys_by_token():
                act.wait_ge(kdt_ps, 1)
                act.activation(kdtok[0:META, 0, :], wk[0:META, 0, 0:T], ACT.Copy)
                act.activation(kdtok[:, 1, :], wk[0:64, 0, T:512], ACT.Copy).then_inc(kdt_ready, 1)
                act.wait_ge(kdt_ps, 2)
                act.activation(kdtok[:, 2:4, :], wk[0:64, 1, :].rearrange("p (c d) -> p c d", c=2),
                               ACT.Copy).then_inc(kdt_ready, 1)

            steps = {(1, 3): (decay_logs, attention_keys), (2, 1): (decays,), (2, 3): (decays_to_last,), (3, 1): (keys_by_token,),
                     (3, 3): (lambda: values(0), lambda: values(1)), (4, 1): (lambda: values(2), lambda: values(3))}
            for i in range(COUNT["in2k"]):
                for j in range(4):
                    split(BASE["in2k"] + i + 1, j, 1024, ring_lead(BASE["in2k"]))
                    for step in steps.get((i, j), ()):
                        step()

            def gates_split(n):
                split(BASE["in2g"] + n // 4, n % 4, 1024, ring_lead(BASE["in2g"]))

            values(4)
            for s in range(2):
                act.wait_ge(acc_free[s], USE["in2g"])
                act.activation(grT[:, 2 * s:2 * s + 2, :], grT[:, 2 * s:2 * s + 2, :], ACT.Silu).then_inc(gr_ready, 1)
            gates_split(4)
            gates_split(5)
            gsq = (tA, tB)
            grt = (tC, kdT)
            act.wait_ge(go_ps, 1)
            act.activation(og[:, 0:2, 0:T], GO_BANKS[0].rearrange("p (h t) -> p h t", h=2), ACT.Copy)
            act.activation(gsq[0][:, :, 0:T], GO_BANKS[0].rearrange("p (h t) -> p h t", h=2), ACT.Square).then_inc(go_ready, 1)
            act.wait_ge(go_ps, 2)
            act.activation(og[:, 2:4, 0:T], GO_BANKS[1].rearrange("p (h t) -> p h t", h=2), ACT.Copy).then_inc(go_cross, 1)
            act.wait_ge(go_sum, 1)
            act.activation(gsq[1][:, :, 0:T], og[:, 2:4, 0:T], ACT.Square).then_inc(go_ready, 1)
            for n in range(2):
                act.wait_ge(gss_ps, n + 1)
                act.activation(grt[n][:, :, 0:T], wk[:, 2 + n, :].rearrange("p (h t) -> p h t", h=2), ACT.Sqrt, bias=EPS,
                               scale=1.0 / P).then_inc(grms, 1)

            def sigmoid(half):
                for s in range(2):
                    act.wait_ge(acc_free[s], USE["in2g"] + 2 * half + 2)
                g = gab[:, KD * half:KD * half + KD, :]
                act.activation(g, g, ACT.Sigmoid).then_inc(gates_ready, 1)

            for u in range(18):
                w = u - 2
                if w >= 0:
                    b = UNITS[w][1]
                    act.wait_ge(pt_ps, 16 + w + 1)
                    act.activation(pT2[0:META, w % 2, 0:P], wk[0:META, 2, 0:P], ACT.Copy)
                    act.activation(pT2[:, w % 2, P:P * (b + 2)], wk[:, 2, P:P * (b + 2)], ACT.Copy).then_inc(pt_ready, 1)
                if u < 16:
                    hp, b, par = UNITS[u]
                    nk = META + P * (b + 1)
                    exp_scores(16 + u, Sm2[:, u % 2, 0:nk], sinkn[:, 8 + 2 * hp + par:9 + 2 * hp + par])
                gates_split(u + 6)
                if w >= 0 and w % 4 == 3:
                    heads_out(4 + w // 4, w // 4)
                if u in (3, 5, 7, 9):
                    n = u // 2 - 1
                    act.wait_ge(yb_ready, n + 1)
                    act.activation(mixH[:, 4 + HEADS[n], :], og[:, n, 0:T], ACT.Copy).then_inc(ybh_ready, 1)
                if u == 16:
                    sigmoid(1)
            sigmoid(0)

            def evac_bra(i, j):
                act.wait_ge(mx_sum, j + 1)
                act.activation(nH[:, 2 * j:2 * j + 2, 0:T], gab[:, 2 * j:2 * j + 2, :], ACT.Copy).then_inc(mxh_ready, 1)

            pipeline("bra", 1024, evac_bra, K4, True, behind=((0,), (1,), (), (2, 3)))

            def evac_wout2(i, j):
                if j in (1, 3):
                    square_r(ds(4 * i + j - 1, 2), T, META, (acc_free[j // 2], USE["wout2"] + i + 1))

            load_sqrt(3)
            pipeline("wout2", 1024, evac_wout2, K4[0:3] + [None], True)
            for k in range(KD):
                upper(N_F2, k, T, META, (acc_free[1], USE["gu2"]))
            split(BASE["gu2"], 3, 1024, ring_lead(BASE["gu2"]))
            norm_rms(6, T)
            gate_up_scaled("gu2", 2, T, DN)
            load_sqrt(4)
            pipeline("dn2", SLOT, evac_dn(KD, T, META), None, True)
            norm_rms(7, T)

        @block.vector
        def _(dve):
            chain = 0

            def link(ins):
                nonlocal chain
                chain += 1
                ins.then_inc(dve_chain, 1)
                dve.wait_ge(dve_chain, chain)

            def split(g, j, width):
                dve.wait_ge(hi_ready, 4 * g + j + 1)
                dve.tensor_tensor(lo[:, j, 0:width], raw[:, j, 0:width], hi[:, j, 0:width].bitcast(F32),
                                  ALU.subtract).then_inc(lo_ready, 1)

            def pipeline(name, width, evac, ahead, evac_first=False, behind=((0,), (1,), (2,), (3,))):
                first, n = BASE[name], COUNT[name]
                if n > 1:
                    with dve.Fori(1, n) as i:
                        for j in range(4):
                            split(first + i, j, width)
                            evac(i - 1, j)
                for j in range(4):
                    if evac_first or j % 2:
                        evac(n - 1, j)
                    for q in behind[j]:
                        if ahead and ahead[q]:
                            split(first + n, q, ahead[q])
                    if not evac_first and j % 2 == 0:
                        evac(n - 1, j)

            K4 = [1024] * 4
            DN = [SLOT] * 4
            MG = [64, 64, 1024, 1024]
            WG = [1024, 1024, 64, 64]

            def nothing(i, j):
                pass

            def multiplied(name, i, j):
                dve.wait_ge(mm_done, 4 * (BASE[name] + i) + j + 1)

            def col(c):
                return vec[:, c:c + 1]

            def gains(n):
                return vec[:, V_NORM + KD * n:V_NORM + KD * n + KD]

            dve.wait_ge(vec_in, 16)
            dve.tensor_scalar(sinkn[:], vec[:, V_SINK1:V_SINK1 + 16], -1.0, None, ALU.mult)

            def norm_inv(n, width):
                dve.wait_ge(rms_ready, n + 1)
                link(dve.reciprocal(inv[:, 0:width], rms[:, 0:width]))

            for k in range(1, KD):
                dve.wait_ge(sq_ready, 2 * (k // 2) + 2)
                if k >= 2:
                    dve.wait_ge(sq5_sum, k - 1)
                dve.tensor_tensor(sq5[:, 0, :], sq5[:, 0, :], sq5[:, k, :], ALU.add).then_inc(sq5_sum, 1)
            norm_inv(0, 512)
            for k in range(KD):
                dve.tensor_tensor(sq5[:, k, 0:T], R[:, k, META:TM], inv[:, 0:T], ALU.mult)
                ins = dve.tensor_tensor(sq5[:, k, T:512], ctxT[:, k, :], inv[:, T:512], ALU.mult)
            split(0, 0, 1024)
            dve.wait_ge(ada_cols, 1)
            link(dve.tensor_tensor(mods[:, 0:16, :], wk[:, 1, 0:32].rearrange("p (m c) -> p m c", c=2),
                                   vec[:, V_BADA:V_BADA + 16].unsqueeze(-1).broadcast_to([P, 16, 2]), ALU.add))
            for c in range(2):
                ins = dve.scalar_tensor_tensor(out=gmod[:, :, c], in0=mods[:, 8:16, c], scalar=1.0, in1=gains(N_PRE),
                                               op0=ALU.add, op1=ALU.mult)
            link(ins)

            def pre_lower(n):
                k, c = divmod(n, 2)
                s = slice(T * c, T * c + T)
                dve.wait_ge(nh_ready, n + 1)
                dve.tensor_tensor(n5L[:, k, s], sq5[:, k, s], n5H[:, k, s].bitcast(F32), ALU.subtract).then_inc(nl_ready, 1)

            for n in range(2 * KD):
                k, c = divmod(n, 2)
                s = slice(T * c, T * c + T)
                if n == 8:
                    split(0, 1, 1024)
                dve.tensor_scalar(sq5[:, k, s], sq5[:, k, s], gmod[:, k, c:c + 1], mods[:, k, c:c + 1], ALU.mult,
                                  ALU.add).then_inc(xn_ready, 1)
                if n >= 2:
                    pre_lower(n - 2)
            pre_lower(14)
            pre_lower(15)
            for j in (2, 3):
                split(0, j, WG[j])

            def evac_win1(i, j):
                if j == 3:
                    multiplied("win1", i, j)
                    dve.wait_ge(pads, 1)
                    for t in range(2):
                        ins = dve.tensor_copy(cink[:, t, :, 1:T + 1], acc[:, 2 + t, :].rearrange("p (s t) -> p s t", s=2))
                    ins.then_inc(acc_free[1], 1)

            def evac_win2(i, j):
                if j == 3:
                    multiplied("win2", i, j)
                    dve.tensor_copy(mvT[:, 2:4, :], acc[:, 2:4, :]).then_inc(acc_free[1], 1)

            def evac_win3(i, j):
                if j == 3:
                    multiplied("win3", i, j)
                    dve.tensor_scalar(qT[:, 2:4, :], acc[:, 2:4, 0:T], QS, None, ALU.mult).then_inc(acc_free[1], 1)

            pipeline("win0", 1024, nothing, K4)
            dve.wait_ge(gt_log, 1)
            dve.scalar_tensor_tensor(out=glog[:], in0=gt[:], scalar=0.0, in1=glog[:], op0=ALU.min,
                                     op1=ALU.subtract).then_inc(lf_ready, 1)
            pipeline("win1", 1024, evac_win1, K4)
            dve.wait_ge(acc_free[0], USE["win1"] + 1)
            dve.wait_ge(acc_free[1], USE["win1"] + 1)
            for n in range(4):
                src, dst = (cink[:, n], mk[:, n, :].rearrange("p (s t) -> p s t", s=2)) if n < 2 else \
                    (cinq[:, n - 2:n - 1], mq[:, n - 2:n - 1, :])
                w = V_CONV + 3 * ((n + 2) % 4)
                link(dve.tensor_scalar(dst, src[:, :, 1:T + 1], col(w + 1), None, ALU.mult))
                link(dve.scalar_tensor_tensor(out=dst, in0=src[:, :, 0:T], scalar=col(w), in1=dst, op0=ALU.mult,
                                              op1=ALU.add))
                dve.scalar_tensor_tensor(out=dst, in0=src[:, :, 2:T + 2], scalar=col(w + 2), in1=dst, op0=ALU.mult,
                                         op1=ALU.add).then_inc(conv_ready, 1)


            pipeline("win2", 1024, evac_win2, K4)

            X, C = slice(0, T), slice(T, 512)

            def timed(ap, d):
                return ap if d == 0 else ap[:, ::-1]

            dve.wait_ge(c1_in, 16)
            dve.wait_ge(cst_in, 16)
            dve.wait_ge(rows_ps, 1)
            for d in range(2):
                for s in (X, C):
                    ins = dve.tensor_tensor_scan(timed(bR[:, d, s], d), onerow[0:4, :], timed(wk[0:4, 2 * d + 1, s], d), 0.0,
                                                 ALU.mult, ALU.add)
            link(ins)
            for d in range(2):
                ins = dve.tensor_tensor(rR[:, d, :], wk[0:4, 2 * d, :], bR[:, d, :], ALU.subtract)
            link(ins)
            for d in range(2):
                ins = dve.tensor_tensor_scan(timed(MR[:, d, C], d), timed(rR[:, d, C], d), timed(rR[:, d, C], d), 0.0,
                                             ALU.max, ALU.max)
            link(ins)
            last = (511, T)
            for d in range(2):
                e = slice(last[d], last[d] + 1)
                ins = dve.tensor_tensor(m0[:, d:d + 1], bR[:, d, e], MR[:, d, e], ALU.add)
            link(ins)
            for d in range(2):
                e = slice(last[d], last[d] + 1)
                dve.tensor_tensor_scan(timed(MR[:, d, X], d), timed(rR[:, d, X], d), timed(rR[:, d, X], d), m0[:, d:d + 1],
                                       ALU.max, ALU.max)
                dve.tensor_scalar(D16[:, 4 * d:4 * d + 4], ident[0:4, 0:4], MR[:, d, e], None, ALU.mult)
                ins = dve.tensor_scalar(D16[:, 8 + 4 * d:12 + 4 * d], ident[0:4, 0:4], m0[:, d:d + 1], None, ALU.mult)
            link(ins)
            dve.tensor_tensor(bR[:, :, X], bR[:, :, X], MR[:, :, X], ALU.add).then_inc(rows_ready, 1)

            pipeline("win3", 1024, evac_win3, K4)
            dve.wait_ge(rope_ps, 1)
            jobs = [(kT[:, X], kvraw[:, 0, X], wk[:, 0, X])]
            jobs += [(qT[:, t, :], qT[:, t, :], wk[:, (t + 1) // 2, X if t % 2 else C]) for t in range(4)]
            dve.tensor_copy(kT[:, C], kvraw[:, 0, C])
            for n, (dst, src, part) in enumerate(jobs):
                dve.tensor_tensor(t1[:, n % 2, :], part, sinT, ALU.mult)
                link(dve.tensor_tensor(dst, src, cosT, ALU.mult))
                ins = dve.tensor_tensor(dst, dst, t1[:, n % 2, :], ALU.add)
            ins.then_inc(rope_ready, 1)

            dve.tensor_copy(bc16[:], wk[:, 2, T + 32:T + 48])
            link(dve.tensor_copy(rcol[:], wk[:, 2, T:T + 32].rearrange("p (t n) -> p t n", t=4)))
            dve.tensor_tensor(wkx[:], rcol[:, 2:4, :], bc16[:, 0:8].unsqueeze(1).broadcast_to([P, 2, 8]),
                              ALU.subtract).then_inc(wk_arg, 1)


            dve.wait_ge(wk_ready, 1)
            dve.wait_ge(ktok_ready, 1)
            for d in range(2):
                ins = dve.tensor_tensor(kw[:, d].rearrange("p t (h e) -> p t h e", h=4),
                                        ktok[:].rearrange("p t (h e) -> p t h e", h=4),
                                        wkx[:, :, 4 * d:4 * d + 4].unsqueeze(-1).broadcast_to([P, 2, 4, HD]), ALU.mult)
            ins.then_inc(kw_ready, 1)
            for n in range(4):
                dve.wait_ge(cst_ps, n + 1)
                b = CST_BANKS[n]
                dve.tensor_copy(Cst[0:64, n, 0:P], b[0:64, 0:P])
                dve.tensor_copy(Cst[64:128, n, 0:P], b[64:128, P:T])
                dve.tensor_copy(Cst[:, n, P:T], b[:, T:T + P]).then_inc(cst_ready, 1)

            def softmax_sum(n, sm):
                dve.wait_ge(p_exp, n + 1)
                c = slice(n, n + 1)
                link(dve.tensor_tensor(rinv[:, c], rsum[:, c], esink[:, c], ALU.add))
                link(dve.reciprocal(rinv[:, c], rinv[:, c]))
                dve.tensor_scalar(sm, sm, rinv[:, c], None, ALU.mult).then_inc(p_norm, 1)

            def heads_lower(n, hp):
                dve.wait_ge(oh_ready, n + 1)
                dve.tensor_tensor(mixL[:, hp, :], wk[:, 3, 0:T], mixH[:, hp, :].bitcast(F32),
                                  ALU.subtract).then_inc(ol_ready, 1)

            def ada_columns(a):
                m = 16 + 4 * a
                dve.wait_ge(ada_cols, a + 2)
                dve.tensor_tensor(mods[:, m:m + 4, 0], ADA_BANK[a][:, 0:4], vec[:, V_BADA + m:V_BADA + m + 4],
                                  ALU.add).then_inc(ada_used, 1)

            for u in range(18):
                if 1 <= u <= 16:
                    softmax_sum(u - 1, Sm[:, (u - 1) % 3, :])
                if 9 <= u <= 15:
                    ada_columns(u - 9)
                if 1 <= u <= 8:
                    v = u - 1
                    h, d, (full, part, t0) = order(v)
                    dve.wait_ge(e_ready, v + 1)
                    dve.wait_ge(ms_ps, h + 1)
                    if v >= 1:
                        dve.wait_ge(nd_ps, v)
                    dve.scalar_tensor_tensor(out=Aw[:, 0:T], in0=acc[:, 0, T * full:T * full + T], scalar=HD ** -0.5,
                                             in1=zE[:, 0:T], op0=ALU.mult, op1=ALU.mult)
                    dve.scalar_tensor_tensor(out=Aw[:, T:384], in0=acc[:, 0, T * part + t0:T * part + t0 + P],
                                             scalar=HD ** -0.5, in1=zE[:, T:384], op0=ALU.mult,
                                             op1=ALU.mult).then_inc(a_ready, 1)
                if 2 <= u <= 9:
                    v = u - 2
                    h, d, _ = order(v)
                    dve.wait_ge(nd_ps, v + 1)
                    link(dve.tensor_tensor(den1[:], ND_BANK[v % 2][:, T:512], emt[:, v % 2, :], ALU.max))
                    link(dve.scalar_tensor_tensor(out=den1[:], in0=ND_BANK[v % 2][:, T:512], scalar=-1.0, in1=den1[:],
                                                  op0=ALU.mult, op1=ALU.max))
                    link(dve.reciprocal(den1[:], den1[:]))
                    if d == 0:
                        dve.tensor_tensor(hT[:, h, :], ND_BANK[v % 2][:, 0:T], den1[:], ALU.mult).then_inc(nd_used, 1)
                    else:
                        dve.tensor_tensor(den1[:], ND_BANK[v % 2][:, 0:T], den1[:], ALU.mult).then_inc(nd_used, 1)
                        dve.wait_ge(nd_used, v + 1)
                        dve.tensor_tensor(hT[:, h, :], hT[:, h, :], den1[:], ALU.add).then_inc(hsum_ready, 1)
                if u < 16:
                    hp, b, par = UNITS[u]
                    h = 2 * hp + par
                    dve.wait_ge(s_ps, u + 1)
                    if u >= 3:
                        dve.wait_ge(pt_ps, u - 2)
                    dve.tensor_tensor_reduce(Sm[:, u % 3, :], wk[:, u % 2, :], winmask[:, b, :], 1.0, sinkn[:, h:h + 1],
                                             ALU.add, ALU.min, negm[:, u:u + 1]).then_inc(s_max, 1)
                if u >= 2 and (u - 2) % 4 == 3:
                    heads_lower((u - 2) // 4, (u - 2) // 4)
                if u < 8:
                    v = u
                    h, d, (full, part, t0) = order(v)
                    c = 4 * d + h
                    dve.wait_ge(mw_ready, v + 1)
                    if v >= 1:
                        dve.wait_ge(a_ready, v)
                    dve.scalar_tensor_tensor(out=zE[:, 0:T], in0=acc[:, 1, 0:T], scalar=rcol[:, full, c:c + 1],
                                             in1=ordf if d == 0 else ordb, op0=ALU.subtract, op1=ALU.max)
                    dve.scalar_tensor_tensor(out=zE[:, T:384], in0=acc[:, 1, t0:t0 + P], scalar=rcol[:, part, c:c + 1],
                                             in1=ordf[:, 0:P] if d == 0 else ordlow, op0=ALU.subtract,
                                             op1=ALU.max).then_inc(z_ready, 1)
                    if v >= 2:
                        dve.wait_ge(nd_ps, v - 1)
                    dve.scalar_tensor_tensor(out=qw[lanes(h), v % 2, :], in0=mq[lanes(h), h // 2, :], scalar=HD ** -0.5,
                                             in1=wint[lanes(h), :], op0=ALU.mult, op1=ALU.mult).then_inc(qw_ready, 1)
                if u in (13, 14):
                    hp = u - 13
                    dve.wait_ge(hrms, hp + 1)
                    link(dve.reciprocal(hn[:, hp, :], hn[:, hp, :]))
                    for h in (2 * hp, 2 * hp + 1):
                        link(dve.scalar_tensor_tensor(out=hT[:, h, :], in0=hT[:, h, :], scalar=col(V_GML + h),
                                                      in1=hn[:, hp, T * (h % 2):T * (h % 2) + T], op0=ALU.mult, op1=ALU.mult))
                        dve.tensor_tensor(hT[:, h, :], hT[:, h, :], sgo[:, h, :], ALU.mult).then_inc(mlo_ready, 1)
                if u == 16:
                    for h in range(4):
                        dve.wait_ge(mlh_ready, h + 1)
                        dve.tensor_tensor(mixL[:, 4 + h, :], hT[:, h, :], mixH[:, 4 + h, :].bitcast(F32),
                                          ALU.subtract).then_inc(mll_ready, 1)

                if u >= 16:
                    for j in (2 * u - 32, 2 * u - 31):
                        split(BASE["wout"], j, 1024)
            dve.wait_ge(ada_used, 7)
            dve.scalar_tensor_tensor(out=gmod[:, :, 2], in0=mods[:, 32:40, 0], scalar=1.0, in1=gains(N_PREF),
                                     op0=ALU.add, op1=ALU.mult)
            link(dve.tensor_tensor(gmod[:, :, 3], mods[:, 16:24, 0], gains(N_POST), ALU.mult))

            def post_norm(n, gain, ahead=lambda k: None):
                norm_inv(n, T)
                for k in range(KD + 1):
                    if k < KD:
                        dve.scalar_tensor_tensor(out=Y[:, k, :], in0=Y[:, k, :], scalar=gmod[:, k, gain:gain + 1],
                                                 in1=inv[:, 0:T], op0=ALU.mult, op1=ALU.mult).then_inc(y_scaled, 1)
                    if k >= 1:
                        dve.wait_ge(y_scaled, KD * (gain - 3) + k)
                        dve.tensor_tensor(R[:, k - 1, META:TM], R[:, k - 1, META:TM], Y[:, k - 1, :],
                                          ALU.add).then_inc(r_ready, 1)
                        ahead(k - 1)

            def split_norm(n, first, width, t0, gain, shift, weights):
                norm_inv(n, width)

                def lower(k):
                    dve.wait_ge(nh_ready, first + k + 1)
                    dve.scalar_tensor_tensor(out=nL[:, k, 0:width], in0=sq[:, k, 0:width],
                                             scalar=mods[:, shift + k, 0:1], in1=nH[:, k, 0:width].bitcast(F32),
                                             op0=ALU.add, op1=ALU.subtract).then_inc(nl_ready, 1)

                for k in range(KD):
                    dve.scalar_tensor_tensor(out=sq[:, k, 0:width], in0=R[:, k, t0:t0 + width], scalar=gain(k),
                                             in1=inv[:, 0:width], op0=ALU.mult, op1=ALU.mult).then_inc(xn_ready, 1)
                    if k >= 2:
                        lower(k - 2)
                lower(KD - 2)
                lower(KD - 1)
                for j in (2, 3):
                    split(weights, j, 1024)

            def scaled_lower(first, k, width, t0, n):
                dve.wait_ge(nh_ready, first + k + 1)
                dve.scalar_tensor_tensor(out=nL[:, k, 0:width], in0=R[:, k, t0:t0 + width],
                                         scalar=col(V_NORM + KD * n + k), in1=nH[:, k, 0:width].bitcast(F32),
                                         op0=ALU.mult, op1=ALU.subtract).then_inc(nl_ready, 1)

            def tokens_inv(width, tiles=2, rows=P):
                return inv[0:rows, 0:width].unsqueeze(1).broadcast_to([rows, tiles, width])

            def gate_up_scaled(name, f, width, ahead):
                def evac(i, j):
                    if j == 1:
                        multiplied(name, i, j)
                        dve.tensor_tensor(sg[:, :, 0:width], acc[:, 0:2, 0:width], tokens_inv(width),
                                          ALU.mult).then_inc(acc_free[0], 1)
                    if j == 3:
                        multiplied(name, i, j)
                        dve.wait_ge(sg_ready, COUNT[name] * (f - 1) + i + 1)
                        dve.wait_ge(lo_ready, 4 * (BASE[name] + i) + 5)
                        dve.tensor_tensor(hbuf[:, :, 0:width], acc[:, 2:4, 0:width], sg[:, :, 0:width],
                                          ALU.mult).then_inc(acc_free[1], 1)
                        dve.wait_ge(gh_ready, COUNT[name] * f + i + 1)
                        dve.tensor_tensor(gL[:, ds(2 * i, 2), 0:width], hbuf[:, :, 0:width],
                                          gH[:, ds(2 * i, 2), 0:width].bitcast(F32), ALU.subtract).then_inc(gl_ready, 1)
                pipeline(name, 1024, evac, ahead, behind=((0,), (), (), (1, 2, 3)))

            def gate_up(name, f, width, ahead):
                def evac(i, j):
                    if j == 3:
                        multiplied(name, i, j)
                        dve.wait_ge(acc_free[0], USE[name] + i + 1)
                        dve.wait_ge(lo_ready, 4 * (BASE[name] + i) + 5)
                        dve.tensor_tensor(hbuf[:, :, 0:width], sg[:, :, 0:width], acc[:, 2:4, 0:width],
                                          ALU.mult).then_inc(acc_free[1], 1)
                        dve.wait_ge(gh_ready, COUNT[name] * f + i + 1)
                        dve.tensor_tensor(gL[:, ds(2 * i, 2), 0:width], hbuf[:, :, 0:width],
                                          gH[:, ds(2 * i, 2), 0:width].bitcast(F32), ALU.subtract).then_inc(gl_ready, 1)
                pipeline(name, 1024, evac, ahead, behind=((0,), (), (), (1, 2, 3)))

            def evac_half(name, width, t0):
                def evac(i, j):
                    if j in (1, 3):
                        multiplied(name, i, j)
                        k = ds(2 * i + j // 2, 1)
                        dve.scalar_tensor_tensor(out=xg[:, k, 0:width], in0=acc[:, j - 1:j, 0:width], scalar=0.5,
                                                 in1=tokens_inv(width, 1), op0=ALU.mult,
                                                 op1=ALU.mult).then_inc(acc_free[j // 2], 1)
                        dve.wait_ge(acc_free[j // 2], USE[name] + i + 1)
                        dve.tensor_tensor(R[:, k, t0:t0 + width], R[:, k, t0:t0 + width], xg[:, k, 0:width],
                                          ALU.add).then_inc(half_added, 1)
                return evac

            pipeline("wout", 1024, nothing, None, True)
            post_norm(1, 3)
            for j in (0, 1):
                split(BASE["gu0"], j, 1024)
            split_norm(2, 16, T, META, lambda k: gmod[:, k, 2:3], 24, BASE["gu0"])
            ada_columns(7)
            dve.wait_ge(ada_used, 8)
            link(dve.tensor_tensor(gmod[:, :, 4], mods[:, 40:48, 0], gains(N_POSTF), ALU.mult))
            gate_up("gu0", 0, T, DN)
            pipeline("dn0", SLOT, nothing, K4[0:3] + [None], True)
            def next_tokens(k):
                if k >= 1:
                    scaled_lower(24, k - 1, TM, 0, N_F1)

            post_norm(3, 4, next_tokens)
            scaled_lower(24, KD - 1, TM, 0, N_F1)
            split(BASE["gu1"], 3, 1024)
            norm_inv(4, TM)
            gate_up_scaled("gu1", 1, TM, DN)
            pipeline("dn1", SLOT, evac_half("dn1", TM, 0), MG[0:3] + [None], True)
            dve.wait_ge(half_added, KD)
            for k in range(KD):
                scaled_lower(32, k, TM, 0, N_MIX)
            split(BASE["in2k"], 3, 1024)
            norm_inv(5, TM)

            def evac_in2k(i, j):
                if j not in (1, 3):
                    return
                s = j // 2
                multiplied("in2k", i, j)
                src = acc[:, 2 * s:2 * s + 2, :]
                all_inv, frame_inv = tokens_inv(TM), inv[:, META:TM].unsqueeze(1).broadcast_to([P, 2, T])
                if i == 0 and s == 0:
                    ins = dve.tensor_tensor(glT[:], acc[0:16, 0, 0:TM], inv[0:16, 0:TM], ALU.mult)
                elif i == 3:
                    ins = dve.scalar_tensor_tensor(out=qT2[:, 2 * s:2 * s + 2, :], in0=src[:, :, 0:T], scalar=QS, in1=frame_inv,
                                                   op0=ALU.mult, op1=ALU.mult)
                else:
                    to = {(0, 1): kvraw2, (1, 0): gkT, (1, 1): gqT, (2, 0): gvT[:, 0:2], (2, 1): gvT[:, 2:4],
                          (4, 0): grT[:, 0:2], (4, 1): grT[:, 2:4]}[i, s]
                    width = T if (i, s) in ((1, 1), (4, 0), (4, 1)) else TM
                    ins = dve.tensor_tensor(to[:, :, 0:width], src[:, :, 0:width], all_inv if width == TM else frame_inv,
                                            ALU.mult)
                ins.then_inc(acc_free[s], 1)

            def decay_sums():
                dve.wait_ge(z_abs, 1)
                for t in range(2):
                    ins = dve.tensor_scalar(tB[:, t, :], wk[:, t, 0:TM], col(V_GB + t), 0.0, ALU.add, ALU.min)
                link(ins)
                dve.wait_ge(z_ln, 1)
                link(dve.tensor_tensor(tB[:], tB[:], tA[:], ALU.subtract))
                dve.wait_ge(c2_in, 48)
                for t in range(2):
                    ins = dve.tensor_tensor_scan(tC[:, t, :], reset, tB[:, t, :], 0.0, ALU.mult, ALU.add)
                link(ins)
                dve.tensor_copy(blast[:], tC[:, :, META - 1:META + 192:64]).then_inc(b_ready, 1)

            def decay_to_last():
                dve.wait_ge(eb_ready, 1)
                dve.wait_ge(b_ready, 1)
                for t in range(2):
                    dve.tensor_scalar(tC[:, t, 0:META], tC[:, t, 0:META], blast[:, t, 0:1], None, ALU.subtract)
                    f = tC[:, t, META:META + 192].rearrange("p (c i) -> p c i", c=3)
                    ins = dve.tensor_tensor(f, f, blast[:, t, 1:4].unsqueeze(-1).broadcast_to([P, 3, 64]), ALU.subtract)
                ins.then_inc(bl_ready, 1)
                dve.scalar_tensor_tensor(out=gqT[:], in0=gqT[:], scalar=HD ** -0.5, in1=tA[:, :, META:TM], op0=ALU.mult,
                                         op1=ALU.mult)

            def decayed_keys():
                dve.wait_ge(ed_ready, 1)
                dve.tensor_tensor(kdT[:, :, 0:208], gkT[:, :, 0:208], tC[:, :, 0:208], ALU.mult).then_inc(kd_ready, 1)
                dve.wait_ge(kd_ready, 1)
                dve.tensor_tensor(gkT[:], gkT[:], tB[:], ALU.mult).then_inc(qk_ready, 1)

            def causal_scores():
                dve.wait_ge(zero2, 1)
                for n in range(2):
                    dve.wait_ge(at_ps, n + 1)
                    dve.copy_predicated(attm[:, 2 * n:2 * n + 2].rearrange("p h c i -> p (h c) i"), causal[0:64],
                                        wk[0:64, n, :].rearrange("p (m i) -> p m i", m=8)).then_inc(at_ready, 1)

            steps = {(1, 3): decay_sums, (2, 1): decay_to_last, (2, 3): decayed_keys, (4, 1): causal_scores}
            for i in range(COUNT["in2k"]):
                for j in range(4):
                    split(BASE["in2k"] + i + 1, j, 1024)
                    evac_in2k(i, j)
                    if (i, j) in steps:
                        steps[i, j]()

            def gates_split(n):
                split(BASE["in2g"] + n // 4, n % 4, 1024)

            def gates_evac(p):
                multiplied("in2g", p // 2, 2 * (p % 2) + 1)
                dve.tensor_tensor(gab[:, 2 * p:2 * p + 2, :], acc[:, 2 * (p % 2):2 * (p % 2) + 2, 0:T],
                                  inv[:, META:TM].unsqueeze(1).broadcast_to([P, 2, T]), ALU.mult).then_inc(acc_free[p % 2], 1)

            def state(c):
                dve.wait_ge(kv_ps, c + 1)
                for t in range(2):
                    for q in range(2):
                        s = slice(64 * q, 64 * q + 64)
                        new = KV_BANKS[c][s, T * t + P * q:T * t + P * q + P]
                        if c == 0:
                            ins = dve.tensor_copy(St[s, 0, t, :], new)
                        else:
                            e = chunk(c)[1] - 1
                            ins = dve.scalar_tensor_tensor(out=St[s, c, t, :], in0=St[s, c - 1, t, :],
                                                           scalar=tA[s, t, e:e + 1], in1=new, op0=ALU.mult, op1=ALU.add)
                ins.then_inc(st_ready, 1)
                dve.wait_ge(st_ready, c + 1)

            for c in range(3):
                state(c)
            gates_split(4)
            state(3)
            gates_split(5)
            gates_evac(0)
            dve.wait_ge(go_cross, 1)
            dve.tensor_tensor(og[:, 2:4, 0:T], og[:, 2:4, 0:T], GO_CROSS.rearrange("p (h t) -> p h t", h=2),
                              ALU.add).then_inc(go_sum, 1)

            branch = [b[:, :, 0:T] for b in (tA, tB, tC, kdT)]

            def branch_out(j):
                multiplied("brb", 0, j)
                dve.tensor_copy(branch[j], acc[:, 2 * (j % 2):2 * (j % 2) + 2, 0:T]).then_inc(acc_free[j % 2], 1)

            for u in range(19):
                if 1 <= u <= 16:
                    softmax_sum(16 + u - 1, Sm2[:, (u - 1) % 2, 0:META + P * (UNITS[u - 1][1] + 1)])
                if u < 16:
                    hp, b, par = UNITS[u]
                    h = 2 * hp + par
                    nk = META + P * (b + 1)
                    dve.wait_ge(s_ps, 16 + u + 1)
                    dve.wait_ge(bias_ready, h + 1)
                    if u >= 2:
                        dve.wait_ge(pt_ps, 16 + u - 1)
                    dve.tensor_tensor_reduce(Sm2[:, u % 2, 0:nk], wk[:, u % 2, 0:nk], bias2[:, h % 2, b, 0:nk], 1.0,
                                             sinkn[:, 8 + h:9 + h], ALU.add, ALU.min,
                                             negm[:, 16 + u:17 + u]).then_inc(s_max, 1)
                if u >= 3 and (u - 3) % 4 == 3:
                    heads_lower(4 + (u - 3) // 4, (u - 3) // 4)
                if u >= 1:
                    gates_split(u + 5)
                if u in range(1, 14, 2):
                    gates_evac(u // 2 + 1)
                if u in (2, 4, 6, 8):
                    n = u // 2 - 1
                    root = (tC, kdT)[n // 2][:, n % 2, 0:T]
                    dve.wait_ge(gr_ready, 2)
                    dve.wait_ge(grms, n // 2 + 1)
                    link(dve.reciprocal(root, root))
                    link(dve.scalar_tensor_tensor(out=og[:, n, 0:T], in0=og[:, n, 0:T], scalar=col(V_GO), in1=root,
                                                  op0=ALU.mult, op1=ALU.mult))
                    dve.tensor_tensor(og[:, n, 0:T], og[:, n, 0:T], grT[:, HEADS[n], :], ALU.mult).then_inc(yb_ready, 1)
                if u in (4, 6, 8, 10):
                    n = u // 2 - 2
                    dve.wait_ge(ybh_ready, n + 1)
                    dve.tensor_tensor(mixL[:, 4 + HEADS[n], :], og[:, n, 0:T], mixH[:, 4 + HEADS[n], :].bitcast(F32),
                                      ALU.subtract).then_inc(ybl_ready, 1)
                if 14 <= u <= 17:
                    branch_out(u - 14)
                if u == 17:
                    dve.wait_ge(gates_ready, 1)
                    dve.wait_ge(acc_free[1], USE["brb"] + 2)
                    for j in range(4):
                        b = gab[:, KD + 2 * j:KD + 2 * j + 2, :]
                        dve.tensor_tensor(b, b, branch[j], ALU.mult)

            def evac_bra(i, j):
                s = 2 * (j % 2)
                a, b = gab[:, 2 * j:2 * j + 2, :], gab[:, KD + 2 * j:KD + 2 * j + 2, :]
                multiplied("bra", i, j)
                dve.wait_ge(gates_ready, 2)
                dve.tensor_tensor(a, a, acc[:, s:s + 2, 0:T], ALU.mult).then_inc(acc_free[j % 2], 1)
                dve.wait_ge(acc_free[j % 2], USE["bra"] + j // 2 + 1)
                dve.tensor_tensor(a, a, b, ALU.add).then_inc(mx_sum, 1)
                for n in ((), (0,), (1,), (2, 3))[j]:
                    dve.wait_ge(mxh_ready, n + 1)
                    dve.tensor_tensor(nL[:, 2 * n:2 * n + 2, 0:T], gab[:, 2 * n:2 * n + 2, :],
                                      nH[:, 2 * n:2 * n + 2, 0:T].bitcast(F32), ALU.subtract).then_inc(mxl_ready, 1)

            pipeline("bra", 1024, evac_bra, K4, True, ((0,), (1,), (), (2, 3)))

            def evac_wout2(i, j):
                if j in (1, 3):
                    multiplied("wout2", i, j)
                    k = ds(4 * i + j - 1, 2)
                    dve.tensor_tensor(R[:, k, META:TM], R[:, k, META:TM], acc[:, j - 1:j + 1, 0:T],
                                      ALU.add).then_inc(acc_free[j // 2], 1)

            pipeline("wout2", 1024, evac_wout2, K4[0:3] + [None], True)
            dve.wait_ge(acc_free[1], USE["gu2"])
            for k in range(KD):
                scaled_lower(40, k, T, META, N_F2)
            split(BASE["gu2"], 3, 1024)
            norm_inv(6, T)
            gate_up_scaled("gu2", 2, T, DN)
            pipeline("dn2", SLOT, evac_half("dn2", T, META), None, True)

            norm_inv(7, T)
            for k in range(KD):
                dve.scalar_tensor_tensor(out=Y[:, k, :], in0=R[:, k, META:TM], scalar=col(V_NORM + KD * N_FIN + k),
                                         in1=inv[:, 0:T], op0=ALU.mult, op1=ALU.mult).then_inc(out_ready, 1)

        @block.tensor
        def _(pe):
            def split_mm(out_, wH, wL, xH, xL, start, stop):
                pe.matmul(out_, wH, xH, start=start, stop=False)
                pe.matmul(out_, wH, xL, start=False, stop=False)
                return pe.matmul(out_, wL, xH, start=False, stop=stop)

            def set_free(s, use):
                if not (isinstance(use, int) and use == 0):
                    pe.wait_ge(acc_free[s], use)

            def arrived(g, j):
                pe.wait_ge(lo_ready, 4 * g + j + 1)

            def pair(g, use, s, xH, xL, n, ready=None, beside=None):
                set_free(s, use)
                for q in range(2):
                    half(g, s, q, xH, xL, n, ready, beside)

            def half(g, s, q, xH, xL, n, ready=None, beside=None):
                j = 2 * s + q
                arrived(g, j)
                for kk in range(4):
                    k = 4 * q + kk
                    if beside:
                        beside(k)
                    if ready:
                        pe.wait_ge(ready[0], ready[1] + int(ready[2] * k) + (1 if ready[2] < 1 else ready[2]))
                    for m in range(2):
                        w = slice(256 * kk + P * m, 256 * kk + P * m + P)
                        ins = split_mm(acc[:, 2 * s + m, 0:n], hi[:, j, w], lo[:, j, w], xH(k), xL(k),
                                       k == 0, k == KD - 1)
                ins.then_inc(mm_done, 1)

            def pairs(name, xs, n, ready=None, beside=None):
                with pe.Fori(0, COUNT[name]) as i:
                    for s in range(2):
                        pair(BASE[name] + i, USE[name] + i, s, *xs, n, ready, beside)

            def sum_square(k, src, width):
                ins = pe.matmul(wk[:, 0, 0:width], ones, src[:, k, 0:width], start=k == 0, stop=k == KD - 1)
                if k == KD - 1:
                    ins.then_inc(ssq_ps, 1)

            def sum_squares(src, width, squared):
                for k in range(KD):
                    pe.wait_ge(*squared(k))
                    sum_square(k, src, width)

            def ada(name, a, j, out_, n):
                pe.wait_ge(raw_ready[j], 16 * (RING_AT[name] + a) + 16)
                for kk in range(2):
                    k = 2 * j + kk
                    ins = pe.matmul(out_[0:n, :], silu_c[:, 2 * k:2 * k + n], raw[:, j, 512 * kk:512 * kk + 512],
                                    start=k == 0, stop=k == KD - 1)
                ins.then_inc(ada_done, 1)

            pe.wait_ge(silu_ready, 1)
            for a in range(4):
                for j in range(4):
                    ada("ada1", a, j, acc[:, a, :], 2)
                if a == 1:
                    pe.wait_ge(cst_in, 16)
                    pe.wait_ge(sq5_sum, KD - 1)
                    pe.matmul(wk[:, 0, :], ones, sq5[:, 0, :], start=True, stop=True).then_inc(ssq_ps, 1)
            pe.wait_ge(ada_row, 4)
            for m in range(16):
                ins = pe.transpose(wk[:, 1, 2 * m:2 * m + 2], row1[:, m // 4, P * (m % 4):P * (m % 4) + P], ident[0:2, 0:2])
            ins.then_inc(ada_cols, 1)

            both = (lambda k: n5H[:, k, :], lambda k: n5L[:, k, :])
            frames = (lambda k: n5H[:, k, 0:T], lambda k: n5L[:, k, 0:T])
            g = BASE["win0"]
            pair(g, 0, 0, *both, 512, (nl_ready, 0, 2))
            for q in range(2):
                arrived(g, 2 + q)
                for kk in range(4):
                    k, w = 4 * q + kk, slice(16 * kk, 16 * kk + 16)
                    ins = split_mm(acc[0:16, 2, :], hi[:, 2 + q, w], lo[:, 2 + q, w], n5H[:, k, :], n5L[:, k, :],
                                   k == 0, k == KD - 1)
                ins.then_inc(mm_done, 1)
            for name, xs, width in (("win1", both, 512), ("win2", both, 512), ("win3", frames, T)):
                for s in range(2):
                    pair(BASE[name], USE[name], s, *xs, width)
                if name == "win1":
                    pe.wait_ge(lf_ready, 1)
                    for q in range(4):
                        ins = pe.matmul(wk[0:4, q, :], ident[0:16, 4 * q:4 * q + 4], (glog if q % 2 else gt)[:],
                                        start=True, stop=True)
                    ins.then_inc(rows_ps, 1)
            pair(BASE["win4"], USE["win4"], 0, *frames, T)

            pe.wait_ge(c1_in, 16)
            pe.wait_ge(rows_ready, 1)
            for s in range(2):
                pe.wait_ge(acc_free[s], USE["win4"])
            pe.matmul(wk[:, 0, 0:T], perm, kvraw[:, 0, 0:T], start=True, stop=True)
            for t in range(4):
                ins = pe.matmul(wk[:, (t + 1) // 2, T * ((t + 1) % 2):T * ((t + 1) % 2) + T], perm, qT[:, t, :],
                                start=True, stop=True)
            for t in range(4):
                for d in range(2):
                    c = T + 8 * t + 4 * d
                    pe.transpose(wk[:, 2, c:c + 4], rR[:, d, P * t:P * t + P], ident[0:4, 0:4])
            pe.matmul(wk[:, 2, T + 32:T + 48], ones[0:4, :], D16[:], start=True, stop=True).then_inc(rope_ps, 1)
            pe.wait_ge(mqk_ready, 2)
            for t in range(2):
                for n in range(2):
                    ins = pe.transpose(wk[:, 3, T * t + P * n:T * t + P * n + P], mk[:, n, T + P * t:T + P * t + P], ident)
            ins.then_inc(kt_ps, 1)
            pair(BASE["win4"], USE["win4"], 1, *frames, T)
            pe.wait_ge(rope_ready, 1)
            pe.wait_ge(wk_arg, 1)
            for t in (2, 3, 0, 1):
                if t == 1:
                    pe.wait_ge(ktok_ready, 1)
                for h in range(4):
                    ins = pe.transpose(MV_BANKS[t][:, P * h:P * h + P], mvT[:, h, P * t:P * t + P], ident)
                ins.then_inc(mvt_ps, 1)
            pe.wait_ge(acc_free[0], USE["wout"])
            for t in range(4):
                ins = pe.transpose(acc[:, 0, P * t:P * t + P], kvraw[:, 1, P * t:P * t + P], ident)
            ins.then_inc(avt_ps, 1)
            pe.matmul(acc[:, 1, :], swap, kT[:], start=True, stop=True).then_inc(ks_ps, 1)
            pe.wait_ge(acc_free[1], USE["wout"])
            pe.wait_ge(kw_ready, 1)
            pe.wait_ge(vtok_ready, 4)
            pe.wait_ge(avz_ready, 1)
            for n in range(4):
                d, hp = divmod(n, 2)
                for part in range(2):
                    for t in range(2):
                        lhs = kw[:, d, t, P * hp:P * hp + P]
                        if part == 0:
                            pe.matmul(CST_BANKS[n][:, 0:T], lhs, vtok[:, 2 + t, T * hp:T * hp + T], start=t == 0, stop=t == 1)
                        else:
                            ins = pe.matmul(CST_BANKS[n][:, T:T + P], lhs, ones, start=t == 0, stop=t == 1)
                ins.then_inc(cst_ps, 1)

            def transposed_out(par, b, keys):
                for i, (v, p) in enumerate(keys):
                    ins = pe.matmul(wk[:, 3, P * b:P * b + P], v, p, start=par == 0 and i == 0,
                                    stop=par == 1 and i == len(keys) - 1)
                if b == 1 and par == 1:
                    ins.then_inc(o_ps, 1)

            pe.wait_ge(cst_ready, 4)
            pe.wait_ge(ks_ready, 1)
            pe.wait_ge(mqk_ready, 4)
            def ada_turn(a):
                pe.wait_ge(ada_row, 4 + a + 1)
                for m in range(4):
                    ins = pe.transpose(ADA_BANK[a][:, m:m + 1], row2[:, P * m:P * m + P], ident[0:1, 0:1])
                ins.then_inc(ada_cols, 1)

            for u in range(17):
                if 9 <= u <= 15:
                    ada_turn(u - 9)
                if u < 16:
                    hp, b, par = UNITS[u]
                    h = 2 * hp + par
                    keys = kT if h // 4 == h % 2 else kTs
                    if u >= 2:
                        pe.wait_ge(s_max, u - 1)
                    pe.matmul(wk[:, u % 2, :], qT[lanes(h), hp, P * b:P * b + P], keys[lanes(h), :],
                              start=True, stop=True).then_inc(s_ps, 1)
                if u >= 1:
                    hp, b, par = UNITS[u - 1]
                    pe.wait_ge(p_norm, u)
                    if u >= 2:
                        pe.wait_ge(pt_ready, u - 1)
                    for t in range(4):
                        ins = pe.transpose(wk[:, 2, P * t:P * t + P], Sm[:, (u - 1) % 3, P * t:P * t + P], ident)
                    ins.then_inc(pt_ps, 1)
                if u < 8:
                    v = u
                    h, d, _ = order(v)
                    if d == 0:
                        if v >= 1:
                            pe.wait_ge(a_ready, v)
                        for s in range(2):
                            ins = pe.matmul(acc[:, 0, T * s:T * s + T], mk[lanes(h), h // 2, P * s:P * s + P],
                                            mq[lanes(h), h // 2, :], start=True, stop=True)
                        ins.then_inc(ms_ps, 1)
                    if v >= 1:
                        pe.wait_ge(z_ready, v)
                    pe.matmul(acc[:, 1, 0:T], sel4[0:4, h, :], MR[:, d, 0:T], start=True, stop=True)
                    pe.matmul(acc[:, 1, T:512], sel4[0:4, h, :], bR[:, d, 0:T], start=True, stop=True).then_inc(mb_ps, 1)
                if 1 <= u <= 8:
                    v = u - 1
                    h, d, (full, part, t0) = order(v)
                    pe.wait_ge(a_ready, v + 1)
                    pe.wait_ge(qw_ready, v + 1)
                    if v >= 2:
                        pe.wait_ge(nd_used, v - 1)
                    for o, lhs in ((0, lambda s: vtok[:, s, P * h:P * h + P]), (T, lambda s: ones)):
                        pe.matmul(ND_BANK[v % 2][:, o:o + T], lhs(full), Aw[:, 0:T], start=True, stop=False)
                        pe.matmul(ND_BANK[v % 2][:, o + t0:o + t0 + P], lhs(part), Aw[:, T:384], start=False, stop=False)
                        ins = pe.matmul(ND_BANK[v % 2][:, o:o + T], Cst[lanes(h), 2 * d + h // 2, o // 2:o // 2 + P],
                                        qw[lanes(h), v % 2, :], start=False, stop=True)
                    ins.then_inc(nd_ps, 1)
                if 8 <= u < 15:
                    a = u - 8
                    if a >= 1:
                        pe.wait_ge(ada_used, a)
                    else:
                        pe.wait_ge(nd_used, 7)
                    for j in range(4):
                        ada("ada2", a, j, ADA_BANK[a], 1)
                if u == 12:
                    for hp in range(2):
                        pe.wait_ge(hsq_ready, hp + 1)
                        pe.matmul(acc[:, hp, :], ones, hn[:, hp, :], start=True, stop=True).then_inc(hss_ps, 1)
                if u >= 1:
                    pe.wait_ge(pt_ready, u)
                    hp, b, par = UNITS[u - 1]
                    if b == 0 and par == 0 and hp >= 1:
                        pe.wait_ge(ol_ready, hp)
                    g4 = (2 * hp + par) // 4
                    vs = slice(64, 192) if par == 0 else slice(0, P)
                    transposed_out(par, b, [(avz[:, t, g4, vs], pT[:, (u - 1) % 2, P * t:P * t + P])
                                                   for t in range(4)])

            def gate_up(name, first, t0, width, beside=None):
                xs = (lambda k: nH[:, k, t0:t0 + width], lambda k: nL[:, k, t0:t0 + width])
                for s in range(2):
                    pair(BASE[name], USE[name], s, *xs, width, None if s else (nl_ready, first, 1), None if s else beside)
                with pe.Fori(1, COUNT[name]) as i:
                    for s in range(2):
                        pair(BASE[name] + i, USE[name] + i, s, *xs, width)

            def down(name, f, width):
                with pe.Fori(0, COUNT[name]) as i:
                    for j in range(4):
                        s = j // 2
                        if j % 2 == 0:
                            set_free(s, USE[name] + i)
                        arrived(BASE[name] + i, j)
                        pe.wait_ge(gl_ready, 11 * f + (6 if j % 2 == 0 else 11))
                        for kk in range(HALF):
                            k = HALF * (j % 2) + kk
                            w = slice(P * kk, P * kk + P)
                            ins = split_mm(acc[:, 2 * s, 0:width], hi[:, j, w], lo[:, j, w], gH[:, k, 0:width],
                                           gL[:, k, 0:width], k == 0, k == KH - 1)
                        ins.then_inc(mm_done, 1)

            def mixer_half(k):
                pe.wait_ge(*((mll_ready, k + 1) if k < 4 else (ol_ready, k - 3)))

            mixed = (lambda k: mixH[:, (k + 4) % KD, :], lambda k: mixL[:, (k + 4) % KD, :])
            pairs("wout", mixed, T, None, mixer_half)
            sum_squares(sq, T, lambda k: (acc_free[k % 4 // 2], USE["wout"] + k // 4 + 1))
            for j in range(4):
                ada("ada3", 0, j, ADA_BANK[7], 1)
            sum_squares(sq, T, lambda k: (sq_ready, 8 + k + 1))
            ada_turn(7)
            gate_up("gu0", 16, 0, T)
            down("dn0", 0, T)
            sum_squares(sq, T, lambda k: (acc_free[k % 2], USE["dn0"] + k // 2 + 1))

            def square_behind(k):
                pe.wait_ge(sq_ready, 16 + k + 1)
                sum_square(k, sq, TM)

            gate_up("gu1", 24, 0, TM, square_behind)
            down("dn1", 1, TM)
            sum_squares(sq, TM, lambda k: (sq_ready, 24 + k + 1))

            allT = (lambda k: nH[:, k, :], lambda k: nL[:, k, :])
            frames = (lambda k: nH[:, k, META:TM], lambda k: nL[:, k, META:TM])
            g = BASE["in2k"]
            set_free(0, USE["in2k"])
            for q in range(2):
                arrived(g, q)
                for kk in range(4):
                    k, w = 4 * q + kk, slice(16 * kk, 16 * kk + 16)
                    pe.wait_ge(nl_ready, 32 + k + 1)
                    ins = split_mm(acc[0:16, 0, 0:TM], hi[:, q, w], lo[:, q, w], nH[:, k, :], nL[:, k, :], k == 0, k == KD - 1)
                ins.then_inc(mm_done, 1)
            pair(g, USE["in2k"], 1, *allT, TM)

            def log_decays():
                pe.wait_ge(c2_in, 48)
                for t in range(2):
                    ins = pe.matmul(wk[:, t, 0:TM], gatew[:, P * t:P * t + P], glT[:], start=True, stop=True)
                ins.then_inc(z_ps, 1)

            def attention_keys():
                pe.transpose(wk[0:META, 2, 0:P], kvraw2[:, 1, 0:META], ident)
                for t in range(2):
                    ins = pe.transpose(wk[:, 2, P + P * t:2 * P + P * t], kvraw2[:, 1, META + P * t:META + P * t + P], ident)
                ins.then_inc(av2_ps, 1)
                pe.matmul(wk[:, 3, 0:TM], swap, kvraw2[:, 0, :], start=True, stop=True).then_inc(ks2_ps, 1)

            def values(c):
                a, e = chunk(c)
                if c >= 2:
                    pe.wait_ge(gvt_ready, c - 1)
                else:
                    pe.wait_ge((av2_ready, ks2_ready)[c], 1)
                for h in range(4):
                    ins = pe.transpose(GV_BANKS[c][0:e - a, P * h:P * h + P], gvT[:, h, a:e], ident)
                ins.then_inc(gvt_ps, 1)

            def decayed_keys():
                pe.wait_ge(kd_ready, 1)
                for c in range(4):
                    a, e = chunk(c)
                    for t in range(2):
                        o = T * (c % 2) + P * t
                        ins = pe.transpose(wk[0:e - a, c // 2, o:o + P], kdT[:, t, a:e], ident)
                    if c % 2:
                        ins.then_inc(kdt_ps, 1)

            def chunk_scores():
                pe.wait_ge(qk_ready, 1)
                for n, h in enumerate(HEADS):
                    if n % 2 == 0:
                        pe.wait_ge(kdt_ready, n // 2 + 1)
                    for c in range(4):
                        a, e = chunk(c + 1)
                        o = T * (n % 2) + 64 * c
                        ins = pe.matmul(wk[0:64, n // 2, o:o + 64], gkT[lanes(h), h // 2, a:e],
                                        gqT[lanes(h), h // 2, 64 * c:64 * c + 64], start=True, stop=True)
                    if n % 2:
                        ins.then_inc(at_ps, 1)

            def increment(c):
                n = chunk(c)[1] - chunk(c)[0]
                if c in (0, 3):
                    pe.wait_ge(gvt_ready, 4 if c == 0 else 5)
                else:
                    pe.wait_ge(at_ready, c)
                for t in range(2):
                    ins = pe.matmul(KV_BANKS[c][:, T * t:T * t + T], kdtok[0:n, c, P * t:P * t + P],
                                    gvtok[0:n, c, T * t:T * t + T], start=True, stop=True)
                ins.then_inc(kv_ps, 1)

            def linear_head(k):
                n = k % 4
                bank, h = n // 2, HEADS[n]
                if n == 0:
                    pe.wait_ge(st_ready, 4)
                for c in range(4):
                    o = slice(T * (n % 2) + 64 * c, T * (n % 2) + 64 * c + 64)
                    pe.matmul(GO_BANKS[bank][:, o], gvtok[:, c + 1, P * h:P * h + P], attm[:, n, c, :], start=True,
                              stop=bank == 1)
                    ins = pe.matmul((GO_BANKS[0], GO_CROSS)[bank][:, o], St[lanes(h), c, h // 2, :],
                                    gqT[lanes(h), h // 2, 64 * c:64 * c + 64], start=bank == 1, stop=True)
                if n % 2:
                    ins.then_inc(go_ps, 1)

            steps = {(1, 1): (log_decays, attention_keys), (3, 0): (decayed_keys,), (3, 1): (lambda: values(0), lambda: values(1)),
                     (4, 0): (lambda: values(2), lambda: values(3), chunk_scores)}
            for n, (a, b) in enumerate(((allT, frames), (allT, allT), (frames, frames), (frames, frames))):
                for s, xs in enumerate((a, b)):
                    pair(g + 1 + n, USE["in2k"] + 1 + n, s, *xs, TM if xs is allT else T)
                    for step in steps.get((1 + n, s), ()):
                        step()

            def gates_half(n, beside=None):
                i, s, q = n // 4, n // 2 % 2, n % 2
                if q == 0:
                    set_free(s, USE["in2g"] + i)
                half(BASE["in2g"] + i, s, q, *frames, T, None, beside)

            def branch_part(name, k0, j, tiles=range(4)):
                s = j % 2
                set_free(s, USE[name] + j // 2)
                arrived(BASE[name], j)
                for kk in tiles:
                    for m in range(2):
                        w = slice(256 * kk + P * m, 256 * kk + P * m + P)
                        ins = split_mm(acc[:, 2 * s + m, 0:T], hi[:, j, w], lo[:, j, w], mixH[:, k0 + kk, :],
                                       mixL[:, k0 + kk, :], kk == 0, kk == 3)
                if 3 in tiles:
                    ins.then_inc(mm_done, 1)

            values(4)
            for c in range(3):
                increment(c)
            gates_half(0)
            increment(3)
            gates_half(1)
            gates_half(2, linear_head)
            gates_half(3)
            for n, src in enumerate((tA, tB)):
                pe.wait_ge(go_ready, n + 1)
                pe.matmul(wk[:, 2 + n, :], ones, src[:, :, 0:T], start=True, stop=True).then_inc(gss_ps, 1)

            for u in range(18):
                if u < 16:
                    hp, b, par = UNITS[u]
                    h = 2 * hp + par
                    keys = kvraw2[:, 0, :] if h // 4 == h % 2 else kS2
                    nk = META + P * (b + 1)
                    if u >= 2:
                        pe.wait_ge(s_max, 16 + u - 1)
                    pe.matmul(wk[:, u % 2, 0:nk], qT2[lanes(h), hp, P * b:P * b + P], keys[lanes(h), 0:nk],
                              start=True, stop=True).then_inc(s_ps, 1)
                w = u - 2
                if w >= 0:
                    hp, b, par = UNITS[w]
                    sm, pt = Sm2[:, w % 2, :], pT2[:, w % 2, :]
                    pe.wait_ge(p_norm, 16 + w + 1)
                    if w >= 1:
                        pe.wait_ge(pt_ready, 16 + w)
                    else:
                        pe.wait_ge(grms, 2)
                    pe.transpose(wk[0:META, 2, 0:P], sm[:, 0:META], ident)
                    for t in range(b + 1):
                        ins = pe.transpose(wk[:, 2, P + P * t:2 * P + P * t], sm[:, META + P * t:META + P * t + P], ident)
                    ins.then_inc(pt_ps, 1)
                if 1 <= u <= 12:
                    gates_half(u + 3)
                elif 13 <= u <= 16:
                    if u == 13:
                        pe.wait_ge(ybl_ready, 4)
                    branch_part("brb", 4, u - 13)
                elif u == 17:
                    pe.wait_ge(ol_ready, 7)
                    branch_part("bra", 0, 0, range(3))
                if w >= 0:
                    pe.wait_ge(pt_ready, 16 + w + 1)
                    if b == 0 and par == 0 and hp >= 1:
                        pe.wait_ge(ol_ready, 4 + hp)
                    g4 = (2 * hp + par) // 4
                    vs = slice(64, 192) if par == 0 else slice(0, P)
                    keys = [(avz2[0:META, 0, g4, vs], pt[0:META, 0:P])]
                    keys += [(avz2[:, 1 + t, g4, vs], pt[:, P + P * t:2 * P + P * t]) for t in range(b + 1)]
                    transposed_out(par, b, keys)

            pe.wait_ge(ol_ready, 8)
            branch_part("bra", 0, 0, range(3, 4))
            for j in range(1, 4):
                branch_part("bra", 0, j)
            pairs("wout2", (lambda k: nH[:, k, 0:T], lambda k: nL[:, k, 0:T]), T, (mxl_ready, 0, 0.5))
            sum_squares(sq, T, lambda k: (sq_ready, 32 + k // 2 + 1))
            gate_up("gu2", 40, 0, T)
            down("dn2", 2, T)
            sum_squares(sq, T, lambda k: (sq_ready, 36 + k + 1))


_WEIGHTS = ["w_ada", "w_in", "w_out", "w_ffn_in", "w_ffn_out", "ffn1_w_gate_2", "ffn1_w_up_2", "ffn1_w_down_2", "w_in_2",
            "gla_gate_w_2", "w_branch_att_2", "w_branch_gla_2", "w_out_2", "ffn2_w_gate_2", "ffn2_w_up_2", "ffn2_w_down_2"]


def kernel(**inputs):
    import numpy as _np
    import concourse.bacc as _bacc
    from concourse import mybir as _mybir
    from concourse.bass_utils import run_bass_kernel_spmd as _run

    a = {n: _np.asarray(v) for n, v in inputs.items()}

    def cols(v):
        return v.reshape(-1, P).T

    def tokens(x):
        return x.reshape(-1, KD, P).transpose(2, 1, 0)

    def every(v):
        return _np.broadcast_to(v.reshape(1, -1), (P, v.size))

    norms = ("g_pre_mix", "g_post_mix", "g_pre_ffn", "g_post_ffn", "ffn1_norm_2", "mix_norm_2", "ffn2_norm_2", "final_norm_2")
    parts = [_np.stack([cols(a["c"]), cols(a["c_ctx"])], -1).reshape(P, -1), cols(a["b_ada"])]
    parts += [cols(a[n]) for n in norms]
    parts += [a["w_conv_qk"][0].T.reshape(4, P, 3).transpose(1, 0, 2).reshape(P, -1), cols(a["g_mlstm_out"])]
    parts += [cols(a["gla_gate_b_2"]), cols(a["gla_out_norm_2"])]
    parts += [every(a["attn_sink"]), every(a["att_sinks_2"]), _np.concatenate([a["b_gates"].reshape(16, 1), _np.zeros((P - 16, 1), _np.float32)])]
    host = {"vecs": _np.concatenate(parts, 1)}
    host["hT"] = tokens(_np.concatenate([a["meta_tokens_2"], a["x"][0]], 0))
    host["ctxT"] = tokens(a["ctx"][0])
    host["cst"], host["c1"], host["c2"], host["causal"] = shape_constants()
    for n in _WEIGHTS:
        host[n] = a[n][0]

    nc = _bacc.Bacc("TRN2", target_bir_lowering=False, num_devices=1)
    arrays, dr = {}, {}
    for n, v in host.items():
        v = _np.ascontiguousarray(v)
        arrays[f"in_{n}"] = v
        dr[n] = nc.dram_tensor(f"in_{n}", v.shape, _mybir.dt.from_np(v.dtype), kind="ExternalInput").ap()
    out = nc.dram_tensor("out_0", (P, KD, T), _mybir.dt.float32, kind="ExternalOutput").ap()
    program(nc, dr, out)
    r = _run(nc, [arrays], core_ids=[0])
    y = r.results[0]["out_0"]
    return _np.ascontiguousarray(y.transpose(2, 1, 0)).reshape(1, T, D)
```
